# Optimizing a Trainium2 kernel written in Bass

```python
import jax, jax.numpy as jnp
from jax import lax
import numpy as np

D_MODEL = 2048
BATCH = 1
SEQ = 256
DEPTH = 1

HEAD_DIM = 64
N_HEADS_SWA = 16
N_KV_SWA = 2
N_HEADS_FOX = 16
WINDOW = 128
BLOCK = 128
D_FF = 5632
CONV_WIDTH = 3
EPS = 1e-6
D_SWA = N_HEADS_SWA * HEAD_DIM
D_KV_SWA = N_KV_SWA * HEAD_DIM
D_FOX = N_HEADS_FOX * HEAD_DIM
D_MIX = D_SWA + D_FOX
D_IN = D_SWA + 2 * D_KV_SWA + 3 * D_FOX + N_HEADS_FOX


def rmsnorm(x, g):
    xf = x.astype(jnp.float32)
    y = xf * lax.rsqrt(jnp.mean(xf * xf, axis=-1, keepdims=True) + EPS)
    return (y * g.astype(jnp.float32)).astype(x.dtype)

def alibi_slopes(n):
    return jnp.asarray(2.0 ** (-8.0 * np.arange(1, n + 1) / n), dtype=jnp.float32)

def swa_sink_attention(q, k, v, sinks):
    B, S, H, D = q.shape
    KV = k.shape[2]
    G = H // KV
    nB = S // BLOCK
    scale = 1.0 / np.sqrt(D)
    qb = q.reshape(B, nB, BLOCK, KV, G, D)

    def band(t):
        tp = jnp.pad(t, ((0, 0), (BLOCK, 0), (0, 0), (0, 0)))[:, :S]
        return jnp.concatenate([tp.reshape(B, nB, BLOCK, KV, D), t.reshape(B, nB, BLOCK, KV, D)], axis=2)

    kb, vb = band(k), band(v)
    s = jnp.einsum('bnqkgd,bnskd->bnkgqs', qb, kb).astype(jnp.float32) * scale
    q_loc = BLOCK + jnp.arange(BLOCK)
    k_loc = jnp.arange(2 * BLOCK)
    dist = (q_loc[:, None] - k_loc[None, :]).astype(jnp.float32)
    blk_start = jnp.arange(nB) * BLOCK - BLOCK
    k_abs = blk_start[:, None] + k_loc[None, :]
    mask = (dist >= 0)[None] & (dist < WINDOW)[None] & (k_abs >= 0)[:, None, :]
    slopes = alibi_slopes(H).reshape(KV, G)
    s = s - slopes[:, :, None, None] * dist
    s = jnp.where(mask[None, :, None, None], s, -jnp.inf)
    sink = sinks.astype(jnp.float32).reshape(KV, G)[None, None, :, :, None, None]
    m = jnp.maximum(jnp.max(s, axis=-1, keepdims=True), sink)
    p = jnp.exp(s - m)
    p = p / (jnp.sum(p, axis=-1, keepdims=True) + jnp.exp(sink - m))
    o = jnp.einsum('bnkgqs,bnskd->bnqkgd', p.astype(v.dtype), vb)
    return o.reshape(B, S, H, D)

def forgetting_attention(q, k, v, log_f):
    B, S, H, D = q.shape
    nB = S // BLOCK
    scale = 1.0 / np.sqrt(D)
    c = lax.cumsum(log_f, axis=1)
    cT = jnp.transpose(c, (0, 2, 1))
    qb = jnp.moveaxis(q.reshape(B, nB, BLOCK, H, D), 1, 0)
    cb = jnp.moveaxis(cT.reshape(B, H, nB, BLOCK), 2, 0)
    k_pos = jnp.arange(S)

    def one_block(args):
        q_blk, c_blk, n = args
        s = jnp.einsum('bqhd,bshd->bhqs', q_blk, k).astype(jnp.float32) * scale
        s = s + c_blk[..., None] - cT[:, :, None, :]
        q_pos = n * BLOCK + jnp.arange(BLOCK)
        s = jnp.where((q_pos[:, None] >= k_pos[None, :])[None, None], s, -jnp.inf)
        p = jax.nn.softmax(s, axis=-1)
        return jnp.einsum('bhqs,bshd->bqhd', p.astype(v.dtype), v)

    o = lax.map(one_block, (qb, cb, jnp.arange(nB)))
    return jnp.moveaxis(o, 0, 1).reshape(B, S, H, D)

def causal_dwconv(u, w, b):
    S = u.shape[1]
    up = jnp.pad(u, ((0, 0), (CONV_WIDTH - 1, 0), (0, 0)))
    y = b
    for kk in range(CONV_WIDTH):
        y = y + up[:, kk:kk + S] * w[kk]
    return y

def first_inputs(seed: int = 0) -> dict:
    key = jax.random.key(seed)
    ks = jax.random.split(key, 17)
    f32 = jnp.float32
    nrm = lambda k, shape, s: jax.random.normal(k, shape, f32) * s
    gain = lambda k, n: 1.0 + 0.05 * jax.random.normal(k, (DEPTH, n), f32)
    return {
        "x": jax.random.normal(ks[0], (BATCH, SEQ, D_MODEL), f32),
        "pre_mix_g": gain(ks[1], D_MODEL),
        "w_in": nrm(ks[2], (DEPTH, D_MODEL, D_IN), D_MODEL ** -0.5),
        "b_forget": 2.0 + 0.5 * jax.random.normal(ks[3], (DEPTH, N_HEADS_FOX), f32),
        "sinks": nrm(ks[4], (DEPTH, N_HEADS_SWA), 1.0),
        "grp_swa_g": gain(ks[5], D_SWA),
        "grp_fox_g": gain(ks[6], D_FOX),
        "w_out": nrm(ks[7], (DEPTH, D_MIX, D_MODEL), D_MIX ** -0.5),
        "post_mix_g": gain(ks[8], D_MODEL),
        "pre_ffn_g": gain(ks[9], D_MODEL),
        "w_up": nrm(ks[10], (DEPTH, D_MODEL, 2 * D_FF), D_MODEL ** -0.5),
        "conv_w": nrm(ks[11], (DEPTH, CONV_WIDTH, 2 * D_FF), CONV_WIDTH ** -0.5),
        "conv_b": nrm(ks[12], (DEPTH, 2 * D_FF), 0.02),
        "w_down": nrm(ks[13], (DEPTH, D_FF, D_MODEL), D_FF ** -0.5),
        "post_ffn_g": gain(ks[14], D_MODEL),
    }

def first_block(x, pre_mix_g, w_in, b_forget, sinks, grp_swa_g, grp_fox_g, w_out, post_mix_g,
              pre_ffn_g, w_up, conv_w, conv_b, w_down, post_ffn_g):
    B, S, _ = x.shape
    cuts = np.cumsum([D_SWA, D_KV_SWA, D_KV_SWA, D_FOX, D_FOX, D_FOX])
    for l in range(DEPTH):
        h = rmsnorm(x, pre_mix_g[l])
        proj = h @ w_in[l]
        q_a, k_a, v_a, q_b, k_b, v_b, f_b = jnp.split(proj, cuts, axis=-1)
        o_a = swa_sink_attention(q_a.reshape(B, S, N_HEADS_SWA, HEAD_DIM),
                                 k_a.reshape(B, S, N_KV_SWA, HEAD_DIM),
                                 v_a.reshape(B, S, N_KV_SWA, HEAD_DIM), sinks[l])
        log_f = jax.nn.log_sigmoid(f_b.astype(jnp.float32) + b_forget[l].astype(jnp.float32))
        o_b = forgetting_attention(q_b.reshape(B, S, N_HEADS_FOX, HEAD_DIM),
                                   k_b.reshape(B, S, N_HEADS_FOX, HEAD_DIM),
                                   v_b.reshape(B, S, N_HEADS_FOX, HEAD_DIM), log_f)
        o_a = rmsnorm(o_a.reshape(B, S, D_SWA), grp_swa_g[l])
        o_b = rmsnorm(o_b.reshape(B, S, D_FOX), grp_fox_g[l])
        mix = jnp.concatenate([o_a, o_b], axis=-1) @ w_out[l]
        x = x + rmsnorm(mix, post_mix_g[l])
        h = rmsnorm(x, pre_ffn_g[l])
        u = causal_dwconv(h @ w_up[l], conv_w[l], conv_b[l])
        gate, val = jnp.split(u, 2, axis=-1)
        y = (jax.nn.gelu(gate, approximate=True) * val) @ w_down[l]
        x = x + rmsnorm(y, post_ffn_g[l])
    return x


MIX_WIDTH = D_MODEL
HEAD_DIM_2 = 128
SB_HEADS = 8
SB_WIDTH = SB_HEADS * HEAD_DIM_2
SB_BLOCK = 128
GLA_HEADS = 4
GLA_HEAD_V = HEAD_DIM_2
GLA_HEAD_K = HEAD_DIM_2 // 2
GLA_WIDTH = GLA_HEADS * GLA_HEAD_V
GLA_KEY_WIDTH = GLA_HEADS * GLA_HEAD_K
GLA_GATE_RANK = 16
GLA_GATE_TAU = 16.0
GLA_CHUNK = 64
SGU_GROUPS = 4
SGU_WIDTH = MIX_WIDTH - SB_WIDTH - GLA_WIDTH
SGU_GROUP_DIM = SGU_WIDTH // SGU_GROUPS
SGU_CHUNK = 128
N_MIX_HEADS = MIX_WIDTH // HEAD_DIM_2
N_MEM = 256
XA_HEADS = 4
XA_HEAD_DIM = 128
XA_WIDTH = XA_HEADS * XA_HEAD_DIM

IN_SPLITS = [SB_WIDTH, SB_WIDTH, SB_WIDTH, SB_WIDTH,
             GLA_KEY_WIDTH, GLA_KEY_WIDTH, GLA_WIDTH, GLA_GATE_RANK, GLA_WIDTH,
             SGU_WIDTH, SGU_WIDTH, SGU_WIDTH]
IN_WIDTH = sum(IN_SPLITS)
IN_OFFSETS = [int(o) for o in np.cumsum(IN_SPLITS)[:-1]]


def rmsnorm_2(x, g):
    xf = x.astype(jnp.float32)
    y = xf * lax.rsqrt(jnp.mean(xf * xf, axis=-1, keepdims=True) + EPS)
    return (y * g.astype(jnp.float32)).astype(x.dtype)

def to_heads(t, n_heads):
    b, s, _ = t.shape
    return t.reshape(b, s, n_heads, -1).transpose(0, 2, 1, 3)

def from_heads(t):
    b, h, s, d = t.shape
    return t.transpose(0, 2, 1, 3).reshape(b, s, h * d)

def stick_breaking_attention(q, k, v):
    B, H, S, d = q.shape
    nblk = S // SB_BLOCK
    scale = d ** -0.5
    qb = q.reshape(B, H, nblk, SB_BLOCK, d).transpose(2, 0, 1, 3, 4)
    key_pos = jnp.arange(S)

    def block(args):
        q_blk, i = args
        z = jnp.einsum('bhqd,bhkd->bhqk', q_blk, k).astype(jnp.float32) * scale
        q_pos = i * SB_BLOCK + jnp.arange(SB_BLOCK)
        causal = key_pos[None, :] < q_pos[:, None]
        log_keep = jnp.where(causal, jax.nn.log_sigmoid(-z), 0.0)
        suffix = lax.cumsum(log_keep, axis=3, reverse=True) - log_keep
        a = jnp.where(causal, jnp.exp(jax.nn.log_sigmoid(z) + suffix), 0.0)
        return jnp.einsum('bhqk,bhkd->bhqd', a.astype(v.dtype), v)

    out = lax.map(block, (qb, jnp.arange(nblk)))
    return out.transpose(1, 2, 0, 3, 4).reshape(B, H, S, d)

def gla_chunked(q, k, v, log_alpha):
    B, H, S, dk = q.shape
    dv = v.shape[-1]
    C = GLA_CHUNK
    N = S // C
    qc = q.reshape(B, H, N, C, dk).astype(jnp.float32) * (dk ** -0.5)
    kc = k.reshape(B, H, N, C, dk).astype(jnp.float32)
    vc = v.reshape(B, H, N, C, dv).astype(jnp.float32)
    bcum = jnp.cumsum(log_alpha.reshape(B, H, N, C, dk).astype(jnp.float32), axis=3)
    tril = jnp.tril(jnp.ones((C, C), dtype=bool))
    rel = bcum[:, :, :, :, None, :] - bcum[:, :, :, None, :, :]
    decay = jnp.exp(jnp.where(tril[:, :, None], rel, -jnp.inf))
    attn = jnp.einsum('bhntd,bhnsd,bhntsd->bhnts', qc, kc, decay)
    o_intra = jnp.einsum('bhnts,bhnsv->bhntv', attn, vc)
    q_dec = qc * jnp.exp(bcum)
    b_last = bcum[:, :, :, -1:, :]
    k_dec = kc * jnp.exp(b_last - bcum)
    chunk_decay = jnp.exp(b_last[:, :, :, 0, :])
    xs = (jnp.moveaxis(q_dec, 2, 0), jnp.moveaxis(k_dec, 2, 0),
          jnp.moveaxis(vc, 2, 0), jnp.moveaxis(chunk_decay, 2, 0))

    def step(state, inp):
        qn, kn, vn, dn = inp
        o = jnp.einsum('bhtd,bhdv->bhtv', qn, state)
        state = dn[..., None] * state + jnp.einsum('bhsd,bhsv->bhdv', kn, vn)
        return state, o

    state0 = jnp.zeros((B, H, dk, dv), jnp.float32)
    _, o_inter = lax.scan(step, state0, xs)
    o = o_intra + jnp.moveaxis(o_inter, 0, 2)
    return o.reshape(B, H, S, dv).astype(v.dtype)

def chunked_sgu(u, v, g_norm, w_s, b_s):
    B, S, _ = v.shape
    N = S // SGU_CHUNK
    v = rmsnorm_2(v, g_norm)
    vb = v.reshape(B, N, SGU_CHUNK, SGU_GROUPS, SGU_GROUP_DIM)
    w = w_s * jnp.tril(jnp.ones((SGU_CHUNK, SGU_CHUNK), w_s.dtype))[None]
    mixed = jnp.einsum('gts,bnsgc->bntgc', w, vb) + b_s.T[None, None, :, :, None]
    return u * mixed.reshape(B, S, SGU_WIDTH)

def memory_cross_attention(h, m, w_q, w_kv, w_o):
    B, S, _ = h.shape
    q = (h @ w_q).reshape(B, S, XA_HEADS, XA_HEAD_DIM)
    k, v = jnp.split(m @ w_kv, 2, axis=-1)
    k = k.reshape(B, -1, XA_HEADS, XA_HEAD_DIM)
    v = v.reshape(B, -1, XA_HEADS, XA_HEAD_DIM)
    s = jnp.einsum('bqhd,bkhd->bhqk', q, k).astype(jnp.float32) * (XA_HEAD_DIM ** -0.5)
    p = jax.nn.softmax(s, axis=-1).astype(v.dtype)
    o = jnp.einsum('bhqk,bkhd->bqhd', p, v).reshape(B, S, XA_WIDTH)
    return o @ w_o

def second_inputs(seed: int = 0) -> dict:
    key = jax.random.key(seed)
    ks = jax.random.split(key, 17)
    f32 = jnp.float32
    nrm = lambda k, shape, s: jax.random.normal(k, shape, f32) * s
    return {
        "x": nrm(ks[0], (BATCH, SEQ, D_MODEL), 1.0),
        "mem": nrm(ks[1], (BATCH, N_MEM, D_MODEL), 1.0),
        "norm_mix": 1.0 + nrm(ks[2], (DEPTH, D_MODEL), 0.02),
        "w_in": nrm(ks[3], (DEPTH, D_MODEL, IN_WIDTH), D_MODEL ** -0.5),
        "w_gla_gate_up": nrm(ks[4], (DEPTH, GLA_GATE_RANK, GLA_KEY_WIDTH), GLA_GATE_RANK ** -0.5),
        "b_gla_gate": nrm(ks[5], (DEPTH, GLA_KEY_WIDTH), 0.1),
        "sgu_norm": 1.0 + nrm(ks[6], (DEPTH, SGU_WIDTH), 0.02),
        "w_sgu": nrm(ks[7], (DEPTH, SGU_GROUPS, SGU_CHUNK, SGU_CHUNK), SGU_CHUNK ** -0.5),
        "b_sgu": 1.0 + nrm(ks[8], (DEPTH, SGU_GROUPS, SGU_CHUNK), 0.1),
        "out_norm": 1.0 + nrm(ks[9], (DEPTH, MIX_WIDTH), 0.02),
        "w_out": nrm(ks[10], (DEPTH, MIX_WIDTH, D_MODEL), MIX_WIDTH ** -0.5),
        "norm_xattn": 1.0 + nrm(ks[11], (DEPTH, D_MODEL), 0.02),
        "norm_mem": 1.0 + nrm(ks[12], (DEPTH, D_MODEL), 0.02),
        "w_xq": nrm(ks[13], (DEPTH, D_MODEL, XA_WIDTH), D_MODEL ** -0.5),
        "w_xkv": nrm(ks[14], (DEPTH, D_MODEL, 2 * XA_WIDTH), D_MODEL ** -0.5),
        "w_xo": nrm(ks[15], (DEPTH, XA_WIDTH, D_MODEL), XA_WIDTH ** -0.5),
        "final_norm": 1.0 + nrm(ks[16], (D_MODEL,), 0.02),
    }

def second_block(x, mem, norm_mix, w_in, w_gla_gate_up, b_gla_gate, sgu_norm, w_sgu, b_sgu,
              out_norm, w_out, norm_xattn, norm_mem, w_xq, w_xkv, w_xo, final_norm):
    B, S, _ = x.shape
    for l in range(DEPTH):
        h = rmsnorm_2(x, norm_mix[l])
        (sb_q, sb_k, sb_v, sb_g,
         gla_q, gla_k, gla_v, gla_r, gla_g,
         sgu_u, sgu_v, sgu_g) = jnp.split(h @ w_in[l], IN_OFFSETS, axis=-1)

        o_sb = from_heads(stick_breaking_attention(
            to_heads(sb_q, SB_HEADS), to_heads(sb_k, SB_HEADS), to_heads(sb_v, SB_HEADS)))

        gate_logits = (gla_r @ w_gla_gate_up[l] + b_gla_gate[l]).astype(jnp.float32)
        log_alpha = jax.nn.log_sigmoid(gate_logits) / GLA_GATE_TAU
        o_gla = from_heads(gla_chunked(
            to_heads(gla_q, GLA_HEADS), to_heads(gla_k, GLA_HEADS),
            to_heads(gla_v, GLA_HEADS), to_heads(log_alpha, GLA_HEADS)))

        o_sgu = chunked_sgu(jax.nn.gelu(sgu_u), jax.nn.gelu(sgu_v), sgu_norm[l], w_sgu[l], b_sgu[l])

        mix = jnp.concatenate([o_sb, o_gla, o_sgu], axis=-1)
        mix = rmsnorm_2(mix.reshape(B, S, N_MIX_HEADS, HEAD_DIM_2),
                      out_norm[l].reshape(N_MIX_HEADS, HEAD_DIM_2)).reshape(B, S, MIX_WIDTH)
        gate = jax.nn.silu(jnp.concatenate([sb_g, gla_g, sgu_g], axis=-1))
        x = x + (mix * gate) @ w_out[l]
        x = x + memory_cross_attention(rmsnorm_2(x, norm_xattn[l]), rmsnorm_2(mem, norm_mem[l]),
                                       w_xq[l], w_xkv[l], w_xo[l])
    return rmsnorm_2(x, final_norm)


def setup_inputs(seed=0):
    out = dict(first_inputs(seed))
    for name, value in second_inputs(seed + 1).items():
        if name != "x":
            out[name + "_2"] = value
    return out


def reference(
    x, pre_mix_g, w_in, b_forget, sinks, grp_swa_g, grp_fox_g, w_out, post_mix_g, pre_ffn_g,
    w_up, conv_w, conv_b, w_down, post_ffn_g, mem_2, norm_mix_2, w_in_2, w_gla_gate_up_2,
    b_gla_gate_2, sgu_norm_2, w_sgu_2, b_sgu_2, out_norm_2, w_out_2, norm_xattn_2, norm_mem_2,
    w_xq_2, w_xkv_2, w_xo_2, final_norm_2,
):
    x = first_block(
        x, pre_mix_g, w_in, b_forget, sinks, grp_swa_g, grp_fox_g, w_out, post_mix_g, pre_ffn_g,
        w_up, conv_w, conv_b, w_down, post_ffn_g,
    )
    return second_block(
        x, mem_2, norm_mix_2, w_in_2, w_gla_gate_up_2, b_gla_gate_2, sgu_norm_2, w_sgu_2,
        b_sgu_2, out_norm_2, w_out_2, norm_xattn_2, norm_mem_2, w_xq_2, w_xkv_2, w_xo_2,
        final_norm_2,
    )


_drawn_inputs = setup_inputs


def setup_inputs(seed=0):
    import zlib

    import numpy as np

    out = dict(_drawn_inputs(seed))
    spreads = {}
    factors = {'conv_b': 3.208,
     'norm_mix_2': 5.144,
     'b_gla_gate_2': 7.893,
     'sgu_norm_2': 8.0,
     'b_sgu_2': 6.186,
     'out_norm_2': 8.0,
     'norm_xattn_2': 8.0,
     'norm_mem_2': 8.0,
     'final_norm_2': 2.76}
    for name, (base, spread) in spreads.items():
        noise = np.random.default_rng([zlib.crc32(name.encode()), seed]).standard_normal(out[name].shape)
        drawn = base * np.exp(spread * noise) if base else spread * noise
        out[name] = __import__('jax').numpy.asarray(drawn.astype(out[name].dtype))
    for name, factor in factors.items():
        out[name] = (out[name] * factor).astype(out[name].dtype)
    return out
```

```python
from contextlib import ExitStack

import concourse.bass as bass
from concourse import mybir

F32 = mybir.dt.float32
F32R = mybir.dt.float32r
BF16 = mybir.dt.bfloat16
I32 = mybir.dt.int32
ALU = mybir.AluOpType
ACT = mybir.ActivationFunctionType
AX = mybir.AxisListType.X

P = 128
S = 256
NB = S // P
D = 2048
KC = D // P
EPS = 1e-6
BIG = 1e30

HD = 64
NH = 16
D_SWA = NH * HD
WINDOW = 128
D_FF = 5632
FFT = D_FF // P
QA, KA, VA, QB, KB, VB, FB = 0, 1024, 1152, 1280, 2304, 3328, 4352
SBQ, SBK, SBV, SBG = 0, 1024, 2048, 3072
GLQ, GLV, GLR, GLG = 4096, 4608, 5120, 5136
SGUU, SGUV, SGUG = 5648, 6160, 6672
SB_HEADS = 8
GLA_HEADS = 4
GATE_RANK = 16
GATE_TAU = 16.0
SGU_GROUPS = 4
XA_HEADS = 4
WIDE_SCALE = 128 ** -0.5

W = 512
PIECE = 1024
SLOTS = 4

PLAN = (
    [("kv_a", 4), ("q_a", 8), ("q_a", 8), ("v_b", 8), ("v_b", 8), ("q_b", 8), ("k_b", 8), ("q_b", 8), ("k_b", 8)]
    + [("w_out", 8)] * 4 + [("w_up", 8)] * 22 + [("w_down", 24)] * 4
    + [("gla_qk", 8), ("gla_v", 8)] + [("sb_q", 8)] * 2 + [("sb_k", 8)] * 2 + [("sb_v", 8)] * 2
    + [("gla_g", 8), ("sgu_u", 8), ("sgu_v", 8), ("sgu_g", 8)] + [("sb_g", 8)] * 2
    + [("xk", 8), ("xv", 8)] + [("w_out2", 8)] * 4 + [("xq", 8)] + [("xo", 2)] * 4
)
FIRST_PIECE = [sum(n for _, n in PLAN[:g]) for g in range(len(PLAN) + 1)]
GROUP = {}
for _g, (_name, _n) in enumerate(PLAN):
    GROUP.setdefault(_name, []).append(_g)
TOTAL = FIRST_PIECE[-1]
DOWN = [2] * 20 + [1] * 4

GAINS = ["pre_mix", "grp", "pre_ffn", "norm_mix_2", "out_norm_2", "norm_mem_2", "norm_xattn_2"]
GAIN_AT = {n: i * KC for i, n in enumerate(GAINS)}
BSGU_AT = KC * len(GAINS)
GAIN_ROWS = BSGU_AT + SGU_GROUPS
PHASES = ["pre_mix", "grp", "pre_ffn", "norm_mix_2", "norm_mem_2", "out_norm_2", "norm_xattn_2"]


def build(nc, A, out):
    with ExitStack() as ctx:
        def sem(name):
            return ctx.enter_context(nc.semaphore(name))

        def region(specs):
            with ExitStack() as scope:
                return [scope.enter_context(nc.sbuf_tensor(n, shape, dt)) for n, shape, dt in specs]

        def keep(name, shape, dt=F32):
            return ctx.enter_context(nc.sbuf_tensor(name, shape, dt))

        x_tok = keep("x_tok", [P, NB, D])
        raw = keep("raw", [P, SLOTS, PIECE])
        w_hi = keep("w_hi", [P, SLOTS, PIECE], F32R)
        w_lo = keep("w_lo", [P, SLOTS, PIECE], F32R)
        ident = keep("ident", [P, P])
        tri = keep("tri", [P, P])
        ones = keep("ones", [P, P])
        gains = keep("gains", [P, GAIN_ROWS])
        conv = keep("conv", [P, 4, 2 * FFT])
        fr_raw = keep("fr_raw", [P, KC, 16])
        fr_hi = keep("fr_hi", [P, KC, 16], F32R)
        fr_lo = keep("fr_lo", [P, KC, 16], F32R)
        stat = keep("stat", [P, 4 * 64])

        hT_hi, hT_lo = region([("hT_hi", [P, KC, S], F32R), ("hT_lo", [P, KC, S], F32R)])
        y_tok, ffn_gain = region([("y_tok", [P, NB, D], F32), ("ffn_gain", [P, D], F32)])
        hold = ctx.enter_context(nc.sbuf_tensor("h_place", [P, 2 * KC * S], F32))

        (work, mix_gain, qaT, kaT, ka2, va, qbT, kbT, vb, sel, distm, foxm, probs, probsT, biased, sink, sink8,
         bf, fz, fm, fa, lf, c8, cT8, gain_rows, conv_rows, junk, junk_d) = region([
             ("work", [P, NB, D], F32), ("mix_gain", [P, D], F32), ("qaT", [P, 8, S], F32), ("kaT", [P, S], F32),
             ("ka2", [P, 2, S], F32), ("va", [P, NB, P], F32), ("qbT", [P, 8, S], F32), ("kbT", [P, 8, S], F32),
             ("vb", [P, NB, 1024], F32), ("sel", [16, NH, P], F32), ("distm", [P, 384], F32), ("foxm", [P, 384], F32),
             ("probs", [P, 2, 384], F32), ("probsT", [P, 2, 384], F32), ("biased", [P, 2, 384], F32),
             ("sink", [P, NH], F32), ("sink8", [P, NH], F32), ("bf", [P, 16], F32), ("fz", [P, NB, 16], F32),
             ("fm", [P, NB, 16], F32), ("fa", [P, NB, 16], F32), ("lf", [P, NB, 16], F32), ("c8", [P, NB, 16], F32),
             ("cT8", [16, S], F32), ("gain_rows", [GAIN_ROWS, P], F32), ("conv_rows", [2 * FFT, 4, P], F32),
             ("junk", [P, 2048], BF16), ("junk_d", [P, 2048], BF16)])
        g_hi, g_lo, cv_gate, cv_val, coef = region([
            ("g_hi", [P, FFT, S], F32R), ("g_lo", [P, FFT, S], F32R), ("cv_gate", [P, 4, S], F32),
            ("cv_val", [P, 4, S], F32), ("coef", [P, 2, 4, 4], F32)])
        with ExitStack() as scope:
            def loc(name, shape, dt=F32):
                return scope.enter_context(nc.sbuf_tensor(name, shape, dt))
            mix2 = loc("mix2", [P, NB, D])
            with ExitStack() as inner:
                def part(name, shape, dt=F32):
                    return inner.enter_context(nc.sbuf_tensor(name, shape, dt))
                gqk = part("gqk", [P, 2, 2, S])
                gvv = part("gvv", [P, NB, 512])
                la = part("la", [P, NB, S])
                gm = part("gm", [P, NB, S])
                bT = part("bT", [P, 2, S])
                rel = part("rel", [P, 2 * S])
            with ExitStack() as inner:
                x_p = inner.enter_context(nc.sbuf_tensor("x_p", [P, XA_HEADS, 512], F32))
                x_pT = inner.enter_context(nc.sbuf_tensor("x_pT", [P, 2, 512], F32))
            gate = loc("gate", [P, NB, D])
            with ExitStack() as inner:
                sbq = inner.enter_context(nc.sbuf_tensor("sbq", [P, 8, S], F32))
                sbk = inner.enter_context(nc.sbuf_tensor("sbk", [P, 8, S], F32))
            mem_tok = loc("mem_tok", [P, NB, D])
            sbv = loc("sbv", [P, NB, 1024])
            xkT = loc("xkT", [P, XA_HEADS, S])
            xv = loc("xv", [P, NB, 512])
            with ExitStack() as inner:
                xor_s = inner.enter_context(nc.sbuf_tensor("xor_s", [P, P], I32))
                xor_t = inner.enter_context(nc.sbuf_tensor("xor_t", [P, P], I32))
                lev = inner.enter_context(nc.sbuf_tensor("lev", [P, P], F32))
            sgu_u = loc("sgu_u", [P, NB, 512])
            sgu_v = loc("sgu_v", [P, NB, 512])
            sgu_gain = loc("sgu_gain", [P, 512])
            w_sgu = loc("w_sgu", [P, SGU_GROUPS, P])
            w_sguT = loc("w_sguT", [P, SGU_GROUPS, P])
            sb_neg = loc("sb_neg", [P, P])
            sb_one = loc("sb_one", [P, P])
            tri_neg = loc("tri_neg", [P, P])
            ones_neg = loc("ones_neg", [P, P])
            with ExitStack() as inner:
                def part(name, shape, dt=F32):
                    return inner.enter_context(nc.sbuf_tensor(name, shape, dt))
                rT = part("rT", [16, S])
                wgu = part("wgu", [16, S])
                bgg = part("bgg", [1, S])
                decay = part("decay", [P, 2, 2 * S])
                qkd = part("qkd", [P, 2, 2, S])
                acc = part("acc", [P, NB, 512])
                inter = part("inter", [P, 512])
                prod = part("prod", [P, 512])
                levels = part("levels", [P, 8, P])
            with ExitStack() as inner:
                def part(name, shape, dt=F32):
                    return inner.enter_context(nc.sbuf_tensor(name, shape, dt))
                z_s = part("z_s", [P, 2, 384])
                z_m = part("z_m", [P, 2, 384])
                z_e = part("z_e", [P, 2, 384])
                z_p = part("z_p", [P, 2, 384])
                z_a = part("z_a", [P, 2, 384])
            with ExitStack() as inner:
                def part(name, shape, dt=F32):
                    return inner.enter_context(nc.sbuf_tensor(name, shape, dt))
                out_gain = part("out_gain", [P, D])
                junk2 = part("junk2", [P, 2048], BF16)
                junk2_d = part("junk2_d", [P, 2048], BF16)

        bank = [ctx.enter_context(nc.psum_tensor(f"bank{i}", [P, 512], F32)) for i in range(4)]
        upper = ctx.enter_context(nc.psum_tensor("upper", [P, 4, 512], F32))
        bank += [upper[:, i, :] for i in range(4)]

        raw_loaded = [sem(f"raw_loaded{i}") for i in range(SLOTS)]
        hi_ready, lo_ready, mm_done = sem("hi_ready"), sem("lo_ready"), sem("mm_done")
        banks_free = sem("banks_free")
        x_loaded, rows_loaded, consts_loaded = sem("x_loaded"), sem("rows_loaded"), sem("consts_loaded")
        fr_loaded, fr_split_hi, fr_split_lo, fr_done = sem("fr_loaded"), sem("fr_split_hi"), sem("fr_split_lo"), sem("fr_done")
        pool_ready, dve_ready = sem("pool_ready"), sem("dve_ready")
        rows_T, tables_ready = sem("rows_T"), sem("tables_ready")
        squares, mean_ready, root_ready, rstd_ready, scaled = (
            sem("squares"), sem("mean_ready"), sem("root_ready"), sem("rstd_ready"), sem("scaled"))
        squares_d = sem("squares_d")
        tr_done, hiT_done, loT_done = sem("tr_done"), sem("hiT_done"), sem("loT_done")
        k_copied = sem("k_copied")
        f_z, f_abs, f_exp, f_ln, f_min, f_log, f_cum, f_c = [sem("f_" + n) for n in ("z", "abs", "exp", "ln", "min", "log", "cum", "c")]
        scores_done, biased_done, row_max, neg_max, exp_done, den_done, recip_done, probs_T, probsT_copied, pv_done, out_done = [
            sem(n) for n in ("scores_done", "biased_done", "row_max", "neg_max", "exp_done", "den_done", "recip_done",
                             "probs_T", "probsT_copied", "pv_done", "out_done")]
        gain_loaded, y_scaled, x_added = sem("gain_loaded"), sem("y_scaled"), sem("x_added")
        coef_ready, conv_tap2, conv_tap1, gelu_done, glu_done, g_hi_done, g_lo_done = [
            sem(n) for n in ("coef_ready", "conv_tap2", "conv_tap1", "gelu_done", "glu_done", "g_hi_done", "g_lo_done")]
        second_loaded, second_pool, second_dve = sem("second_loaded"), sem("second_pool"), sem("second_dve")
        r_copied, gate_logits, ga_abs, ga_exp, ga_ln, ga_min, ga_log, cum_done, b_ready = [
            sem(n) for n in ("r_copied", "gate_logits", "ga_abs", "ga_exp", "ga_ln", "ga_min", "ga_log", "cum_done", "b_ready")]
        rel_ready, clamped, decayed, qk_decayed, level_scores, level_masked, level_added, gla_out, gla_copied = [
            sem(n) for n in ("rel_ready", "clamped", "decayed", "qk_decayed", "level_scores", "level_masked", "level_added", "gla_out", "gla_copied")]
        z_done, zs_done, zabs_done, zexp_done, zln_done, zmask_done, zmax_done, sp_done, spm_done, inc_done, t_done, a_done, so_done, so_copied = [
            sem(n) for n in ("z_done", "zs_done", "zabs_done", "zexp_done", "zln_done", "zmask_done", "zmax_done", "sp_done",
                             "spm_done", "inc_done", "t_done", "a_done", "so_done", "so_copied")]
        sgu_sq, sgu_mean, sgu_root, sgu_rstd, sgu_vn, sguT_done, sguT_ready, sgu_mixed, sgu_done = [
            sem(n) for n in ("sgu_sq", "sgu_mean", "sgu_root", "sgu_rstd", "sgu_vn", "sguT_done", "sguT_ready", "sgu_mixed", "sgu_done")]
        mem_loaded, hsq_done, hsum_done, hmean, hroot, hrstd, hscaled, hgated = [
            sem(n) for n in ("mem_loaded", "hsq_done", "hsum_done", "hmean", "hroot", "hrstd", "hscaled", "hgated")]
        xs_done, xmax_done, xneg_done, xexp_done, xrecip_done, xnorm_done, xpT_done, xpT_copied, xo_done, xo_hi, xo_lo = [
            sem(n) for n in ("xs_done", "xmax_done", "xneg_done", "xexp_done", "xrecip_done", "xnorm_done", "xpT_done",
                             "xpT_copied", "xo_done", "xo_hi", "xo_lo")]
        out_scaled, stored = sem("out_scaled"), sem("stored")

        def st(k, n=2):
            return stat[:, 4 * k:4 * k + n]

        def wide(t, s, kcs, w):
            return t[:, s, 0:kcs * w].rearrange("p (k n) -> p k n", k=kcs)

        def broadcast(ap, shape):
            return ap.unsqueeze(2).broadcast_to(shape)

        def evacuated(g, off=0):
            return 2 * (g + 1) + off

        def piece_size(u):
            g = max(i for i in range(len(PLAN)) if FIRST_PIECE[i] <= u)
            return P * 4 if PLAN[g][0] == "w_down" and u - FIRST_PIECE[g] >= 20 else PIECE

        block = ctx.enter_context(nc.Block())

        @block.sync
        def _(sp):
            def load(src, row, kcs, col, w, u, i=None, step=0):
                s = u % SLOTS
                if u >= SLOTS:
                    sp.wait_ge(lo_ready, u - SLOTS + 1 + (0 if i is None else i * step))
                rows = src[row:row + kcs * P]
                cols = rows[:, col:col + w] if i is None or isinstance(col, int) else rows[:, bass.ds(col, w)]
                sp.dma_start(wide(raw, s, kcs, w), cols.rearrange("(k p) n -> p k n", p=P)).then_inc(raw_loaded[s], 16)

            def group(src, col, g, i=None, step=0, pieces=(2,) * 8, w=W):
                row = 0
                for j, kcs in enumerate(pieces):
                    load(src, row, kcs, col, w, FIRST_PIECE[g] + j, i, step)
                    row += kcs * P

            w_in = A["w_in"][0]
            xr = A["x"][0].rearrange("(b p) d -> b p d", p=P)
            for b in range(NB):
                sp.dma_start(x_tok[:, b, :], xr[b]).then_inc(x_loaded, 16)
            group(w_in, KA, 0, pieces=(4,) * 4, w=256)
            sp.dma_start(fr_raw[:, :, :], w_in[:, FB:FB + 16].rearrange("(k p) n -> p k n", p=P)).then_inc(fr_loaded, 16)
            for g, col in enumerate([QA, QA + W, VB, VB + W, QB, KB, QB + W, KB + W], 1):
                group(w_in, col, g)
            with sp.Fori(0, 2) as i:
                for e in range(2):
                    group(A["w_out"][0], i * (2 * W) + e * W, GROUP["w_out"][e], i, 16)
            with sp.Fori(0, 11) as i:
                for e in range(2):
                    group(A["w_up"][0], i * W + e * D_FF, GROUP["w_up"][e], i, 16)
            with sp.Fori(0, 2) as i:
                for e in range(2):
                    group(A["w_down"][0], i * (2 * W) + e * W, GROUP["w_down"][e], i, 48, pieces=DOWN)
            w_in2 = A["w_in_2"][0]
            sp.wait_ge(fr_split_lo, 1)
            sp.dma_start(fr_raw[:, :, :], w_in2[:, GLR:GLR + 16].rearrange("(k p) n -> p k n", p=P)).then_inc(fr_loaded, 16)
            group(w_in2, GLQ, GROUP["gla_qk"][0])
            group(w_in2, GLV, GROUP["gla_v"][0])
            with sp.Fori(0, 3) as i:
                for e in range(2):
                    group(w_in2, i * (2 * W) + e * W, GROUP["sb_q"][e], i, 16)
            for n, col in (("gla_g", GLG), ("sgu_u", SGUU), ("sgu_v", SGUV), ("sgu_g", SGUG)):
                group(w_in2, col, GROUP[n][0])
            for e in range(2):
                group(w_in2, SBG + e * W, GROUP["sb_g"][e])
                if e == 0:
                    sp.wait_ge(z_done, SB_HEADS)
                    mr = A["mem_2"][0].rearrange("(b p) d -> b p d", p=P)
                    for b in range(NB):
                        sp.dma_start(mem_tok[:, b, :], mr[b]).then_inc(mem_loaded, 16)
            group(A["w_xkv_2"][0], 0, GROUP["xk"][0])
            group(A["w_xkv_2"][0], W, GROUP["xv"][0])
            with sp.Fori(0, 2) as i:
                for e in range(2):
                    group(A["w_out_2"][0], i * (2 * W) + e * W, GROUP["w_out2"][e], i, 16)
            group(A["w_xq_2"][0], 0, GROUP["xq"][0])
            for e in range(4):
                group(A["w_xo_2"][0], e * W, GROUP["xo"][e], pieces=(2, 2))
            orr = out[0].rearrange("(b p) d -> b p d", p=P)
            for b in range(NB):
                sp.wait_ge(out_scaled, b + 1)
                sp.dma_start(orr[b], x_tok[:, b, :]).then_inc(stored, 16)
            sp.wait_ge(stored, 16 * NB)

        @block.gpsimd
        def _(pool):
            def gain(name, lo, n, src):
                r = GAIN_AT[name] + lo
                pool.dma_start(gain_rows[r:r + n, :], src[0].rearrange("(k p) -> k p", p=P)).then_inc(rows_loaded, 16)
            gain("pre_mix", 0, 16, A["pre_mix_g"])
            gain("grp", 0, 8, A["grp_swa_g"])
            gain("grp", 8, 8, A["grp_fox_g"])
            gain("pre_ffn", 0, 16, A["pre_ffn_g"])
            gain("norm_mix_2", 0, 16, A["norm_mix_2"])
            gain("out_norm_2", 0, 16, A["out_norm_2"])
            gain("norm_mem_2", 0, 16, A["norm_mem_2"])
            gain("norm_xattn_2", 0, 16, A["norm_xattn_2"])
            pool.dma_start(gain_rows[BSGU_AT:BSGU_AT + SGU_GROUPS, :], A["b_sgu_2"][0]).then_inc(rows_loaded, 16)
            pool.dma_start(conv_rows[:, 0:3, :], A["conv_w"][0].rearrange("c (t p) -> t c p", p=P)).then_inc(rows_loaded, 16)
            pool.dma_start(conv_rows[:, 3, :], A["conv_b"][0].rearrange("(t p) -> t p", p=P)).then_inc(rows_loaded, 16)
            pool.dma_start(sink[:, :], A["sinks"][0].partition_broadcast(P)).then_inc(consts_loaded, 16)
            pool.dma_start(bf[:, :], A["b_forget"][0].partition_broadcast(P)).then_inc(consts_loaded, 16)
            pool.dma_start(mix_gain[:, :], A["post_mix_g"][0].partition_broadcast(P)).then_inc(gain_loaded, 16)
            pool.memset(ident[:, :], 0.0).then_inc(pool_ready, 1)
            pool.memset(tri[:, :], 1.0).then_inc(pool_ready, 1)
            pool.memset(foxm[:, :], 0.0).then_inc(pool_ready, 1)
            pool.memset(sel[:, :, :], 0.0).then_inc(pool_ready, 1)
            pool.iota(distm[:, 0:128], [[-1, 128]], base=0, channel_multiplier=1, allow_small_or_imprecise_dtypes=True).then_inc(pool_ready, 1)
            pool.iota(distm[:, 128:384], [[-1, 256]], base=128, channel_multiplier=1, allow_small_or_imprecise_dtypes=True).then_inc(pool_ready, 1)
            pool.wait_ge(pool_ready, 6)
            pool.affine_select(out=ident[:, :], in_=ident[:, :], compare_op=ALU.not_equal, fill=1.0, base=0,
                               pattern=[[-1, P]], channel_multiplier=1).then_inc(pool_ready, 1)
            pool.affine_select(out=tri[:, :], in_=tri[:, :], compare_op=ALU.is_ge, fill=0.0, base=0,
                               pattern=[[1, P]], channel_multiplier=-1).then_inc(pool_ready, 1)
            pool.affine_select(out=sel[:, :, :], in_=sel[:, :, :], compare_op=ALU.not_equal, fill=1.0, base=0,
                               pattern=[[-1, NH], [0, P]], channel_multiplier=1).then_inc(pool_ready, 1)
            for t, fill in ((distm, BIG), (foxm, -BIG)):
                pool.affine_select(out=t[:, 0:128], in_=t[:, 0:128], compare_op=ALU.is_ge, fill=fill, base=0,
                                   pattern=[[-1, 128]], channel_multiplier=1).then_inc(pool_ready, 1)
                pool.affine_select(out=t[:, 128:384], in_=t[:, 128:384], compare_op=ALU.is_ge, fill=fill, base=128,
                                   pattern=[[-1, 256]], channel_multiplier=1).then_inc(pool_ready, 1)
            pool.wait_ge(pool_ready, 13)
            pool.affine_select(out=distm[:, 128:384], in_=distm[:, 128:384], compare_op=ALU.is_ge, fill=BIG,
                               base=WINDOW - 1 - 128, pattern=[[1, 256]], channel_multiplier=-1).then_inc(pool_ready, 1)
            pool.wait_ge(banks_free, evacuated(0))
            for kv in range(2):
                for half in range(2):
                    pool.dma_start(ka2[half * HD:(half + 1) * HD, kv, :], kaT[kv * HD:(kv + 1) * HD, :]).then_inc(k_copied, 16)
            pool.wait_ge(mm_done, FIRST_PIECE[GROUP["w_down"][0]])
            pool.dma_start(ffn_gain[:, :], A["post_ffn_g"][0].partition_broadcast(P)).then_inc(gain_loaded, 16)
            pool.wait_ge(mm_done, FIRST_PIECE[GROUP["gla_qk"][0]])
            pool.dma_start(wgu[:, :], A["w_gla_gate_up_2"][0]).then_inc(second_loaded, 16)
            pool.dma_start(bgg[:, :], A["b_gla_gate_2"][0].rearrange("(a n) -> a n", a=1)).then_inc(second_loaded, 16)
            pool.dma_start(sgu_gain[:, :], A["sgu_norm_2"][0].partition_broadcast(P)).then_inc(second_loaded, 16)
            pool.dma_start(w_sgu[:, :, :], A["w_sgu_2"][0].rearrange("g t s -> t g s")).then_inc(second_loaded, 16)
            pool.iota(xor_s[:, :], [[0, P]], base=0, channel_multiplier=1).then_inc(second_pool, 1)
            pool.iota(xor_t[:, :], [[1, P]], base=0, channel_multiplier=0).then_inc(second_pool, 1)
            pool.memset(sb_neg[:, :], 0.0).then_inc(second_pool, 1)
            pool.memset(sb_one[:, :], 1.0).then_inc(second_pool, 1)
            pool.memset(tri_neg[:, :], -1.0).then_inc(second_pool, 1)
            pool.memset(ones_neg[:, :], -1.0).then_inc(second_pool, 1)
            pool.wait_ge(second_pool, 6)
            pool.affine_select(out=sb_neg[:, :], in_=sb_neg[:, :], compare_op=ALU.is_gt, fill=-BIG, base=0,
                               pattern=[[1, P]], channel_multiplier=-1).then_inc(second_pool, 1)
            pool.affine_select(out=sb_one[:, :], in_=sb_one[:, :], compare_op=ALU.is_gt, fill=0.0, base=0,
                               pattern=[[1, P]], channel_multiplier=-1).then_inc(second_pool, 1)
            pool.affine_select(out=tri_neg[:, :], in_=tri_neg[:, :], compare_op=ALU.is_ge, fill=0.0, base=0,
                               pattern=[[-1, P]], channel_multiplier=1).then_inc(second_pool, 1)
            pool.wait_ge(so_copied, SB_HEADS)
            pool.dma_start(out_gain[:, :], A["final_norm_2"].partition_broadcast(P)).then_inc(gain_loaded, 16)

        @block.scalar
        def _(act):
            def split(u, i=None, step=0, n=None):
                if u >= TOTAL:
                    return
                s = u % SLOTS
                n = n or piece_size(u)
                act.wait_ge(raw_loaded[s], 16 * (u // SLOTS + 1) + (0 if i is None else i * (16 * step // SLOTS)))
                if u >= SLOTS:
                    act.wait_ge(mm_done, u - SLOTS + 1 + (0 if i is None else i * step))
                act.activation(w_hi[:, s, 0:n], raw[:, s, 0:n], ACT.Copy).then_inc(hi_ready, 1)

            def group(g, i=None, step=0, side=None):
                u = FIRST_PIECE[g]
                for j in range(PLAN[g][1]):
                    split(u + j + SLOTS, i, step)
                    if side:
                        side(j)
                act.wait_ge(mm_done, FIRST_PIECE[g + 1] + (0 if i is None else i * step))

            def out_of(g, b):
                return bank[2 * (g % 2) + b][:, :]

            def copy_out(dst, g, b=0, func=ACT.Copy):
                act.activation(dst, out_of(g, b), func).then_inc(banks_free, 1)

            def phase(n):
                at = GAIN_AT[PHASES[n]]
                if n == 0:
                    act.wait_ge(tables_ready, 1)
                for c in range(KC):
                    if c % 2 == 0:
                        act.wait_ge(tr_done, (KC * n + c) // 2 + 1)
                    ins = act.activation(hT_hi[:, c, :], bank[4 + c // 2 % 4][:, c % 2 * S:(c % 2 + 1) * S], ACT.Copy,
                                         scale=gains[:, at + c:at + c + 1])
                    if c % 2:
                        ins.then_inc(hiT_done, 1)

            n_squares = [0]

            def square(src, col, done, jk):
                if done is squares:
                    if n_squares[0]:
                        act.wait_ge(squares, n_squares[0])
                    n_squares[0] += 1
                act.activation(jk, src, ACT.Square, accum_out=col).then_inc(done, 1)

            def root(n, k, wait, done, width=2):
                act.wait_ge(wait, n)
                act.activation(stat[:, 4 * k:4 * k + width], stat[:, 4 * k:4 * k + width], ACT.Sqrt).then_inc(done, 1)

            for b in range(2):
                act.wait_ge(x_loaded, 32)
                square(x_tok[:, b, :], st(0)[:, b:b + 1], squares, junk[:, :])
            root(1, 0, mean_ready, root_ready)
            for u in range(SLOTS):
                split(u)
            act.wait_ge(fr_loaded, 16)
            act.activation(fr_hi[:, :, :], fr_raw[:, :, :], ACT.Copy).then_inc(fr_split_hi, 1)
            phase(0)

            def probs_copy(i):
                act.wait_ge(probs_T, i + 1)
                if i >= 2:
                    act.wait_ge(pv_done, i - 1)
                act.activation(probsT[:, i % 2, :], bank[6][:, 0:384], ACT.Copy).then_inc(probsT_copied, 1)

            def exps(i):
                act.wait_ge(neg_max, i + 1)
                if i >= 2:
                    act.wait_ge(probs_T, i - 1)
                    act.wait_ge(recip_done, i - 1)
                s = i % 2
                nm, den, es = st(8 + s), st(10 + s), st(12 + s)
                if i < NH:
                    act.activation(es, nm, ACT.Exp, bias=sink[:, i:i + 1]).then_inc(exp_done, 1)
                else:
                    act.activation(es, nm, ACT.Exp).then_inc(exp_done, 1)
                act.activation(probs[:, s, 0:128], biased[:, s, 0:128], ACT.Exp, bias=nm[:, 0:1], scale=HD ** -0.5,
                               accum_out=den[:, 0:1]).then_inc(exp_done, 1)
                act.activation(probs[:, s, 128:384], biased[:, s, 128:384], ACT.Exp, bias=nm[:, 1:2], scale=HD ** -0.5,
                               accum_out=den[:, 1:2]).then_inc(exp_done, 1)

            def head(i):
                if 1 <= i <= 2 * NH:
                    probs_copy(i - 1)
                if i < 2 * NH:
                    exps(i)

            group(0)
            act.activation(kaT[:, :], bank[0][:, 0:S], ACT.Copy).then_inc(banks_free, 1)
            act.wait_ge(f_z, 1)
            act.activation(fa[:, :, :], fz[:, :, :], ACT.Abs).then_inc(f_abs, 1)
            act.wait_ge(f_abs, 1)
            act.activation(fa[:, :, :], fa[:, :, :], ACT.Exp, scale=-1.0).then_inc(f_exp, 1)
            act.wait_ge(f_exp, 1)
            act.activation(fa[:, :, :], fa[:, :, :], ACT.Ln, bias=1.0).then_inc(f_ln, 1)
            for g in (1, 2):
                group(g)
                copy_out(qaT[:, 4 * (g - 1):4 * (g - 1) + 2, :].rearrange("p a b -> p (a b)"), g)
            for g in (3, 4):
                group(g, side=lambda j, g=g: head(4 * (g - 3) + j // 2) if j % 2 else None)
                copy_out(vb[:, 0, W * (g - 3):W * (g - 2)], g)
            for n, g in enumerate((5, 6, 7, 8)):
                group(g, side=lambda j, n=n: head(8 + 4 * n + j // 2) if j % 2 else None)
                dst = (qbT, kbT)[n % 2]
                copy_out(dst[:, 4 * (n // 2):4 * (n // 2) + 2, :].rearrange("p a b -> p (a b)"), g)
            for i in range(24, 2 * NH + 2):
                head(i)
            act.wait_ge(out_done, 2 * NH)
            for b in range(NB):
                for k in range(2):
                    square(work[:, b, 1024 * k:1024 * (k + 1)], stat[:, 4 + 2 * b + k:5 + 2 * b + k], squares, junk[:, 0:1024])
            root(2, 1, mean_ready, root_ready, 4)
            phase(1)
            with act.Fori(0, 2) as i:
                for e in range(2):
                    g = GROUP["w_out"][e]
                    group(g, i, 16)
                    act.activation(work[:, 0, bass.ds(i * (2 * W) + e * W, W)], out_of(g, 0), ACT.Copy).then_inc(banks_free, 1)

            def post(k, src, n_sq, jk, m):
                act.wait_ge(banks_free, m)
                square(src, st(k)[:, 0:1], squares, jk)
                root(n_sq, k, mean_ready, root_ready)

            post(2, work[:, 0, :], 3, junk[:, :], evacuated(GROUP["w_out"][3]))
            act.wait_ge(x_added, 1)
            square(x_tok[:, 0, :], st(3)[:, 0:1], squares, junk[:, :])
            root(4, 3, mean_ready, root_ready)
            phase(2)
            with act.Fori(0, 11) as i:
                for e in range(2):
                    g = GROUP["w_up"][e]
                    group(g, i, 16)
                    cv = (cv_gate, cv_val)[e]
                    act.wait_ge(coef_ready, i + 1)
                    for ft in range(4):
                        ins = act.activation(cv[:, ft, :], bank[2 * (g % 2) + ft // 2][:, ft % 2 * S:(ft % 2 + 1) * S], ACT.Identity,
                                             bias=coef[:, e, 3, ft:ft + 1], scale=coef[:, e, 2, ft:ft + 1])
                    ins.then_inc(conv_tap2, 1)
                    if e == 0:
                        act.wait_ge(banks_free, evacuated(g) + i * 4)
                        act.activation(cv_gate[:, :, :], cv_gate[:, :, :], ACT.Gelu_apprx_tanh).then_inc(gelu_done, 1)
                act.wait_ge(glu_done, i + 1)
                act.activation(g_hi[:, bass.ds(i * 4, 4), :], cv_val[:, :, :], ACT.Copy).then_inc(g_hi_done, 1)
                act.wait_ge(g_lo_done, i + 1)
            with act.Fori(0, 2) as i:
                for e in range(2):
                    g = GROUP["w_down"][e]
                    group(g, i, 48)
                    act.activation(y_tok[:, 0, bass.ds(i * (2 * W) + e * W, W)], out_of(g, 0), ACT.Copy).then_inc(banks_free, 1)
            post(4, y_tok[:, 0, :], 5, junk2[:, :], evacuated(GROUP["w_down"][3]))
            act.wait_ge(x_added, 2)
            square(x_tok[:, 0, :], st(5)[:, 0:1], squares, junk2[:, :])
            root(6, 5, mean_ready, root_ready)
            act.wait_ge(fr_loaded, 32)
            act.wait_ge(fr_done, 1)
            act.activation(fr_hi[:, :, :], fr_raw[:, :, :], ACT.Copy).then_inc(fr_split_hi, 1)
            phase(3)

            g = GROUP["gla_qk"][0]
            group(g)
            act.activation(gqk[:, 0, :, :].rearrange("p a b -> p (a b)"), out_of(g, 0), ACT.Copy, scale=HD ** -0.5).then_inc(banks_free, 1)
            g = GROUP["gla_v"][0]
            act.wait_ge(fr_done, 2)
            act.activation(rT[:, :], bank[4][0:16, 0:S], ACT.Copy).then_inc(r_copied, 1)
            group(g)
            copy_out(gvv[:, 0, :], g)

            def gate_logs():
                act.wait_ge(gate_logits, 1)
                act.activation(la[:, :, :].rearrange("p a b -> p (a b)"), bank[5][:, :], ACT.Abs).then_inc(ga_abs, 1)
                act.wait_ge(ga_abs, 1)
                act.activation(la[:, :, :], la[:, :, :], ACT.Exp, scale=-1.0).then_inc(ga_exp, 1)
                act.wait_ge(ga_exp, 1)
                act.activation(la[:, :, :], la[:, :, :], ACT.Ln, bias=1.0).then_inc(ga_ln, 1)
                act.wait_ge(cum_done, 1)
                act.activation(bT[:, :, :].rearrange("p a b -> p (a b)"), bank[6][:, :], ACT.Copy, scale=1.0 / GATE_TAU).then_inc(b_ready, 1)

            def level(n):
                if n < 8:
                    act.wait_ge(clamped, n + 1)
                    act.activation(decay[:, :, :], decay[:, :, :], ACT.Exp).then_inc(decayed, 1)

            def gla_side(n):
                if n == 0:
                    gate_logs()
                elif n <= 9:
                    level(n - 1)
                elif n == 10:
                    act.wait_ge(gla_out, 2)
                    act.activation(mix2[:, 0, 1024:1536], bank[6][:, :], ACT.Copy).then_inc(gla_copied, 1)

            dsts = [(sbq, 0), (sbq, 4), (sbk, 0), (sbk, 4)]
            for n in range(6):
                g = GROUP["sb_q"][0] + n
                group(g, side=lambda j, n=n: gla_side(2 * n + j // 4) if j % 4 == 3 else None)
                if n < 4:
                    copy_out(dsts[n][0][:, dsts[n][1]:dsts[n][1] + 2, :].rearrange("p a b -> p (a b)"), g)
                else:
                    copy_out(sbv[:, 0, W * (n - 4):W * (n - 3)], g)

            def stick(i):
                if i < SB_HEADS:
                    s = i % 2
                    act.wait_ge(z_done, i + 1)
                    if i >= 2:
                        act.wait_ge(zmask_done, i - 1)
                        act.wait_ge(zmax_done, i - 1)
                    act.activation(z_s[:, s, :], bank[4][:, 0:384], ACT.Copy, scale=WIDE_SCALE).then_inc(zs_done, 1)
                    act.wait_ge(zs_done, i + 1)
                    if i >= 2:
                        act.wait_ge(sp_done, i - 1)
                    act.activation(z_e[:, s, :], z_s[:, s, :], ACT.Abs).then_inc(zabs_done, 1)
                    act.wait_ge(zabs_done, i + 1)
                    act.activation(z_e[:, s, :], z_e[:, s, :], ACT.Exp, scale=-1.0).then_inc(zexp_done, 1)
                    act.wait_ge(zexp_done, i + 1)
                    act.activation(z_e[:, s, :], z_e[:, s, :], ACT.Ln, bias=1.0).then_inc(zln_done, 1)
                if 1 <= i <= SB_HEADS:
                    act.wait_ge(t_done, i)
                    if i >= 3:
                        act.wait_ge(so_done, i - 2)
                    act.activation(z_a[:, (i - 1) % 2, :], z_m[:, (i - 1) % 2, :], ACT.Exp).then_inc(a_done, 1)

            def both(dst, g, func):
                for b in range(NB):
                    copy_out(dst[b], g, b, func)

            gates = {"gla_g": 1024, "sgu_g": 1536}
            for n, name in enumerate(("gla_g", "sgu_u", "sgu_v", "sgu_g")):
                g = GROUP[name][0]
                group(g, side=lambda j, n=n: stick(2 * n + j // 4) if j % 4 == 3 else None)
                if name in gates:
                    both([gate[:, b, gates[name]:gates[name] + W] for b in range(NB)], g, ACT.Silu)
                else:
                    t = sgu_u if name == "sgu_u" else sgu_v
                    both([t[:, b, :] for b in range(NB)], g, ACT.Gelu_apprx_tanh)
            for n in range(2):
                g = GROUP["sb_g"][n]

                def side(j, n=n):
                    if n == 0 and j == 1:
                        stick(8)
                    if n == 0 and j == 5:
                        for b in range(NB):
                            act.wait_ge(banks_free, evacuated(GROUP["sgu_v"][0]))
                            square(sgu_v[:, b, :], st(14)[:, b:b + 1], sgu_sq, z_p[:, b, 0:256].bitcast(BF16))
                        root(1, 14, sgu_mean, sgu_root)
                group(g, side=side)
                both([gate[:, b, W * n:W * (n + 1)] for b in range(NB)], g, ACT.Silu)
            act.wait_ge(mem_loaded, 32)
            for b in range(NB):
                square(mem_tok[:, b, :], st(6)[:, b:b + 1], squares, junk2[:, :])
            root(7, 6, mean_ready, root_ready)
            phase(4)
            act.wait_ge(hmean, 1)
            act.activation(stat[:, 128:160], stat[:, 128:160], ACT.Sqrt).then_inc(hroot, 1)
            g = GROUP["xk"][0]
            group(g)
            copy_out(xkT[:, 0:2, :].rearrange("p a b -> p (a b)"), g)
            g = GROUP["xv"][0]
            group(g)
            copy_out(xv[:, 0, :], g)
            phase(5)
            with act.Fori(0, 2) as i:
                for e in range(2):
                    group(GROUP["w_out2"][e], i, 16)
            act.wait_ge(banks_free, evacuated(GROUP["w_out2"][3]))
            square(x_tok[:, 0, :], st(7)[:, 0:1], squares, junk2[:, :])
            root(8, 7, mean_ready, root_ready)
            phase(6)
            g = GROUP["xq"][0]
            group(g)
            copy_out(mix2[:, 0, 0:W], g)
            for h in range(XA_HEADS):
                act.wait_ge(xneg_done, h + 1)
                for b in range(NB):
                    ins = act.activation(x_p[:, h, b * S:(b + 1) * S], bank[4 + h][:, b * S:(b + 1) * S], ACT.Exp,
                                         bias=st(20 + h)[:, b:b + 1], scale=WIDE_SCALE, accum_out=st(24 + h)[:, b:b + 1])
                    ins.then_inc(xexp_done, 1)
            for h in range(XA_HEADS):
                act.wait_ge(xpT_done, h + 1)
                if h >= 2:
                    act.wait_ge(xo_done, h - 1)
                act.activation(x_pT[:, h % 2, :], bank[4 + h][:, :], ACT.Copy).then_inc(xpT_copied, 1)
            for h in range(XA_HEADS):
                act.wait_ge(xo_done, h + 1)
                act.activation(hT_hi[:, h, :], bank[4 + h][:, 0:S], ACT.Copy).then_inc(xo_hi, 1)
            for e in range(4):
                group(GROUP["xo"][e])
            act.wait_ge(banks_free, evacuated(GROUP["xo"][3]))
            square(x_tok[:, 0, :], st(16)[:, 0:1], squares, junk2[:, :])
            root(9, 16, mean_ready, root_ready)

        @block.vector
        def _(dve):
            def split(u, i=None, step=0, n=None):
                if u >= TOTAL:
                    return
                s = u % SLOTS
                n = n or piece_size(u)
                dve.wait_ge(hi_ready, u + 1 + (0 if i is None else i * step))
                dve.tensor_tensor(w_lo[:, s, 0:n], raw[:, s, 0:n], w_hi[:, s, 0:n].bitcast(F32), ALU.subtract).then_inc(lo_ready, 1)

            def group(g, i=None, step=0, side=None):
                u = FIRST_PIECE[g]
                for j in range(PLAN[g][1]):
                    split(u + j + SLOTS, i, step)
                    if side:
                        side(j)
                dve.wait_ge(mm_done, FIRST_PIECE[g + 1] + (0 if i is None else i * step))

            def out_of(g, b):
                return bank[2 * (g % 2) + b][:, :]

            def copy_out(dst, g, b=1):
                dve.tensor_copy(dst, out_of(g, b)).then_inc(banks_free, 1)

            def phase(n):
                at = GAIN_AT[PHASES[n]]
                for c in range(KC):
                    if c % 2 == 0:
                        dve.wait_ge(hiT_done, (KC * n + c) // 2 + 1)
                    dve.scalar_tensor_tensor(out=hT_lo[:, c, :], in0=bank[4 + c // 2 % 4][:, c % 2 * S:(c % 2 + 1) * S],
                                             scalar=gains[:, at + c:at + c + 1], in1=hT_hi[:, c, :].bitcast(F32),
                                             op0=ALU.mult, op1=ALU.subtract).then_inc(loT_done, 1)

            def rstd(n, k, n_sq, size, width=2):
                a = stat[:, 4 * k:4 * k + width]
                dve.wait_ge(squares, n_sq)
                dve.tensor_scalar(a, a, 1.0 / size, EPS, ALU.mult, ALU.add).then_inc(mean_ready, 1)
                dve.wait_ge(root_ready, n)
                dve.reciprocal(a, a).then_inc(rstd_ready, 1)
                dve.wait_ge(rstd_ready, n)

            def square1(src, col, n, jk):
                dve.tensor_tensor_reduce(jk, src, src, 1.0, 0.0, ALU.mult, ALU.add, col).then_inc(squares_d, 1)
                dve.wait_ge(squares_d, n)

            def scale_rows(dst, src, k, n):
                for b in range(NB):
                    dve.tensor_scalar(dst[:, b, :], src[:, b, :], st(k)[:, b:b + 1], None, ALU.mult).then_inc(scaled, 1)

            dve.memset(ones[:, :], 1.0).then_inc(dve_ready, 1)
            dve.wait_ge(consts_loaded, 32)
            dve.tensor_scalar(sink8[:, :], sink[:, :], HD ** 0.5, None, ALU.mult).then_inc(dve_ready, 1)
            rstd(1, 0, 2, D)
            scale_rows(work, x_tok, 0, 0)
            dve.wait_ge(rows_T, 1)
            dve.tensor_copy(gains[:, :], bank[6][:, 0:GAIN_ROWS])
            for c in range(4):
                ins = dve.tensor_copy(conv[:, c, :], bank[7][:, c * 2 * FFT:(c + 1) * 2 * FFT])
            ins.then_inc(tables_ready, 1)
            for u in range(SLOTS):
                split(u)
            dve.wait_ge(fr_split_hi, 1)
            dve.tensor_tensor(fr_lo[:, :, :], fr_raw[:, :, :], fr_hi[:, :, :].bitcast(F32), ALU.subtract).then_inc(fr_split_lo, 1)
            dve.wait_ge(tables_ready, 1)
            phase(0)

            def bias(i):
                s = i % 2
                dve.wait_ge(scores_done, i + 1)
                if i >= 2:
                    dve.wait_ge(exp_done, 3 * (i - 1))
                h = i % NH
                if i < NH:
                    slope = 2.0 ** (-8.0 * (h + 1) / NH)
                    dve.scalar_tensor_tensor(out=biased[:, s, :], in0=distm[:, :], scalar=-slope * HD ** 0.5,
                                             in1=bank[4 + s][:, 0:384], op0=ALU.mult, op1=ALU.add).then_inc(biased_done, 2)
                else:
                    for b, (lo, hi) in enumerate(((0, 128), (128, 384))):
                        dve.scalar_tensor_tensor(out=biased[:, s, lo:hi], in0=bank[4 + s][:, lo:hi], scalar=c8[:, b, h:h + 1],
                                                 in1=foxm[:, lo:hi], op0=ALU.add, op1=ALU.add).then_inc(biased_done, 1)
                dve.wait_ge(biased_done, 2 * (i + 1))
                mx, nm = st(18 + s), st(8 + s)
                dve.tensor_reduce(mx[:, 0:1], biased[:, s, 0:128], AX, ALU.max).then_inc(row_max, 1)
                dve.tensor_reduce(mx[:, 1:2], biased[:, s, 128:384], AX, ALU.max).then_inc(row_max, 1)
                dve.wait_ge(row_max, 2 * (i + 1))
                if i < NH:
                    dve.tensor_scalar(nm, mx, sink8[:, h:h + 1], -HD ** -0.5, ALU.max, ALU.mult).then_inc(neg_max, 1)
                else:
                    dve.tensor_scalar(nm, mx, -HD ** -0.5, None, ALU.mult).then_inc(neg_max, 1)

            def recip(i):
                s = i % 2
                den, es, rd = st(10 + s), st(12 + s), st(30 + s)
                dve.wait_ge(exp_done, 3 * (i + 1))
                if i >= 2:
                    dve.wait_ge(out_done, i - 1)
                if i < NH:
                    dve.tensor_tensor(rd, den, es, ALU.add).then_inc(den_done, 1)
                    dve.wait_ge(den_done, i + 1)
                    dve.reciprocal(rd, rd).then_inc(recip_done, 1)
                else:
                    dve.reciprocal(rd, den).then_inc(recip_done, 1)

            def normalise(i):
                s = i % 2
                dve.wait_ge(pv_done, i + 1)
                dve.wait_ge(recip_done, i + 1)
                dve.tensor_tensor(work[:, :, i * HD:(i + 1) * HD], bank[7][:, 0:P].rearrange("p (b n) -> p b n", b=NB),
                                  broadcast(st(30 + s), [P, NB, HD]), ALU.mult).then_inc(out_done, 1)

            def head(i):
                if i < 2 * NH:
                    bias(i)
                if 1 <= i <= 2 * NH:
                    recip(i - 1)
                if 2 <= i < 2 * NH + 2:
                    normalise(i - 2)

            dve.wait_ge(pool_ready, 14)
            group(0)
            dve.tensor_copy(va[:, :, :].rearrange("p a b -> p (a b)"), bank[1][:, 0:S]).then_inc(banks_free, 1)
            dve.wait_ge(fr_done, 1)
            dve.tensor_tensor(fz[:, :, :], bank[7][:, 0:32].rearrange("p (b n) -> p b n", b=NB),
                              bf[:, :].unsqueeze(1).broadcast_to([P, NB, 16]), ALU.add).then_inc(f_z, 1)
            dve.wait_ge(f_z, 1)
            dve.tensor_scalar(fm[:, :, :], fz[:, :, :], 0.0, None, ALU.min).then_inc(f_min, 1)
            dve.wait_ge(f_min, 1)
            dve.wait_ge(f_ln, 1)
            dve.tensor_tensor(lf[:, :, :], fm[:, :, :], fa[:, :, :], ALU.subtract).then_inc(f_log, 1)
            for g in (1, 2):
                group(g)
                copy_out(qaT[:, 4 * (g - 1) + 2:4 * g, :].rearrange("p a b -> p (a b)"), g)
                if g == 1:
                    dve.wait_ge(f_cum, 1)
                    dve.tensor_scalar(c8[:, :, :].rearrange("p a b -> p (a b)"), bank[6][:, 0:32], HD ** 0.5, None, ALU.mult).then_inc(f_c, 1)
                    dve.tensor_scalar(cT8[:, :], bank[7][0:16, 0:S], -HD ** 0.5, None, ALU.mult).then_inc(f_c, 1)
            for g in (3, 4):
                group(g, side=lambda j, g=g: head(4 * (g - 3) + j // 2) if j % 2 else None)
                copy_out(vb[:, 1, W * (g - 3):W * (g - 2)], g)
            for n, g in enumerate((5, 6, 7, 8)):
                group(g, side=lambda j, n=n: head(8 + 4 * n + j // 2) if j % 2 else None)
                dst = (qbT, kbT)[n % 2]
                copy_out(dst[:, 4 * (n // 2) + 2:4 * (n // 2) + 4, :].rearrange("p a b -> p (a b)"), g)
            for i in range(24, 2 * NH + 2):
                head(i)
            dve.wait_ge(out_done, 2 * NH)
            rstd(2, 1, 6, D_SWA, 4)
            for b in range(NB):
                for k in range(2):
                    dve.tensor_scalar(work[:, b, 1024 * k:1024 * (k + 1)], work[:, b, 1024 * k:1024 * (k + 1)],
                                      stat[:, 4 + 2 * b + k:5 + 2 * b + k], None, ALU.mult).then_inc(scaled, 1)
            phase(1)
            with dve.Fori(0, 2) as i:
                for e in range(2):
                    g = GROUP["w_out"][e]
                    group(g, i, 16)
                    dve.tensor_copy(work[:, 1, bass.ds(i * (2 * W) + e * W, W)], out_of(g, 1)).then_inc(banks_free, 1)

            def residual(n, k, src, gain, n_sq, jk, m, nsd):
                dve.wait_ge(banks_free, m)
                square1(src[:, 1, :], st(k)[:, 1:2], nsd, jk)
                rstd(n, k, n_sq, D)
                dve.wait_ge(gain_loaded, 16 * (1 + (n > 3)))
                for b in range(NB):
                    dve.scalar_tensor_tensor(out=src[:, b, :], in0=src[:, b, :], scalar=st(k)[:, b:b + 1], in1=gain[:, :],
                                             op0=ALU.mult, op1=ALU.mult).then_inc(y_scaled, 1)
                for b in range(NB):
                    dve.wait_ge(y_scaled, 2 * (1 + (n > 3)))
                    ins = dve.tensor_tensor(x_tok[:, b, :], x_tok[:, b, :], src[:, b, :], ALU.add)
                ins.then_inc(x_added, 1)
                dve.wait_ge(x_added, 1 + (n > 3))

            residual(3, 2, work, mix_gain, 7, junk_d[:, :], evacuated(GROUP["w_out"][3]), 1)
            square1(x_tok[:, 1, :], st(3)[:, 1:2], 2, junk_d[:, :])
            rstd(4, 3, 8, D)
            scale_rows(work, x_tok, 3, 2)
            phase(2)
            with dve.Fori(0, 11) as i:
                for e in range(2):
                    ins = dve.tensor_copy(coef[:, e, :, :], conv[:, :, bass.ds(i * 4 + e * FFT, 4)])
                ins.then_inc(coef_ready, 1)
                for e in range(2):
                    g = GROUP["w_up"][e]
                    group(g, i, 16)
                    cv = (cv_gate, cv_val)[e]
                    dve.wait_ge(conv_tap2, 2 * i + e + 1)
                    dve.wait_ge(coef_ready, i + 1)
                    for ft in range(4):
                        ps = bank[2 * (g % 2) + ft // 2][:, ft % 2 * S:(ft % 2 + 1) * S]
                        ins = dve.scalar_tensor_tensor(out=cv[:, ft, 1:S], in0=ps[:, 0:S - 1], scalar=coef[:, e, 1, ft:ft + 1],
                                                       in1=cv[:, ft, 1:S], op0=ALU.mult, op1=ALU.add)
                    ins.then_inc(conv_tap1, 1)
                    dve.wait_ge(conv_tap1, 2 * i + e + 1)
                    for ft in range(4):
                        ps = bank[2 * (g % 2) + ft // 2][:, ft % 2 * S:(ft % 2 + 1) * S]
                        ins = dve.scalar_tensor_tensor(out=cv[:, ft, 2:S], in0=ps[:, 0:S - 2], scalar=coef[:, e, 0, ft:ft + 1],
                                                       in1=cv[:, ft, 2:S], op0=ALU.mult, op1=ALU.add)
                        if ft % 2:
                            ins.then_inc(banks_free, 1)
                dve.wait_ge(gelu_done, i + 1)
                dve.wait_ge(banks_free, evacuated(g) + i * 4)
                dve.tensor_tensor(cv_val[:, :, :], cv_gate[:, :, :], cv_val[:, :, :], ALU.mult).then_inc(glu_done, 1)
                dve.wait_ge(g_hi_done, i + 1)
                dve.tensor_tensor(g_lo[:, bass.ds(i * 4, 4), :], cv_val[:, :, :], g_hi[:, bass.ds(i * 4, 4), :].bitcast(F32),
                                  ALU.subtract).then_inc(g_lo_done, 1)
                dve.wait_ge(g_lo_done, i + 1)
            with dve.Fori(0, 2) as i:
                for e in range(2):
                    g = GROUP["w_down"][e]
                    group(g, i, 48)
                    dve.tensor_copy(y_tok[:, 1, bass.ds(i * (2 * W) + e * W, W)], out_of(g, 1)).then_inc(banks_free, 1)
            residual(5, 4, y_tok, ffn_gain, 9, junk2_d[:, :], evacuated(GROUP["w_down"][3]), 3)
            square1(x_tok[:, 1, :], st(5)[:, 1:2], 4, junk2_d[:, :])
            rstd(6, 5, 10, D)
            scale_rows(mix2, x_tok, 5, 4)
            dve.wait_ge(fr_split_hi, 2)
            dve.tensor_tensor(fr_lo[:, :, :], fr_raw[:, :, :], fr_hi[:, :, :].bitcast(F32), ALU.subtract).then_inc(fr_split_lo, 1)
            phase(3)

            dve.wait_ge(second_pool, 9)
            dve.tensor_tensor(xor_s[:, :], xor_s[:, :], xor_t[:, :], ALU.bitwise_xor).then_inc(second_dve, 1)
            dve.wait_ge(second_dve, 1)
            dve.tensor_copy(lev[:, :], xor_s[:, :]).then_inc(second_dve, 1)
            dve.tensor_scalar(prod[:, 0:P], tri[:, :], -1024.0, 1024.0, ALU.mult, ALU.add).then_inc(second_dve, 1)
            dve.wait_ge(second_dve, 3)
            dve.tensor_tensor(lev[:, :], lev[:, :], prod[:, 0:P], ALU.add).then_inc(second_dve, 1)
            dve.wait_ge(second_dve, 4)
            for n in range(1, 8):
                dve.tensor_scalar(levels[:, n - 1, :], lev[:, :], float(P >> n), None, ALU.is_ge).then_inc(second_dve, 1)
            dve.wait_ge(second_dve, 11)
            for n in range(1, 8):
                dve.scalar_tensor_tensor(out=levels[:, n - 1, :], in0=lev[:, :], scalar=float(2 * (P >> n)), in1=levels[:, n - 1, :],
                                         op0=ALU.is_lt, op1=ALU.mult).then_inc(second_dve, 1)
            dve.tensor_scalar(levels[:, 7, :], lev[:, :], 1.0, None, ALU.is_lt).then_inc(second_dve, 1)
            dve.wait_ge(second_dve, 19)

            g = GROUP["gla_qk"][0]
            group(g)
            copy_out(gqk[:, 1, :, :].rearrange("p a b -> p (a b)"), g)
            g = GROUP["gla_v"][0]
            group(g)
            copy_out(gvv[:, 1, :], g)

            def gate_logs():
                dve.wait_ge(ga_abs, 1)
                dve.tensor_scalar(gm[:, :, :].rearrange("p a b -> p (a b)"), bank[5][:, :], 0.0, None, ALU.min).then_inc(ga_min, 1)
                dve.wait_ge(ga_min, 1)
                dve.wait_ge(ga_ln, 1)
                dve.tensor_tensor(la[:, :, :], gm[:, :, :], la[:, :, :], ALU.subtract).then_inc(ga_log, 1)

            def level(n):
                if n < 8:
                    half = P >> n
                    bv = bT[:, :, :].rearrange("p a (m c) -> p (a m) c", c=2 * half)
                    dve.wait_ge(b_ready, 1)
                    if n >= 1:
                        dve.wait_ge(clamped, n)
                    dve.tensor_tensor(rel[:, :].rearrange("p (m c) -> p m c", c=2 * half), bv,
                                      bv[:, :, half - 1:half].broadcast_to([P, 2 * S // (2 * half), 2 * half]),
                                      ALU.subtract).then_inc(rel_ready, 1)
                    dve.wait_ge(rel_ready, n + 1)
                    if n >= 1:
                        dve.wait_ge(qk_decayed, n)
                    dve.tensor_scalar(decay[:, 0, :], rel[:, :], 0.0, None, ALU.min)
                    dve.tensor_scalar(decay[:, 1, :], rel[:, :], -1.0, 0.0, ALU.mult, ALU.min).then_inc(clamped, 1)
                if n >= 1:
                    collect(n - 1)
                if n < 8:
                    dve.wait_ge(decayed, n + 1)
                    if n == 0:
                        dve.wait_ge(banks_free, evacuated(GROUP["gla_qk"][0]))
                    dve.tensor_tensor(qkd[:, :, :, :].rearrange("p a b c -> p (a b c)"), gqk[:, :, :, :].rearrange("p a b c -> p (a b c)"),
                                      decay[:, :, :].rearrange("p a b -> p (a b)"), ALU.mult).then_inc(qk_decayed, 1)

            def collect(n):
                dve.wait_ge(level_scores, n + 1)
                def heads(ap):
                    return ap.rearrange("p (c m t) -> p c m t", c=2, m=2)

                def pairs(b):
                    return upper[:, 2 * b:2 * b + 2, 0:2 * P].rearrange("p c (m t) -> p c m t", m=2)
                if n == 0:
                    dve.tensor_copy(heads(inter[:, :]), pairs(0)).then_inc(level_added, 2)
                    return
                for b in range(NB):
                    mask = levels[:, n - 1, :].unsqueeze(1).unsqueeze(1).broadcast_to([P, 2, 2, P])
                    if n == 1:
                        dve.tensor_tensor(heads(acc[:, b, :]), pairs(b), mask, ALU.mult).then_inc(level_added, 1)
                        continue
                    k = 2 * (n - 2) + b
                    dve.wait_ge(level_added, 2 * n + b)
                    dve.tensor_tensor(heads(prod[:, :]), pairs(b), mask, ALU.mult).then_inc(level_masked, 1)
                    dve.wait_ge(level_masked, k + 1)
                    dve.tensor_tensor(acc[:, b, :], acc[:, b, :], prod[:, :], ALU.add).then_inc(level_added, 1)

            def gla_side(n):
                if n == 0:
                    gate_logs()
                elif n <= 9:
                    level(n - 1)
                elif n == 10:
                    collect(8)
                elif n == 11:
                    dve.wait_ge(gla_out, 2)
                    dve.tensor_copy(mix2[:, 1, 1024:1536], bank[7][:, :]).then_inc(gla_copied, 1)

            dsts = [(sbq, 0), (sbq, 4), (sbk, 0), (sbk, 4)]
            for n in range(6):
                g = GROUP["sb_q"][0] + n
                group(g, side=lambda j, n=n: gla_side(2 * n + j // 4) if j % 4 == 3 else None)
                if n < 4:
                    copy_out(dsts[n][0][:, dsts[n][1] + 2:dsts[n][1] + 4, :].rearrange("p a b -> p (a b)"), g)
                else:
                    copy_out(sbv[:, 1, W * (n - 4):W * (n - 3)], g)

            def stick(i):
                s, r = i % 2, (i - 1) % 2
                if i < SB_HEADS:
                    dve.wait_ge(zs_done, i + 1)
                    if i >= 2:
                        dve.wait_ge(a_done, i - 1)
                        dve.wait_ge(inc_done, i - 1)
                    for c in (0, 256):
                        ins = dve.tensor_tensor(z_m[:, s, c:c + P], z_s[:, s, c:c + P], sb_neg[:, :], ALU.add)
                    ins = dve.tensor_copy(z_m[:, s, P:256], z_s[:, s, P:256])
                    ins.then_inc(zmask_done, 1)
                    dve.tensor_scalar(z_p[:, s, :], z_s[:, s, :], 0.0, None, ALU.max).then_inc(zmax_done, 1)
                if 1 <= i <= SB_HEADS:
                    dve.wait_ge(inc_done, i)
                    dve.wait_ge(zmask_done, i)
                    dve.tensor_tensor(z_m[:, r, :], z_m[:, r, :], bank[5 + r][:, 0:384], ALU.add).then_inc(t_done, 1)
                if i < SB_HEADS:
                    dve.wait_ge(zln_done, i + 1)
                    dve.wait_ge(zmax_done, i + 1)
                    dve.tensor_tensor(z_p[:, s, :], z_p[:, s, :], z_e[:, s, :], ALU.add).then_inc(sp_done, 1)
                    dve.wait_ge(sp_done, i + 1)
                    for c in (0, 256):
                        ins = dve.tensor_tensor(z_p[:, s, c:c + P], z_p[:, s, c:c + P], sb_one[:, :], ALU.mult)
                    ins.then_inc(spm_done, 1)
                if 2 <= i < SB_HEADS + 2:
                    dve.wait_ge(so_done, i - 1)
                    dve.tensor_copy(mix2[:, :, (i - 2) * P:(i - 1) * P], bank[7][:, 0:256].rearrange("p (b n) -> p b n", b=NB)).then_inc(so_copied, 1)

            for n, name in enumerate(("gla_g", "sgu_u", "sgu_v", "sgu_g")):
                group(GROUP[name][0], side=lambda j, n=n: stick(2 * n + j // 4) if j % 4 == 3 else None)

            def sgu_norm():
                a = st(14)
                dve.wait_ge(sgu_sq, 2)
                dve.tensor_scalar(a, a, 1.0 / 512, EPS, ALU.mult, ALU.add).then_inc(sgu_mean, 1)
                dve.wait_ge(sgu_root, 1)
                dve.reciprocal(a, a).then_inc(sgu_rstd, 1)
                dve.wait_ge(sgu_rstd, 1)
                dve.wait_ge(second_loaded, 64)
                for b in range(NB):
                    dve.scalar_tensor_tensor(out=sgu_v[:, b, :], in0=sgu_v[:, b, :], scalar=a[:, b:b + 1], in1=sgu_gain[:, :],
                                             op0=ALU.mult, op1=ALU.mult).then_inc(sgu_vn, 1)

            def sgu_weights():
                dve.wait_ge(sguT_done, 1)
                dve.tensor_tensor(w_sguT[:, :, :], bank[6][:, :].rearrange("p (g t) -> p g t", t=P),
                                  tri[:, :].unsqueeze(1).broadcast_to([P, SGU_GROUPS, P]), ALU.mult).then_inc(sguT_ready, 1)

            def sgu_result():
                dve.wait_ge(sgu_mixed, 2)
                for b in range(NB):
                    for k in range(SGU_GROUPS):
                        dve.scalar_tensor_tensor(out=mix2[:, b, 1536 + k * P:1536 + (k + 1) * P], in0=bank[4 + b][:, k * P:(k + 1) * P],
                                                 scalar=gains[:, BSGU_AT + k:BSGU_AT + k + 1], in1=sgu_u[:, b, k * P:(k + 1) * P],
                                                 op0=ALU.add, op1=ALU.mult).then_inc(sgu_done, 1)

            def tail(j, n):
                if n == 0 and j == 1:
                    stick(8)
                if n == 0 and j == 3:
                    stick(9)
                    sgu_weights()
                if n == 0 and j == 5:
                    sgu_norm()
                if n == 1 and j == 1:
                    sgu_result()
                if n == 1 and j == 4:
                    head_squares(0)
                if n == 1 and j == 6:
                    head_squares(1)

            def head_squares(b):
                dve.wait_ge(so_copied, SB_HEADS)
                dve.wait_ge(gla_copied, 2)
                dve.wait_ge(sgu_done, 8)
                if b:
                    dve.wait_ge(hsum_done, 1)
                sq = sbv[:, :, :].rearrange("p a b -> p (a b)")
                dve.tensor_tensor(sq, mix2[:, b, :], mix2[:, b, :], ALU.mult).then_inc(hsq_done, 1)
                dve.wait_ge(hsq_done, b + 1)
                dve.tensor_reduce(stat[:, 128 + 16 * b:144 + 16 * b], sq.rearrange("p (h n) -> p h n", n=P), AX, ALU.add).then_inc(hsum_done, 1)

            for n in range(2):
                group(GROUP["sb_g"][n], side=lambda j, n=n: tail(j, n))
            rstd(7, 6, 12, D)
            scale_rows(mem_tok, mem_tok, 6, 6)
            phase(4)
            hs = stat[:, 128:160]
            dve.wait_ge(hsum_done, 2)
            dve.tensor_scalar(hs, hs, 1.0 / P, EPS, ALU.mult, ALU.add).then_inc(hmean, 1)

            def gated(j):
                if j == 1:
                    dve.wait_ge(hroot, 1)
                    dve.reciprocal(hs, hs).then_inc(hrstd, 1)
                    dve.wait_ge(hrstd, 1)
                if j in (2, 4):
                    b = j // 2 - 1
                    m = mix2[:, b, :].rearrange("p (h n) -> p h n", n=P)
                    dve.tensor_tensor(m, m, stat[:, 128 + 16 * b:144 + 16 * b].unsqueeze(2).broadcast_to([P, 16, P]), ALU.mult).then_inc(hscaled, 1)
                if j in (3, 5):
                    b = j // 2 - 1
                    dve.wait_ge(hscaled, b + 1)
                    dve.wait_ge(banks_free, evacuated(GROUP["sb_g"][1]))
                    dve.tensor_tensor(mix2[:, b, :], mix2[:, b, :], gate[:, b, :], ALU.mult).then_inc(scaled, 1)

            g = GROUP["xk"][0]
            group(g, side=gated)
            copy_out(xkT[:, 2:4, :].rearrange("p a b -> p (a b)"), g)
            g = GROUP["xv"][0]
            group(g)
            copy_out(xv[:, 1, :], g)
            phase(5)

            def onto_x(g, i, step, col):
                for b in range(NB):
                    dst = x_tok[:, b, bass.ds(col, W)] if i is not None else x_tok[:, b, col:col + W]
                    dve.tensor_tensor(dst, out_of(g, b), dst, ALU.add).then_inc(banks_free, 1)

            with dve.Fori(0, 2) as i:
                for e in range(2):
                    g = GROUP["w_out2"][e]
                    group(g, i, 16)
                    onto_x(g, i, 16, i * (2 * W) + e * W)
            dve.wait_ge(banks_free, evacuated(GROUP["w_out2"][3]))
            square1(x_tok[:, 1, :], st(7)[:, 1:2], 5, junk2_d[:, :])
            rstd(8, 7, 13, D)
            scale_rows(mem_tok, x_tok, 7, 10)
            phase(6)
            g = GROUP["xq"][0]
            group(g)
            copy_out(mix2[:, 1, 0:W], g)
            for h in range(XA_HEADS):
                dve.wait_ge(xs_done, h + 1)
                dve.tensor_reduce(st(20 + h), bank[4 + h][:, :].rearrange("p (b k) -> p b k", b=NB), AX, ALU.max).then_inc(xmax_done, 1)
                dve.wait_ge(xmax_done, h + 1)
                dve.tensor_scalar(st(20 + h), st(20 + h), -WIDE_SCALE, None, ALU.mult).then_inc(xneg_done, 1)
            for h in range(XA_HEADS):
                dve.wait_ge(xexp_done, 2 * (h + 1))
                dve.reciprocal(st(24 + h), st(24 + h)).then_inc(xrecip_done, 1)
                dve.wait_ge(xrecip_done, h + 1)
                pv = x_p[:, h, :].rearrange("p (b k) -> p b k", b=NB)
                dve.tensor_tensor(pv, pv, broadcast(st(24 + h), [P, NB, S]), ALU.mult).then_inc(xnorm_done, 1)
            for h in range(XA_HEADS):
                dve.wait_ge(xo_hi, h + 1)
                dve.tensor_tensor(hT_lo[:, h, :], bank[4 + h][:, 0:S], hT_hi[:, h, :].bitcast(F32), ALU.subtract).then_inc(xo_lo, 1)
            for e in range(4):
                g = GROUP["xo"][e]
                group(g)
                onto_x(g, None, 0, e * W)
            dve.wait_ge(banks_free, evacuated(GROUP["xo"][3]))
            square1(x_tok[:, 1, :], st(16)[:, 1:2], 6, junk2_d[:, :])
            rstd(9, 16, 14, D)
            dve.wait_ge(gain_loaded, 48)
            for b in range(NB):
                dve.scalar_tensor_tensor(out=x_tok[:, b, :], in0=x_tok[:, b, :], scalar=st(16)[:, b:b + 1], in1=out_gain[:, :],
                                         op0=ALU.mult, op1=ALU.mult).then_inc(out_scaled, 1)

        @block.tensor
        def _(pe):
            def three(o, l_hi, l_lo, r_hi, r_lo, start, stop):
                pe.matmul(o, l_hi, r_hi, start=start, stop=False, skip_group_check=True)
                pe.matmul(o, l_hi, r_lo, start=False, stop=False, skip_group_check=True)
                return pe.matmul(o, l_lo, r_hi, start=False, stop=stop, skip_group_check=True)

            def group(g, mode, i=None, step=0, kcs=(2,) * 8, a_hi=hT_hi, a_lo=hT_lo, first=None, side=None):
                u = FIRST_PIECE[g]
                pair = 2 * (g % 2)
                if g >= 2:
                    pe.wait_ge(banks_free, 2 * (g - 1) + (0 if i is None else i * (4 if step else 0)))
                k = 0
                total = sum(kcs)
                for j, n in enumerate(kcs):
                    s = (u + j) % SLOTS
                    pe.wait_ge(lo_ready, u + j + 1 + (0 if i is None else i * step))
                    hi, lo = wide(w_hi, s, n, W), wide(w_lo, s, n, W)
                    for c in range(n):
                        if first is not None:
                            pe.wait_ge(loT_done, first * KC + k + 1)
                        if mode == "tok":
                            for b in range(NB):
                                ins = three(bank[pair + b][:, :], a_hi[:, k, b * P:(b + 1) * P], a_lo[:, k, b * P:(b + 1) * P],
                                            hi[:, c, :], lo[:, c, :], k == 0, k == total - 1)
                        else:
                            for ft in range(4):
                                o = bank[pair + ft // 2][:, ft % 2 * S:(ft % 2 + 1) * S]
                                ins = three(o, hi[:, c, ft * P:(ft + 1) * P], lo[:, c, ft * P:(ft + 1) * P],
                                            a_hi[:, k, :], a_lo[:, k, :], k == 0 and ft % 2 == 0, k == total - 1)
                        k += 1
                    ins.then_inc(mm_done, 1)
                    if side:
                        side(j)

            def phase(n, src, ready):
                pe.wait_ge(scaled, ready)
                for q in range(KC // 2):
                    t = KC // 2 * n + q
                    if t >= 4:
                        pe.wait_ge(loT_done, 2 * (t - 3))
                    for c in (2 * q, 2 * q + 1):
                        for b in range(NB):
                            ins = pe.transpose(bank[4 + q % 4][:, c % 2 * S + b * P:c % 2 * S + (b + 1) * P],
                                               src[:, b, c * P:(c + 1) * P], ident[:, :])
                    ins.then_inc(tr_done, 1)

            pe.wait_ge(pool_ready, 14)
            pe.wait_ge(rows_loaded, 16 * 11)
            pe.transpose(bank[6][:, 0:GAIN_ROWS], gain_rows[:, :], ident[0:GAIN_ROWS, 0:GAIN_ROWS])
            for c in range(4):
                ins = pe.transpose(bank[7][:, c * 2 * FFT:(c + 1) * 2 * FFT], conv_rows[:, c, :], ident[0:2 * FFT, 0:2 * FFT])
            ins.then_inc(rows_T, 1)
            pe.wait_ge(tables_ready, 1)
            phase(0, work, 2)

            for j in range(4):
                pe.wait_ge(lo_ready, j + 1)
                hi, lo = wide(w_hi, j, 4, 256), wide(w_lo, j, 4, 256)
                for c in range(4):
                    k = 4 * j + c
                    pe.wait_ge(loT_done, k + 1)
                    three(bank[0][:, 0:S], hi[:, c, 0:P], lo[:, c, 0:P], hT_hi[:, k, :], hT_lo[:, k, :], k == 0, k == KC - 1)
                    for b in range(NB):
                        ins = three(bank[1][:, b * P:(b + 1) * P], hT_hi[:, k, b * P:(b + 1) * P], hT_lo[:, k, b * P:(b + 1) * P],
                                    hi[:, c, P:256], lo[:, c, P:256], k == 0 and b == 0, k == KC - 1)
                ins.then_inc(mm_done, 1)
            pe.wait_ge(fr_split_lo, 1)
            for k in range(KC):
                for b in range(NB):
                    ins = three(bank[7][:, b * 16:(b + 1) * 16], hT_hi[:, k, b * P:(b + 1) * P], hT_lo[:, k, b * P:(b + 1) * P],
                                fr_hi[:, k, :], fr_lo[:, k, :], k == 0 and b == 0, k == KC - 1)
            ins.then_inc(fr_done, 1)
            pe.wait_ge(dve_ready, 2)

            def forget_sums():
                pe.wait_ge(f_log, 1)
                pe.matmul(bank[6][:, 0:16], tri[:, :], lf[:, 0, :], start=True, stop=True)
                pe.matmul(bank[6][:, 16:32], ones[:, :], lf[:, 0, :], start=True, stop=False)
                pe.matmul(bank[6][:, 16:32], tri[:, :], lf[:, 1, :], start=False, stop=True)
                pe.matmul(bank[7][0:16, 0:128], lf[:, 0, :], tri[:, :], start=True, stop=True)
                pe.matmul(bank[7][0:16, 128:256], lf[:, 0, :], ones[:, :], start=True, stop=False)
                pe.matmul(bank[7][0:16, 128:256], lf[:, 1, :], tri[:, :], start=False, stop=True).then_inc(f_cum, 1)

            def scores(i):
                s, h = i % 2, i % NH
                po = h % 2 * HD
                if i >= 2:
                    pe.wait_ge(biased_done, 2 * (i - 1))
                if i == 0:
                    pe.wait_ge(k_copied, 64)
                    pe.wait_ge(banks_free, evacuated(2))
                if i == NH:
                    pe.wait_ge(f_c, 2)
                    pe.wait_ge(banks_free, evacuated(6))
                if i == NH + 8:
                    pe.wait_ge(banks_free, evacuated(8))
                o = bank[4 + s]
                for b, (lo, hi) in enumerate(((0, 128), (128, 384))):
                    n = hi - lo
                    if i < NH:
                        ins = pe.matmul(o[:, lo:hi], qaT[po:po + HD, h // 2, b * P:(b + 1) * P], ka2[po:po + HD, h // 8, 0:n],
                                        start=True, stop=True)
                    else:
                        pe.matmul(o[:, lo:hi], qbT[po:po + HD, h // 2, b * P:(b + 1) * P], kbT[po:po + HD, h // 2, 0:n],
                                  start=True, stop=False)
                        ins = pe.matmul(o[:, lo:hi], sel[:, h, :], cT8[:, 0:n], start=False, stop=True)
                ins.then_inc(scores_done, 1)

            def turn(i):
                s = i % 2
                pe.wait_ge(exp_done, 3 * (i + 1))
                if i >= 1:
                    pe.wait_ge(probsT_copied, i)
                if i == 0:
                    pe.wait_ge(f_c, 2)
                for c in range(3):
                    ins = pe.transpose(bank[6][:, c * P:(c + 1) * P], probs[:, s, c * P:(c + 1) * P], ident[:, :])
                ins.then_inc(probs_T, 1)

            def values(i):
                s, h = i % 2, i % NH
                pe.wait_ge(probsT_copied, i + 1)
                if i >= 1:
                    pe.wait_ge(out_done, i)

                def v(b):
                    return va[:, b, h // 8 * HD:(h // 8 + 1) * HD] if i < NH else vb[:, b, h * HD:(h + 1) * HD]
                o = bank[7]
                pe.matmul(o[:, 0:HD], probsT[:, s, 0:128], v(0), start=True, stop=True)
                pe.matmul(o[:, HD:P], probsT[:, s, 128:256], v(0), start=True, stop=False)
                pe.matmul(o[:, HD:P], probsT[:, s, 256:384], v(1), start=False, stop=True).then_inc(pv_done, 1)

            def head(i):
                if i < 2 * NH:
                    scores(i)
                if 1 <= i <= 2 * NH:
                    turn(i - 1)
                if 2 <= i < 2 * NH + 2:
                    values(i - 2)

            group(1, "T")
            forget_sums()
            group(2, "T")
            for g in (3, 4):
                group(g, "tok", side=lambda j, g=g: head(4 * (g - 3) + j // 2) if j % 2 else None)
            for n, g in enumerate((5, 6, 7, 8)):
                group(g, "T", side=lambda j, n=n: head(8 + 4 * n + j // 2) if j % 2 else None)
            for i in range(24, 2 * NH + 2):
                head(i)
            phase(1, work, 2 + 4)
            with pe.Fori(0, 2) as i:
                for e in range(2):
                    if e == 0:
                        pe.wait_ge(loT_done, 2 * KC)
                    group(GROUP["w_out"][e], "tok", i, 16)
            phase(2, work, 8)
            with pe.Fori(0, 11) as i:
                for e in range(2):
                    if e == 0:
                        pe.wait_ge(loT_done, 3 * KC)
                    group(GROUP["w_up"][e], "T", i, 16)
            with pe.Fori(0, 2) as i:
                for e in range(2):
                    if e == 0:
                        pe.wait_ge(g_lo_done, 11)
                    group(GROUP["w_down"][e], "tok", i, 48, kcs=DOWN, a_hi=g_hi, a_lo=g_lo)
            phase(3, mix2, 10)

            pe.wait_ge(fr_split_lo, 2)
            group(GROUP["gla_qk"][0], "T", first=3)
            for k in range(KC):
                ins = three(bank[4][0:16, 0:S], fr_hi[:, k, :], fr_lo[:, k, :], hT_hi[:, k, :], hT_lo[:, k, :], k == 0, k == KC - 1)
            ins.then_inc(fr_done, 1)

            def gate_mm(j):
                if j == 3:
                    pe.wait_ge(r_copied, 1)
                    pe.wait_ge(second_loaded, 64)
                    for b in range(NB):
                        pe.matmul(bank[5][:, b * S:(b + 1) * S], rT[:, b * P:(b + 1) * P], wgu[:, :], start=True, stop=False)
                        ins = pe.matmul(bank[5][:, b * S:(b + 1) * S], ones[0:1, :], bgg[:, :], start=False, stop=True)
                    ins.then_inc(gate_logits, 1)

            group(GROUP["gla_v"][0], "tok", side=gate_mm)

            def gate_sums():
                pe.wait_ge(ga_log, 1)
                for t in range(2):
                    o = bank[6][:, t * S:(t + 1) * S]
                    pe.matmul(o[:, 0:P], la[:, 0, t * P:(t + 1) * P], tri[:, :], start=True, stop=True)
                    pe.matmul(o[:, P:S], la[:, 0, t * P:(t + 1) * P], ones[:, :], start=True, stop=False)
                    ins = pe.matmul(o[:, P:S], la[:, 1, t * P:(t + 1) * P], tri[:, :], start=False, stop=True)
                ins.then_inc(cum_done, 1)

            def level(n):
                if n < 8:
                    pe.wait_ge(qk_decayed, n + 1)
                    src = qkd
                else:
                    src = gqk
                if n >= 1:
                    pe.wait_ge(level_added, 2 * n)
                for b in range(NB if n else 1):
                    for h in range(GLA_HEADS):
                        po, t = h % 2 * HD, h // 2
                        qb = b if n else 1
                        ins = pe.matmul(bank[4 + 2 * b + h % 2][:, t * P:(t + 1) * P], src[po:po + HD, 1, t, b * P:(b + 1) * P],
                                        src[po:po + HD, 0, t, qb * P:(qb + 1) * P], start=True, stop=True)
                ins.then_inc(level_scores, 1)

            def gla_values():
                pe.wait_ge(level_added, 18)
                pe.wait_ge(b_ready, 1)
                for h in range(GLA_HEADS):
                    c = slice(h * P, (h + 1) * P)
                    a = slice((h % 2 * 2 + h // 2) * P, (h % 2 * 2 + h // 2 + 1) * P)
                    pe.matmul(bank[6][:, c], acc[:, 0, a], gvv[:, 0, c], start=True, stop=True)
                    pe.matmul(bank[7][:, c], inter[:, a], gvv[:, 0, c], start=True, stop=False)
                    ins = pe.matmul(bank[7][:, c], acc[:, 1, a], gvv[:, 1, c], start=False, stop=True)
                ins.then_inc(gla_out, 2)

            def gla_side(n):
                if n == 0:
                    gate_sums()
                elif n <= 9:
                    level(n - 1)
                elif n == 10:
                    gla_values()

            for n in range(6):
                group(GROUP["sb_q"][0] + n, "T" if n < 4 else "tok",
                      side=lambda j, n=n: gla_side(2 * n + j // 4) if j % 4 == 3 else None)

            def stick(i):
                if i < SB_HEADS:
                    if i == 0:
                        pe.wait_ge(gla_copied, 2)
                        pe.wait_ge(banks_free, evacuated(GROUP["sb_k"][1]))
                    if i >= 1:
                        pe.wait_ge(zs_done, i)
                    pe.matmul(bank[4][:, 0:256], sbk[:, i, 0:P], sbq[:, i, :], start=True, stop=True)
                    pe.matmul(bank[4][:, 256:384], sbk[:, i, P:S], sbq[:, i, P:S], start=True, stop=True).then_inc(z_done, 1)
                if 1 <= i <= SB_HEADS:
                    k = i - 1
                    r = k % 2
                    pe.wait_ge(spm_done, i)
                    if k >= 2:
                        pe.wait_ge(t_done, k - 1)
                    pe.matmul(bank[5 + r][:, 0:384], tri_neg[:, :], z_p[:, r, :], start=True, stop=False, skip_group_check=True)
                    pe.matmul(bank[5 + r][:, P:256], ones_neg[:, :], z_p[:, r, 256:384], start=False, stop=True,
                              skip_group_check=True).then_inc(inc_done, 1)
                if 2 <= i < SB_HEADS + 2:
                    k = i - 2
                    r = k % 2
                    pe.wait_ge(a_done, k + 1)
                    if k >= 1:
                        pe.wait_ge(so_copied, k)
                    if k == 0:
                        pe.wait_ge(banks_free, evacuated(GROUP["sb_v"][1]))
                    c = slice(k * P, (k + 1) * P)
                    pe.matmul(bank[7][:, 0:P], z_a[:, r, 0:P], sbv[:, 0, c], start=True, stop=True)
                    pe.matmul(bank[7][:, P:256], z_a[:, r, P:256], sbv[:, 0, c], start=True, stop=False)
                    pe.matmul(bank[7][:, P:256], z_a[:, r, 256:384], sbv[:, 1, c], start=False, stop=True).then_inc(so_done, 1)

            for n, name in enumerate(("gla_g", "sgu_u", "sgu_v", "sgu_g")):
                group(GROUP[name][0], "tok", side=lambda j, n=n: stick(2 * n + j // 4) if j % 4 == 3 else None)

            def tail(j, n):
                if n == 0 and j == 1:
                    stick(8)
                if n == 0 and j == 3:
                    stick(9)
                    pe.wait_ge(t_done, SB_HEADS)
                    for k in range(SGU_GROUPS):
                        ins = pe.transpose(bank[6][:, k * P:(k + 1) * P], w_sgu[:, k, :], ident[:, :])
                    ins.then_inc(sguT_done, 1)
                if n == 1 and j == 0:
                    pe.wait_ge(sguT_ready, 1)
                    pe.wait_ge(sgu_vn, 2)
                    for b in range(NB):
                        for k in range(SGU_GROUPS):
                            ins = pe.matmul(bank[4 + b][:, k * P:(k + 1) * P], w_sguT[:, k, :], sgu_v[:, b, k * P:(k + 1) * P],
                                            start=True, stop=True)
                    ins.then_inc(sgu_mixed, 2)

            for n in range(2):
                group(GROUP["sb_g"][n], "tok", side=lambda j, n=n: tail(j, n))
            pe.wait_ge(sgu_done, 8)
            phase(4, mem_tok, 12)
            group(GROUP["xk"][0], "T", first=4)
            group(GROUP["xv"][0], "tok")
            phase(5, mix2, 14)
            with pe.Fori(0, 2) as i:
                for e in range(2):
                    if e == 0:
                        pe.wait_ge(loT_done, 6 * KC)
                    group(GROUP["w_out2"][e], "tok", i, 16)
            phase(6, mem_tok, 16)
            group(GROUP["xq"][0], "T", first=6)
            pe.wait_ge(banks_free, evacuated(GROUP["xq"][0]))
            for h in range(XA_HEADS):
                for b in range(NB):
                    ins = pe.matmul(bank[4 + h][:, b * S:(b + 1) * S], mix2[:, h // 2, h % 2 * S + b * P:h % 2 * S + (b + 1) * P],
                                    xkT[:, h, :], start=True, stop=True)
                ins.then_inc(xs_done, 1)
            for h in range(XA_HEADS):
                pe.wait_ge(xnorm_done, h + 1)
                for k in range(2):
                    for b in range(NB):
                        ins = pe.transpose(bank[4 + h][:, k * S + b * P:k * S + (b + 1) * P], x_p[:, h, b * S + k * P:b * S + (k + 1) * P], ident[:, :])
                ins.then_inc(xpT_done, 1)
            for h in range(XA_HEADS):
                pe.wait_ge(xpT_copied, h + 1)
                for k in range(2):
                    ins = pe.matmul(bank[4 + h][:, 0:S], xv[:, k, h * P:(h + 1) * P], x_pT[:, h % 2, k * S:(k + 1) * S],
                                    start=(k == 0), stop=(k == 1))
                ins.then_inc(xo_done, 1)
            pe.wait_ge(xo_lo, XA_HEADS)
            for e in range(4):
                group(GROUP["xo"][e], "tok", kcs=(2, 2))


_INS = ['x', 'pre_mix_g', 'w_in', 'b_forget', 'sinks', 'grp_swa_g', 'grp_fox_g', 'w_out', 'post_mix_g', 'pre_ffn_g',
        'w_up', 'conv_w', 'conv_b', 'w_down', 'post_ffn_g', 'mem_2', 'norm_mix_2', 'w_in_2', 'w_gla_gate_up_2',
        'b_gla_gate_2', 'sgu_norm_2', 'w_sgu_2', 'b_sgu_2', 'out_norm_2', 'w_out_2', 'norm_xattn_2', 'norm_mem_2',
        'w_xq_2', 'w_xkv_2', 'w_xo_2', 'final_norm_2']


def kernel(**inputs):
    import numpy as np
    import concourse.bacc as bacc
    from concourse.bass_utils import run_bass_kernel_spmd

    nc = bacc.Bacc("TRN2", target_bir_lowering=False, num_devices=1)
    arrays, aps = {}, {}
    for name in _INS:
        a = np.ascontiguousarray(inputs[name])
        arrays[f"in_{name}"] = a
        aps[name] = nc.dram_tensor(f"in_{name}", a.shape, mybir.dt.from_np(a.dtype), kind="ExternalInput").ap()
    out = nc.dram_tensor("out_0", (1, S, D), F32, kind="ExternalOutput").ap()
    build(nc, aps, out)
    r = run_bass_kernel_spmd(nc, [arrays], core_ids=[0])
    return r.results[0]["out_0"]
```

```python
from contextlib import ExitStack

import concourse.bass as bass
from concourse import mybir

F32 = mybir.dt.float32
F32R = mybir.dt.float32r
BF16 = mybir.dt.bfloat16
I32 = mybir.dt.int32
ALU = mybir.AluOpType
ACT = mybir.ActivationFunctionType
AX = mybir.AxisListType.X

P = 128
S = 256
NB = S // P
D = 2048
KC = D // P
EPS = 1e-6
BIG = 1e30

HD = 64
NH = 16
D_SWA = NH * HD
WINDOW = 128
D_FF = 5632
FFT = D_FF // P
QA, KA, VA, QB, KB, VB, FB = 0, 1024, 1152, 1280, 2304, 3328, 4352
SBQ, SBK, SBV, SBG = 0, 1024, 2048, 3072
GLQ, GLV, GLR, GLG = 4096, 4608, 5120, 5136
SGUU, SGUV, SGUG = 5648, 6160, 6672
SB_HEADS = 8
GLA_HEADS = 4
GATE_RANK = 16
GATE_TAU = 16.0
SGU_GROUPS = 4
XA_HEADS = 4
WIDE_SCALE = 128 ** -0.5

W = 512
PIECE = 1024
SLOTS = 4

PLAN = (
    [("kv_a", 4), ("q_a", 8), ("q_a", 8), ("v_b", 8), ("v_b", 8), ("q_b", 8), ("k_b", 8), ("q_b", 8), ("k_b", 8)]
    + [("w_out", 8)] * 4 + [("w_up", 8)] * 22 + [("w_down", 24)] * 4
    + [("gla_qk", 8), ("gla_v", 8)] + [("sb_q", 8)] * 2 + [("sb_k", 8)] * 2 + [("sb_v", 8)] * 2
    + [("gla_g", 8), ("sgu_u", 8), ("sgu_v", 8), ("sgu_g", 8)] + [("sb_g", 8)] * 2
    + [("xk", 8), ("xv", 8)] + [("w_out2", 8)] * 4 + [("xq", 8)] + [("xo", 2)] * 4
)
FIRST_PIECE = [sum(n for _, n in PLAN[:g]) for g in range(len(PLAN) + 1)]
GROUP = {}
for _g, (_name, _n) in enumerate(PLAN):
    GROUP.setdefault(_name, []).append(_g)
TOTAL = FIRST_PIECE[-1]
DOWN = [2] * 20 + [1] * 4

GAINS = ["pre_mix", "grp", "pre_ffn", "norm_mix_2", "out_norm_2", "norm_mem_2", "norm_xattn_2"]
GAIN_AT = {n: i * KC for i, n in enumerate(GAINS)}
BSGU_AT = KC * len(GAINS)
GAIN_ROWS = BSGU_AT + SGU_GROUPS
PHASES = ["pre_mix", "grp", "pre_ffn", "norm_mix_2", "norm_mem_2", "out_norm_2", "norm_xattn_2"]
READER = [GROUP[n][0] for n in ("kv_a", "w_out", "w_up", "gla_qk", "xk", "w_out2", "xq")]


def pair_bank(n, q):
    p = 2 * (READER[n] % 2)
    return [p, p + 1, 4, 5, 6, 7, 2 - p, 3 - p][q]


def build(nc, A, out):
    with ExitStack() as ctx:
        def sem(name):
            return ctx.enter_context(nc.semaphore(name))

        def region(specs):
            with ExitStack() as scope:
                return [scope.enter_context(nc.sbuf_tensor(n, shape, dt)) for n, shape, dt in specs]

        def keep(name, shape, dt=F32):
            return ctx.enter_context(nc.sbuf_tensor(name, shape, dt))

        x_tok = keep("x_tok", [P, NB, D])
        raw = keep("raw", [P, SLOTS, PIECE])
        w_hi = keep("w_hi", [P, SLOTS, PIECE], F32R)
        w_lo = keep("w_lo", [P, SLOTS, PIECE], F32R)
        ident = keep("ident", [P, P])
        tri = keep("tri", [P, P])
        ones = keep("ones", [P, P])
        gains = keep("gains", [P, GAIN_ROWS])
        conv = keep("conv", [P, 4, 2 * FFT])
        fr_raw = keep("fr_raw", [P, KC, 16])
        fr_hi = keep("fr_hi", [P, KC, 16], F32R)
        fr_lo = keep("fr_lo", [P, KC, 16], F32R)
        stat = keep("stat", [P, 4 * 64])

        part_sq = keep("part_sq", [P, NB, 8])

        hT_hi, hT_lo = region([("hT_hi", [P, KC, S], F32R), ("hT_lo", [P, KC, S], F32R)])
        y_tok, ffn_gain = region([("y_tok", [P, NB, D], F32), ("ffn_gain", [P, D], F32)])
        hold = ctx.enter_context(nc.sbuf_tensor("h_place", [P, 2 * KC * S], F32))

        (work, mix_gain, qaT, kaT, ka2, va, qbT, kbT, vb, sel, distm, foxm, probs, probsT, biased, sink, sink8,
         bf, fz, fm, fa, lf, c8, cT8, gain_rows, conv_rows, junk, junk_d) = region([
             ("work", [P, NB, D], F32), ("mix_gain", [P, D], F32), ("qaT", [P, 8, S], F32), ("kaT", [P, S], F32),
             ("ka2", [P, 2, S], F32), ("va", [P, NB, P], F32), ("qbT", [P, 8, S], F32), ("kbT", [P, 8, S], F32),
             ("vb", [P, NB, 1024], F32), ("sel", [16, NH, P], F32), ("distm", [P, 384], F32), ("foxm", [P, 384], F32),
             ("probs", [P, 2, 384], F32), ("probsT", [P, 2, 384], F32), ("biased", [P, 2, 384], F32),
             ("sink", [P, NH], F32), ("sink8", [P, NH], F32), ("bf", [P, 16], F32), ("fz", [P, NB, 16], F32),
             ("fm", [P, NB, 16], F32), ("fa", [P, NB, 16], F32), ("lf", [P, NB, 16], F32), ("c8", [P, NB, 16], F32),
             ("cT8", [16, S], F32), ("gain_rows", [GAIN_ROWS, P], F32), ("conv_rows", [2 * FFT, 4, P], F32),
             ("junk", [P, 2048], BF16), ("junk_d", [P, 2048], BF16)])
        g_hi, g_lo, cv_gate, cv_val, coef = region([
            ("g_hi", [P, FFT, S], F32R), ("g_lo", [P, FFT, S], F32R), ("cv_gate", [P, 4, S], F32),
            ("cv_val", [P, 4, S], F32), ("coef", [P, 2, 4, 4], F32)])
        with ExitStack() as scope:
            def loc(name, shape, dt=F32):
                return scope.enter_context(nc.sbuf_tensor(name, shape, dt))
            mix2 = loc("mix2", [P, NB, D])
            with ExitStack() as inner:
                def part(name, shape, dt=F32):
                    return inner.enter_context(nc.sbuf_tensor(name, shape, dt))
                gqk = part("gqk", [P, 2, 2, S])
                gvv = part("gvv", [P, NB, 512])
                la = part("la", [P, NB, S])
                bT = part("bT", [P, 2, S])
            with ExitStack() as inner:
                x_p = inner.enter_context(nc.sbuf_tensor("x_p", [P, XA_HEADS, 512], F32))
                x_pT = inner.enter_context(nc.sbuf_tensor("x_pT", [P, 2, 512], F32))
            gate = loc("gate", [P, NB, D])
            with ExitStack() as inner:
                sbq = inner.enter_context(nc.sbuf_tensor("sbq", [P, 8, S], F32))
                sbk = inner.enter_context(nc.sbuf_tensor("sbk", [P, 8, S], F32))
            mem_tok = loc("mem_tok", [P, NB, D])
            sbv = loc("sbv", [P, NB, 1024])
            xkT = loc("xkT", [P, XA_HEADS, S])
            xv = loc("xv", [P, NB, 512])
            with ExitStack() as inner:
                xor_s = inner.enter_context(nc.sbuf_tensor("xor_s", [P, P], I32))
                xor_t = inner.enter_context(nc.sbuf_tensor("xor_t", [P, P], I32))
                lev = inner.enter_context(nc.sbuf_tensor("lev", [P, P], F32))
            sgu_u = loc("sgu_u", [P, NB, 512])
            sgu_v = loc("sgu_v", [P, NB, 512])
            sgu_gain = loc("sgu_gain", [P, 512])
            w_sgu = loc("w_sgu", [P, SGU_GROUPS, P])
            w_sguT = loc("w_sguT", [P, SGU_GROUPS, P])
            sb_neg = loc("sb_neg", [P, P])
            sb_one = loc("sb_one", [P, P])
            tri_neg = loc("tri_neg", [P, P])
            ones_neg = loc("ones_neg", [P, P])
            with ExitStack() as inner:
                def part(name, shape, dt=F32):
                    return inner.enter_context(nc.sbuf_tensor(name, shape, dt))
                rT = part("rT", [16, S])
                wgu = part("wgu", [16, S])
                bgg = part("bgg", [1, S])
                decay = part("decay", [P, 2, 2 * S])
                qkd = part("qkd", [P, 2, 2, S])
                acc = part("acc", [P, NB, 512])
                inter = part("inter", [P, 512])
                prod = part("prod", [P, 512])
                levels = part("levels", [P, 8, P])
            with ExitStack() as inner:
                def part(name, shape, dt=F32):
                    return inner.enter_context(nc.sbuf_tensor(name, shape, dt))
                z_s = part("z_s", [P, 2, 384])
                z_m = part("z_m", [P, 2, 384])
                z_e = part("z_e", [P, 2, 384])
                z_p = part("z_p", [P, 2, 384])
                z_a = part("z_a", [P, 2, 384])
            with ExitStack() as inner:
                def part(name, shape, dt=F32):
                    return inner.enter_context(nc.sbuf_tensor(name, shape, dt))
                out_gain = part("out_gain", [P, D])
                junk2 = part("junk2", [P, 2048], BF16)
                junk2_d = part("junk2_d", [P, 2048], BF16)

        bank = [ctx.enter_context(nc.psum_tensor(f"bank{i}", [P, 512], F32)) for i in range(4)]
        upper = ctx.enter_context(nc.psum_tensor("upper", [P, 4, 512], F32))
        bank += [upper[:, i, :] for i in range(4)]

        raw_loaded = [sem(f"raw_loaded{i}") for i in range(SLOTS)]
        hi_ready, lo_ready, mm_done = sem("hi_ready"), sem("lo_ready"), sem("mm_done")
        banks_free = sem("banks_free")
        x_loaded = [sem("x_loaded0"), sem("x_loaded1")]
        rows_loaded, consts_loaded = sem("rows_loaded"), sem("consts_loaded")
        conv_loaded, conv_T, conv_ready = sem("conv_loaded"), sem("conv_T"), sem("conv_ready")
        fr_loaded, fr_split_hi, fr_split_lo, fr_done = sem("fr_loaded"), sem("fr_split_hi"), sem("fr_split_lo"), sem("fr_done")
        ident_ready, pool_ready, dve_ready = sem("ident_ready"), sem("pool_ready"), sem("dve_ready")
        rows_T, tables_ready = sem("rows_T"), sem("tables_ready")
        squares, mean_ready, root_ready, rstd_ready, scaled = (
            sem("squares"), sem("mean_ready"), sem("root_ready"), sem("rstd_ready"), sem("scaled"))
        squares_d = sem("squares_d")
        tr_done, hiT_done, loT_done = sem("tr_done"), sem("hiT_done"), sem("loT_done")
        k_copied = sem("k_copied")
        f_z, f_abs, f_exp, f_ln, f_min, f_log, f_cum, f_c = [sem("f_" + n) for n in ("z", "abs", "exp", "ln", "min", "log", "cum", "c")]
        scores_done, biased_done, row_max, neg_max, exp_done, den_done, recip_done, probs_T, probsT_copied, pv_done, out_done = [
            sem(n) for n in ("scores_done", "biased_done", "row_max", "neg_max", "exp_done", "den_done", "recip_done",
                             "probs_T", "probsT_copied", "pv_done", "out_done")]
        gain_loaded, y_scaled, x_added = sem("gain_loaded"), sem("y_scaled"), sem("x_added")
        sq_first, mul_first, sums_ready = sem("sq_first"), sem("mul_first"), sem("sums_ready")
        coef_ready, conv_tap2, conv_tap1, gelu_done, glu_done, g_hi_done, g_lo_done = [
            sem(n) for n in ("coef_ready", "conv_tap2", "conv_tap1", "gelu_done", "glu_done", "g_hi_done", "g_lo_done")]
        second_loaded, second_pool, second_dve = sem("second_loaded"), sem("second_pool"), sem("second_dve")
        r_copied, gate_logits, ga_abs, ga_exp, ga_ln, ga_log, cum_done, b_ready = [
            sem(n) for n in ("r_copied", "gate_logits", "ga_abs", "ga_exp", "ga_ln", "ga_log", "cum_done", "b_ready")]
        cleared, rel_ready, decayed, qk_decayed, level_scores, level_added, gla_out, gla_copied = [
            sem(n) for n in ("cleared", "rel_ready", "decayed", "qk_decayed", "level_scores", "level_added", "gla_out", "gla_copied")]
        z_done, zs_done, zabs_done, zexp_done, zln_done, zmask_done, zmax_done, sp_done, spm_done, inc_done, t_done, a_done, so_done, so_copied = [
            sem(n) for n in ("z_done", "zs_done", "zabs_done", "zexp_done", "zln_done", "zmask_done", "zmax_done", "sp_done",
                             "spm_done", "inc_done", "t_done", "a_done", "so_done", "so_copied")]
        sgu_sq, sgu_mean, sgu_root, sgu_rstd, sgu_vn, sguT_done, sguT_ready, sgu_mixed, sgu_done = [
            sem(n) for n in ("sgu_sq", "sgu_mean", "sgu_root", "sgu_rstd", "sgu_vn", "sguT_done", "sguT_ready", "sgu_mixed", "sgu_done")]
        mem_loaded, hsq_done, hsum_done, hmean, hroot, hrstd, hscaled, hgated = [
            sem(n) for n in ("mem_loaded", "hsq_done", "hsum_done", "hmean", "hroot", "hrstd", "hscaled", "hgated")]
        xs_done, xmax_done, xneg_done, xexp_done, xrecip_done, xnorm_done, xpT_done, xpT_copied, xo_done, xo_hi, xo_lo = [
            sem(n) for n in ("xs_done", "xmax_done", "xneg_done", "xexp_done", "xrecip_done", "xnorm_done", "xpT_done",
                             "xpT_copied", "xo_done", "xo_hi", "xo_lo")]
        out_scaled0, out_scaled, stored, x_gained = sem("out_scaled0"), sem("out_scaled"), sem("stored"), sem("x_gained")

        def st(k, n=2):
            return stat[:, 4 * k:4 * k + n]

        def wide(t, s, kcs, w):
            return t[:, s, 0:kcs * w].rearrange("p (k n) -> p k n", k=kcs)

        def broadcast(ap, shape):
            return ap.unsqueeze(2).broadcast_to(shape)

        def evacuated(g, off=0):
            return 2 * (g + 1) + off

        def piece_size(u):
            g = max(i for i in range(len(PLAN)) if FIRST_PIECE[i] <= u)
            return P * 4 if PLAN[g][0] == "w_down" and u - FIRST_PIECE[g] >= 20 else PIECE

        block = ctx.enter_context(nc.Block())

        @block.sync
        def _(sp):
            def load(src, row, kcs, col, w, u, i=None, step=0):
                s = u % SLOTS
                if u >= SLOTS:
                    sp.wait_ge(lo_ready, u - SLOTS + 1 + (0 if i is None else i * step))
                rows = src[row:row + kcs * P]
                cols = rows[:, col:col + w] if i is None or isinstance(col, int) else rows[:, bass.ds(col, w)]
                sp.dma_start(wide(raw, s, kcs, w), cols.rearrange("(k p) n -> p k n", p=P)).then_inc(raw_loaded[s], 16)

            def group(src, col, g, i=None, step=0, pieces=(2,) * 8, w=W):
                row = 0
                for j, kcs in enumerate(pieces):
                    load(src, row, kcs, col, w, FIRST_PIECE[g] + j, i, step)
                    row += kcs * P

            w_in = A["w_in"][0]
            xr = A["x"][0].rearrange("(b p) d -> b p d", p=P)
            for b in range(NB):
                sp.dma_start(x_tok[:, b, :], xr[b]).then_inc(x_loaded[b], 16)
            group(w_in, KA, 0, pieces=(4,) * 4, w=256)
            sp.dma_start(fr_raw[:, :, :], w_in[:, FB:FB + 16].rearrange("(k p) n -> p k n", p=P)).then_inc(fr_loaded, 16)
            for g, col in enumerate([QA, QA + W, VB, VB + W, QB, KB, QB + W, KB + W], 1):
                group(w_in, col, g)
            with sp.Fori(0, 2) as i:
                for e in range(2):
                    group(A["w_out"][0], i * (2 * W) + e * W, GROUP["w_out"][e], i, 16)
            with sp.Fori(0, 11) as i:
                for e in range(2):
                    group(A["w_up"][0], i * W + e * D_FF, GROUP["w_up"][e], i, 16)
            with sp.Fori(0, 2) as i:
                for e in range(2):
                    group(A["w_down"][0], i * (2 * W) + e * W, GROUP["w_down"][e], i, 48, pieces=DOWN)
            w_in2 = A["w_in_2"][0]
            sp.wait_ge(fr_split_lo, 1)
            sp.dma_start(fr_raw[:, :, :], w_in2[:, GLR:GLR + 16].rearrange("(k p) n -> p k n", p=P)).then_inc(fr_loaded, 16)
            group(w_in2, GLQ, GROUP["gla_qk"][0])
            group(w_in2, GLV, GROUP["gla_v"][0])
            with sp.Fori(0, 3) as i:
                for e in range(2):
                    group(w_in2, i * (2 * W) + e * W, GROUP["sb_q"][e], i, 16)
            for n, col in (("gla_g", GLG), ("sgu_u", SGUU), ("sgu_v", SGUV), ("sgu_g", SGUG)):
                group(w_in2, col, GROUP[n][0])
            sp.wait_ge(z_done, SB_HEADS)
            mr = A["mem_2"][0].rearrange("(b p) d -> b p d", p=P)
            for b in range(NB):
                sp.dma_start(mem_tok[:, b, :], mr[b]).then_inc(mem_loaded, 16)
            for e in range(2):
                group(w_in2, SBG + e * W, GROUP["sb_g"][e])
            group(A["w_xkv_2"][0], 0, GROUP["xk"][0])
            group(A["w_xkv_2"][0], W, GROUP["xv"][0])
            with sp.Fori(0, 2) as i:
                for e in range(2):
                    group(A["w_out_2"][0], i * (2 * W) + e * W, GROUP["w_out2"][e], i, 16)
            group(A["w_xq_2"][0], 0, GROUP["xq"][0])
            for e in range(4):
                group(A["w_xo_2"][0], e * W, GROUP["xo"][e], pieces=(2, 2))
            orr = out[0].rearrange("(b p) d -> b p d", p=P)
            for b in range(NB):
                sp.wait_ge(out_scaled if b else out_scaled0, 1)
                sp.dma_start(orr[b], mem_tok[:, b, :]).then_inc(stored, 16)
            sp.wait_ge(stored, 16 * NB)

        @block.gpsimd
        def _(pool):
            pool.memset(ident[:, :], 0.0).then_inc(ident_ready, 1)
            pool.wait_ge(ident_ready, 1)
            pool.affine_select(out=ident[:, :], in_=ident[:, :], compare_op=ALU.not_equal, fill=1.0, base=0,
                               pattern=[[-1, P]], channel_multiplier=1).then_inc(ident_ready, 1)
            pool.dma_start(conv_rows[:, 0:3, :], A["conv_w"][0].rearrange("c (t p) -> t c p", p=P)).then_inc(conv_loaded, 16)
            pool.dma_start(conv_rows[:, 3, :], A["conv_b"][0].rearrange("(t p) -> t p", p=P)).then_inc(conv_loaded, 16)
            pool.dma_start(sink[:, :], A["sinks"][0].partition_broadcast(P)).then_inc(consts_loaded, 16)
            pool.dma_start(bf[:, :], A["b_forget"][0].partition_broadcast(P)).then_inc(consts_loaded, 16)
            pool.dma_start(mix_gain[:, :], A["post_mix_g"][0].partition_broadcast(P)).then_inc(gain_loaded, 16)
            pool.memset(tri[:, :], 1.0).then_inc(pool_ready, 1)
            pool.memset(foxm[:, :], 0.0).then_inc(pool_ready, 1)
            pool.memset(sel[:, :, :], 0.0).then_inc(pool_ready, 1)
            pool.iota(distm[:, 0:128], [[-1, 128]], base=0, channel_multiplier=1, allow_small_or_imprecise_dtypes=True).then_inc(pool_ready, 1)
            pool.iota(distm[:, 128:384], [[-1, 256]], base=128, channel_multiplier=1, allow_small_or_imprecise_dtypes=True).then_inc(pool_ready, 1)
            pool.wait_ge(pool_ready, 5)
            pool.affine_select(out=tri[:, :], in_=tri[:, :], compare_op=ALU.is_ge, fill=0.0, base=0,
                               pattern=[[1, P]], channel_multiplier=-1).then_inc(pool_ready, 1)
            pool.affine_select(out=sel[:, :, :], in_=sel[:, :, :], compare_op=ALU.not_equal, fill=1.0, base=0,
                               pattern=[[-1, NH], [0, P]], channel_multiplier=1).then_inc(pool_ready, 1)
            for t, fill in ((distm, BIG), (foxm, -BIG)):
                pool.affine_select(out=t[:, 0:128], in_=t[:, 0:128], compare_op=ALU.is_ge, fill=fill, base=0,
                                   pattern=[[-1, 128]], channel_multiplier=1).then_inc(pool_ready, 1)
                pool.affine_select(out=t[:, 128:384], in_=t[:, 128:384], compare_op=ALU.is_ge, fill=fill, base=128,
                                   pattern=[[-1, 256]], channel_multiplier=1).then_inc(pool_ready, 1)
            pool.wait_ge(pool_ready, 11)
            pool.affine_select(out=distm[:, 128:384], in_=distm[:, 128:384], compare_op=ALU.is_ge, fill=BIG,
                               base=WINDOW - 1 - 128, pattern=[[1, 256]], channel_multiplier=-1).then_inc(pool_ready, 1)
            pool.wait_ge(banks_free, evacuated(0))
            for kv in range(2):
                for half in range(2):
                    pool.dma_start(ka2[half * HD:(half + 1) * HD, kv, :], kaT[kv * HD:(kv + 1) * HD, :]).then_inc(k_copied, 16)
            pool.wait_ge(mm_done, FIRST_PIECE[GROUP["w_down"][0]])
            pool.dma_start(ffn_gain[:, :], A["post_ffn_g"][0].partition_broadcast(P)).then_inc(gain_loaded, 16)
            pool.wait_ge(mm_done, FIRST_PIECE[GROUP["gla_qk"][0]])
            pool.dma_start(wgu[:, :], A["w_gla_gate_up_2"][0]).then_inc(second_loaded, 16)
            pool.dma_start(bgg[:, :], A["b_gla_gate_2"][0].rearrange("(a n) -> a n", a=1)).then_inc(second_loaded, 16)
            pool.dma_start(sgu_gain[:, :], A["sgu_norm_2"][0].partition_broadcast(P)).then_inc(second_loaded, 16)
            pool.dma_start(w_sgu[:, :, :], A["w_sgu_2"][0].rearrange("g t s -> t g s")).then_inc(second_loaded, 16)
            pool.iota(xor_s[:, :], [[0, P]], base=0, channel_multiplier=1).then_inc(second_pool, 1)
            pool.iota(xor_t[:, :], [[1, P]], base=0, channel_multiplier=0).then_inc(second_pool, 1)
            pool.memset(sb_neg[:, :], 0.0).then_inc(second_pool, 1)
            pool.memset(sb_one[:, :], 1.0).then_inc(second_pool, 1)
            pool.memset(tri_neg[:, :], -1.0).then_inc(second_pool, 1)
            pool.memset(ones_neg[:, :], -1.0).then_inc(second_pool, 1)
            pool.wait_ge(second_pool, 6)
            pool.affine_select(out=sb_neg[:, :], in_=sb_neg[:, :], compare_op=ALU.is_gt, fill=-BIG, base=0,
                               pattern=[[1, P]], channel_multiplier=-1).then_inc(second_pool, 1)
            pool.affine_select(out=sb_one[:, :], in_=sb_one[:, :], compare_op=ALU.is_gt, fill=0.0, base=0,
                               pattern=[[1, P]], channel_multiplier=-1).then_inc(second_pool, 1)
            pool.affine_select(out=tri_neg[:, :], in_=tri_neg[:, :], compare_op=ALU.is_ge, fill=0.0, base=0,
                               pattern=[[-1, P]], channel_multiplier=1).then_inc(second_pool, 1)
            pool.wait_ge(so_copied, SB_HEADS)
            pool.dma_start(out_gain[:, :], A["final_norm_2"].partition_broadcast(P)).then_inc(gain_loaded, 16)

        @block.scalar
        def _(act):
            def split(u, i=None, step=0, n=None):
                if u >= TOTAL:
                    return
                s = u % SLOTS
                n = n or piece_size(u)
                act.wait_ge(raw_loaded[s], 16 * (u // SLOTS + 1) + (0 if i is None else i * (16 * step // SLOTS)))
                if u >= SLOTS:
                    act.wait_ge(mm_done, u - SLOTS + 1 + (0 if i is None else i * step))
                act.activation(w_hi[:, s, 0:n], raw[:, s, 0:n], ACT.Copy).then_inc(hi_ready, 1)

            def group(g, i=None, step=0, side=None):
                u = FIRST_PIECE[g]
                for j in range(PLAN[g][1]):
                    split(u + j + SLOTS, i, step)
                    if side:
                        side(j)
                act.wait_ge(mm_done, FIRST_PIECE[g + 1] + (0 if i is None else i * step))

            def out_of(g, b):
                return bank[2 * (g % 2) + b][:, :]

            def copy_out(dst, g, b=0, func=ACT.Copy):
                act.activation(dst, out_of(g, b), func).then_inc(banks_free, 1)

            def phase(n):
                at = GAIN_AT[PHASES[n]]
                if n == 0:
                    act.wait_ge(tables_ready, 1)
                for c in range(KC):
                    if c % 2 == 0:
                        act.wait_ge(tr_done, (KC * n + c) // 2 + 1)
                    ins = act.activation(hT_hi[:, c, :], bank[pair_bank(n, c // 2)][:, c % 2 * S:(c % 2 + 1) * S], ACT.Copy,
                                         scale=gains[:, at + c:at + c + 1])
                    if c % 2:
                        ins.then_inc(hiT_done, 1)

            n_squares = [0]

            def square(src, col, done, jk):
                if done is squares:
                    if n_squares[0]:
                        act.wait_ge(squares, n_squares[0])
                    n_squares[0] += 1
                act.activation(jk, src, ACT.Square, accum_out=col).then_inc(done, 1)

            def root(n, k, wait, done, width=2):
                act.wait_ge(wait, n)
                act.activation(stat[:, 4 * k:4 * k + width], stat[:, 4 * k:4 * k + width], ACT.Sqrt).then_inc(done, 1)

            def gain(name, lo, n, src):
                r = GAIN_AT[name] + lo
                act.dma_start(gain_rows[r:r + n, :], src[0].rearrange("(k p) -> k p", p=P)).then_inc(rows_loaded, 16)
            gain("pre_mix", 0, 16, A["pre_mix_g"])
            gain("grp", 0, 8, A["grp_swa_g"])
            gain("grp", 8, 8, A["grp_fox_g"])
            gain("pre_ffn", 0, 16, A["pre_ffn_g"])
            gain("norm_mix_2", 0, 16, A["norm_mix_2"])
            gain("out_norm_2", 0, 16, A["out_norm_2"])
            gain("norm_mem_2", 0, 16, A["norm_mem_2"])
            gain("norm_xattn_2", 0, 16, A["norm_xattn_2"])
            act.dma_start(gain_rows[BSGU_AT:BSGU_AT + SGU_GROUPS, :], A["b_sgu_2"][0]).then_inc(rows_loaded, 16)
            act.wait_ge(x_loaded[0], 16)
            square(x_tok[:, 0, :], st(0)[:, 0:1], squares, junk[:, :])
            root(1, 0, mean_ready, root_ready)
            for u in range(SLOTS):
                split(u)
            act.wait_ge(fr_loaded, 16)
            act.activation(fr_hi[:, :, :], fr_raw[:, :, :], ACT.Copy).then_inc(fr_split_hi, 1)
            phase(0)

            def probs_copy(i):
                act.wait_ge(probs_T, i + 1)
                if i >= 2:
                    act.wait_ge(pv_done, i - 1)
                act.activation(probsT[:, i % 2, :], bank[6][:, 0:384], ACT.Copy).then_inc(probsT_copied, 1)

            def exps(i):
                act.wait_ge(neg_max, i + 1)
                if i >= 2:
                    act.wait_ge(probs_T, i - 1)
                    act.wait_ge(recip_done, i - 1)
                s = i % 2
                nm, den, es = st(8 + s), st(10 + s), st(12 + s)
                if i < NH:
                    act.activation(es, nm, ACT.Exp, bias=sink[:, i:i + 1]).then_inc(exp_done, 1)
                else:
                    act.activation(es, nm, ACT.Exp).then_inc(exp_done, 1)
                act.activation(probs[:, s, 0:128], biased[:, s, 0:128], ACT.Exp, bias=nm[:, 0:1], scale=HD ** -0.5,
                               accum_out=den[:, 0:1]).then_inc(exp_done, 1)
                act.activation(probs[:, s, 128:384], biased[:, s, 128:384], ACT.Exp, bias=nm[:, 1:2], scale=HD ** -0.5,
                               accum_out=den[:, 1:2]).then_inc(exp_done, 1)

            def head(i):
                if 1 <= i <= 2 * NH:
                    probs_copy(i - 1)
                if i < 2 * NH:
                    exps(i)

            group(0)
            act.activation(kaT[:, :], bank[0][:, 0:S], ACT.Copy).then_inc(banks_free, 1)
            act.wait_ge(f_z, 1)
            act.activation(fa[:, :, :], fz[:, :, :], ACT.Abs).then_inc(f_abs, 1)
            act.wait_ge(f_abs, 1)
            act.activation(fa[:, :, :], fa[:, :, :], ACT.Exp, scale=-1.0).then_inc(f_exp, 1)
            act.wait_ge(f_exp, 1)
            act.activation(fa[:, :, :], fa[:, :, :], ACT.Ln, bias=1.0).then_inc(f_ln, 1)
            for g in (1, 2):
                group(g)
                copy_out(qaT[:, 4 * (g - 1):4 * (g - 1) + 2, :].rearrange("p a b -> p (a b)"), g)
            for g in (3, 4):
                group(g, side=lambda j, g=g: head(4 * (g - 3) + j // 2) if j % 2 else None)
                copy_out(vb[:, 0, W * (g - 3):W * (g - 2)], g)
            for n, g in enumerate((5, 6, 7, 8)):
                group(g, side=lambda j, n=n: head(8 + 4 * n + j // 2) if j % 2 else None)
                dst = (qbT, kbT)[n % 2]
                copy_out(dst[:, 4 * (n // 2):4 * (n // 2) + 2, :].rearrange("p a b -> p (a b)"), g)
            for i in range(24, 2 * NH + 2):
                head(i)
            act.wait_ge(out_done, 2 * NH)
            for b in range(NB):
                for k in range(2):
                    square(work[:, b, 1024 * k:1024 * (k + 1)], stat[:, 4 + 2 * b + k:5 + 2 * b + k], squares, junk[:, 0:1024])
            root(2, 1, mean_ready, root_ready, 4)
            phase(1)
            def take(g, i, step, jk, n):
                m = i * 2 + n % 4
                act.activation(jk[:, 0:W], out_of(g, 0), ACT.Square, accum_out=part_sq[:, 0, bass.ds(m, 1)]).then_inc(sq_first, 1)
                act.wait_ge(mul_first, n + 1 + i * 2)
                act.activation(jk[:, W:2 * W], out_of(g, 1), ACT.Square, accum_out=part_sq[:, 1, bass.ds(m, 1)]).then_inc(banks_free, 1)

            def x_squares(k, n):
                for b in range(NB):
                    act.wait_ge(x_added, n + b)
                    square(x_tok[:, b, :], st(k)[:, b:b + 1], squares, (junk if k == 3 else junk2)[:, :])

            with act.Fori(0, 2) as i:
                for e in range(2):
                    g = GROUP["w_out"][e]
                    group(g, i, 16)
                    if e == 0:
                        act.wait_ge(squares, 5)
                    take(g, i, 16, junk, e)
                    act.wait_ge(banks_free, evacuated(g) + i * 4)
            root(3, 2, mean_ready, root_ready)
            x_squares(3, 1)
            root(4, 3, mean_ready, root_ready)
            phase(2)
            def taps(e, i):
                g = GROUP["w_up"][e]
                cv = (cv_gate, cv_val)[e]
                act.wait_ge(coef_ready, i + 1)
                for ft in range(4):
                    ins = act.activation(cv[:, ft, :], bank[2 * (g % 2) + ft // 2][:, ft % 2 * S:(ft % 2 + 1) * S], ACT.Identity,
                                         bias=coef[:, e, 3, ft:ft + 1], scale=coef[:, e, 2, ft:ft + 1])
                ins.then_inc(conv_tap2, 1)

            def glu_hi(i):
                act.wait_ge(glu_done, i + 1)
                act.activation(g_hi[:, bass.ds(i * 4, 4), :], cv_val[:, :, :], ACT.Copy).then_inc(g_hi_done, 1)

            def up(i, last=None):
                group(GROUP["w_up"][0], i, 16, side=lambda j: glu_hi(last) if j == 2 and last is not None else None)
                taps(0, i)

                def gelu(j):
                    if j == 1:
                        act.wait_ge(banks_free, evacuated(GROUP["w_up"][0]) + i * 4)
                        act.activation(cv_gate[:, :, :], cv_gate[:, :, :], ACT.Gelu_apprx_tanh).then_inc(gelu_done, 1)
                group(GROUP["w_up"][1], i, 16, side=gelu)
                act.wait_ge(g_lo_done, i) if last is not None else None
                taps(1, i)

            up(0)
            with act.Fori(1, 11) as i:
                up(i, i - 1)
            glu_hi(10)
            with act.Fori(0, 2) as i:
                for e in range(2):
                    g = GROUP["w_down"][e]
                    group(g, i, 48)
                    if e == 0:
                        act.wait_ge(squares, 7)
                    take(g, i, 48, junk2, 4 + e)
                    act.wait_ge(banks_free, evacuated(g) + i * 4)
            root(5, 4, mean_ready, root_ready)
            x_squares(5, 3)
            root(6, 5, mean_ready, root_ready)
            act.wait_ge(fr_loaded, 32)
            act.wait_ge(fr_done, 1)
            act.activation(fr_hi[:, :, :], fr_raw[:, :, :], ACT.Copy).then_inc(fr_split_hi, 1)
            phase(3)

            g = GROUP["gla_qk"][0]
            group(g)
            act.activation(gqk[:, 0, :, :].rearrange("p a b -> p (a b)"), out_of(g, 0), ACT.Copy, scale=HD ** -0.5).then_inc(banks_free, 1)
            g = GROUP["gla_v"][0]
            act.wait_ge(fr_done, 2)
            act.activation(rT[:, :], bank[4][0:16, 0:S], ACT.Copy).then_inc(r_copied, 1)
            group(g)
            copy_out(gvv[:, 0, :], g)

            def gate_logs():
                act.wait_ge(gate_logits, 1)
                act.activation(la[:, :, :].rearrange("p a b -> p (a b)"), bank[5][:, :], ACT.Abs).then_inc(ga_abs, 1)
                act.wait_ge(ga_abs, 1)
                act.activation(la[:, :, :], la[:, :, :], ACT.Exp, scale=-1.0).then_inc(ga_exp, 1)
                act.wait_ge(ga_exp, 1)
                act.activation(la[:, :, :], la[:, :, :], ACT.Ln, bias=1.0).then_inc(ga_ln, 1)

            def decay_sums():
                act.wait_ge(cum_done, 1)
                act.activation(bT[:, :, :].rearrange("p a b -> p (a b)"), bank[6][:, :], ACT.Copy, scale=1.0 / GATE_TAU).then_inc(b_ready, 1)

            def level(n):
                if n == 0:
                    act.wait_ge(rel_ready, 1)
                half = P >> n
                for c, a in ((0, half), (1, 0)):
                    v = decay[:, c, :].rearrange("p (m c) -> p m c", c=2 * half)[:, :, a:a + half]
                    act.wait_ge(rel_ready, n + 1)
                    ins = act.activation(v, v, ACT.Exp)
                ins.then_inc(decayed, 1)

            def gla_side(n):
                if n == 0:
                    gate_logs()
                elif n == 2:
                    decay_sums()
                if n % 2 == 0 and 2 <= n < 18:
                    level(n // 2 - 1)
                if n == 22:
                    act.wait_ge(gla_out, 2)
                    act.activation(mix2[:, 0, 1024:1536], bank[6][:, :], ACT.Copy).then_inc(gla_copied, 1)

            dsts = [(sbq, 0), (sbq, 4), (sbk, 0), (sbk, 4)]
            for n in range(6):
                g = GROUP["sb_q"][0] + n
                group(g, side=lambda j, n=n: gla_side(4 * n + j // 2) if j % 2 else None)
                if n < 4:
                    copy_out(dsts[n][0][:, dsts[n][1]:dsts[n][1] + 2, :].rearrange("p a b -> p (a b)"), g)
                else:
                    copy_out(sbv[:, 0, W * (n - 4):W * (n - 3)], g)

            def stick(i):
                if i < SB_HEADS:
                    s = i % 2
                    act.wait_ge(z_done, i + 1)
                    if i >= 2:
                        act.wait_ge(zmask_done, i - 1)
                        act.wait_ge(sp_done, i - 1)
                    act.activation(z_s[:, s, :], bank[4][:, 0:384], ACT.Copy, scale=WIDE_SCALE).then_inc(zs_done, 1)
                    act.wait_ge(zs_done, i + 1)
                    act.activation(z_e[:, s, :], z_s[:, s, :], ACT.Abs).then_inc(zabs_done, 1)
                    act.wait_ge(zabs_done, i + 1)
                    act.activation(z_e[:, s, :], z_e[:, s, :], ACT.Exp, scale=-1.0).then_inc(zexp_done, 1)
                    act.wait_ge(zexp_done, i + 1)
                    act.activation(z_e[:, s, :], z_e[:, s, :], ACT.Ln, bias=1.0).then_inc(zln_done, 1)
                if 3 <= i < SB_HEADS + 3:
                    k = i - 3
                    act.wait_ge(t_done, k + 1)
                    if k >= 2:
                        act.wait_ge(so_done, k - 1)
                    act.activation(z_a[:, k % 2, :], z_m[:, k % 2, :], ACT.Exp).then_inc(a_done, 1)

            def both(dst, g, func):
                for b in range(NB):
                    copy_out(dst[b], g, b, func)

            gates = {"gla_g": 1024, "sgu_g": 1536}
            for n, name in enumerate(("gla_g", "sgu_u", "sgu_v", "sgu_g")):
                g = GROUP[name][0]
                group(g, side=lambda j, n=n: stick(3 * n + j // 2) if j in (1, 3, 5) else None)
                if name in gates:
                    both([gate[:, b, gates[name]:gates[name] + W] for b in range(NB)], g, ACT.Silu)
                else:
                    t = sgu_u if name == "sgu_u" else sgu_v
                    both([t[:, b, :] for b in range(NB)], g, ACT.Gelu_apprx_tanh)
            for n in range(2):
                g = GROUP["sb_g"][n]

                def side(j, n=n):
                    if n == 0 and j == 1:
                        for b in range(NB):
                            act.wait_ge(banks_free, evacuated(GROUP["sgu_v"][0]))
                            square(sgu_v[:, b, :], st(14)[:, b:b + 1], sgu_sq, junk2[:, b * W:(b + 1) * W])
                        root(1, 14, sgu_mean, sgu_root)
                    if n == 0 and j in (3, 5):
                        b = j // 2 - 1
                        act.wait_ge(mem_loaded, 32)
                        square(mem_tok[:, b, :], st(6)[:, b:b + 1], squares, junk2[:, :])
                    if n == 1 and j == 1:
                        root(7, 6, mean_ready, root_ready)
                group(g, side=side)
                both([gate[:, b, W * n:W * (n + 1)] for b in range(NB)], g, ACT.Silu)
            phase(4)
            act.wait_ge(hmean, 1)
            act.activation(stat[:, 128:160], stat[:, 128:160], ACT.Sqrt).then_inc(hroot, 1)
            g = GROUP["xk"][0]
            group(g)
            copy_out(xkT[:, 0:2, :].rearrange("p a b -> p (a b)"), g)
            g = GROUP["xv"][0]
            group(g)
            copy_out(xv[:, 0, :], g)
            phase(5)
            with act.Fori(0, 2) as i:
                for e in range(2):
                    g = GROUP["w_out2"][e]
                    group(g, i, 16)
                    for b in range(NB):
                        act.wait_ge(banks_free, evacuated(g) - 1 + b + i * 4)
                        act.activation(junk2[:, b * W:(b + 1) * W], x_tok[:, b, bass.ds(i * (2 * W) + e * W, W)], ACT.Square,
                                       accum_out=part_sq[:, b, bass.ds(i * 2 + e, 1)]).then_inc(sq_first, 1)
                    act.wait_ge(sq_first, 8 + 2 * (e + 1) + i * 4)
            root(8, 7, mean_ready, root_ready)
            phase(6)
            g = GROUP["xq"][0]
            group(g)
            copy_out(mix2[:, 0, 0:W], g)
            for h in range(XA_HEADS):
                act.wait_ge(xneg_done, h + 1)
                for b in range(NB):
                    ins = act.activation(x_p[:, h, b * S:(b + 1) * S], bank[4 + h][:, b * S:(b + 1) * S], ACT.Exp,
                                         bias=st(20 + h)[:, b:b + 1], scale=WIDE_SCALE, accum_out=st(24 + h)[:, b:b + 1])
                    ins.then_inc(xexp_done, 1)
            for h in range(XA_HEADS):
                act.wait_ge(xpT_done, h + 1)
                if h >= 2:
                    act.wait_ge(xo_done, h - 1)
                act.activation(x_pT[:, h % 2, :], bank[4 + h][:, :], ACT.Copy).then_inc(xpT_copied, 1)
            for h in range(XA_HEADS):
                act.wait_ge(xo_done, h + 1)
                act.activation(hT_hi[:, h, :], bank[4 + h][:, 0:S], ACT.Copy).then_inc(xo_hi, 1)
            for e in range(4):
                g = GROUP["xo"][e]
                group(g)
                for b in range(NB):
                    act.wait_ge(banks_free, evacuated(g) - 1 + b)
                    act.activation(junk2[:, b * W:(b + 1) * W], x_tok[:, b, e * W:(e + 1) * W], ACT.Square,
                                   accum_out=part_sq[:, b, e:e + 1]).then_inc(sq_first, 1)
                act.wait_ge(sq_first, 16 + 2 * (e + 1))
            root(9, 16, mean_ready, root_ready)
            act.wait_ge(rstd_ready, 9)
            act.activation(mem_tok[:, 0, :], x_tok[:, 0, :], ACT.Copy, scale=st(16)[:, 0:1]).then_inc(out_scaled0, 1)

        @block.vector
        def _(dve):
            def split(u, i=None, step=0, n=None):
                if u >= TOTAL:
                    return
                s = u % SLOTS
                n = n or piece_size(u)
                dve.wait_ge(hi_ready, u + 1 + (0 if i is None else i * step))
                dve.tensor_tensor(w_lo[:, s, 0:n], raw[:, s, 0:n], w_hi[:, s, 0:n].bitcast(F32), ALU.subtract).then_inc(lo_ready, 1)

            def group(g, i=None, step=0, side=None):
                u = FIRST_PIECE[g]
                for j in range(PLAN[g][1]):
                    split(u + j + SLOTS, i, step)
                    if side:
                        side(j)
                dve.wait_ge(mm_done, FIRST_PIECE[g + 1] + (0 if i is None else i * step))

            def out_of(g, b):
                return bank[2 * (g % 2) + b][:, :]

            def copy_out(dst, g, b=1):
                dve.tensor_copy(dst, out_of(g, b)).then_inc(banks_free, 1)

            def phase(n):
                at = GAIN_AT[PHASES[n]]
                for c in range(KC):
                    if c % 2 == 0:
                        dve.wait_ge(hiT_done, (KC * n + c) // 2 + 1)
                    dve.scalar_tensor_tensor(out=hT_lo[:, c, :], in0=bank[pair_bank(n, c // 2)][:, c % 2 * S:(c % 2 + 1) * S],
                                             scalar=gains[:, at + c:at + c + 1], in1=hT_hi[:, c, :].bitcast(F32),
                                             op0=ALU.mult, op1=ALU.subtract).then_inc(loT_done, 1)

            def rstd(n, k, n_sq, size, width=2):
                a = stat[:, 4 * k:4 * k + width]
                if n_sq:
                    dve.wait_ge(squares, n_sq)
                dve.tensor_scalar(a, a, 1.0 / size, EPS, ALU.mult, ALU.add).then_inc(mean_ready, 1)
                dve.wait_ge(root_ready, n)
                dve.reciprocal(a, a).then_inc(rstd_ready, 1)
                dve.wait_ge(rstd_ready, n)

            def square1(src, col, n, jk):
                dve.tensor_tensor_reduce(jk, src, src, 1.0, 0.0, ALU.mult, ALU.add, col).then_inc(squares_d, 1)
                dve.wait_ge(squares_d, n)

            def scale_rows(dst, src, k):
                for c in range(2):
                    for b in range(NB):
                        dve.tensor_scalar(dst[:, b, c * D // 2:(c + 1) * D // 2], src[:, b, c * D // 2:(c + 1) * D // 2],
                                          st(k)[:, b:b + 1], None, ALU.mult).then_inc(scaled, 1)

            n_sums = [0]

            def total_squares(k):
                dve.tensor_reduce(st(k), part_sq[:, :, 0:4], AX, ALU.add).then_inc(sums_ready, 1)
                n_sums[0] += 1
                dve.wait_ge(sums_ready, n_sums[0])

            dve.memset(ones[:, :], 1.0).then_inc(dve_ready, 1)
            dve.wait_ge(x_loaded[1], 16)
            dve.wait_ge(x_loaded[0], 16)
            square1(x_tok[:, 1, :], st(0)[:, 1:2], 1, junk_d[:, :])
            rstd(1, 0, 1, D)
            scale_rows(work, x_tok, 0)
            dve.wait_ge(rows_T, 1)
            dve.tensor_copy(gains[:, :], bank[6][:, 0:GAIN_ROWS]).then_inc(tables_ready, 1)
            for u in range(SLOTS):
                split(u)
            dve.wait_ge(fr_split_hi, 1)
            dve.tensor_tensor(fr_lo[:, :, :], fr_raw[:, :, :], fr_hi[:, :, :].bitcast(F32), ALU.subtract).then_inc(fr_split_lo, 1)
            dve.wait_ge(tables_ready, 1)
            phase(0)

            def bias(i):
                s = i % 2
                dve.wait_ge(scores_done, i + 1)
                if i >= 2:
                    dve.wait_ge(exp_done, 3 * (i - 1))
                h = i % NH
                if i < NH:
                    slope = 2.0 ** (-8.0 * (h + 1) / NH)
                    dve.scalar_tensor_tensor(out=biased[:, s, :], in0=distm[:, :], scalar=-slope * HD ** 0.5,
                                             in1=bank[4 + s][:, 0:384], op0=ALU.mult, op1=ALU.add).then_inc(biased_done, 2)
                else:
                    for b, (lo, hi) in enumerate(((0, 128), (128, 384))):
                        dve.scalar_tensor_tensor(out=biased[:, s, lo:hi], in0=bank[4 + s][:, lo:hi], scalar=c8[:, b, h:h + 1],
                                                 in1=foxm[:, lo:hi], op0=ALU.add, op1=ALU.add).then_inc(biased_done, 1)
                dve.wait_ge(biased_done, 2 * (i + 1))
                mx, nm = st(18 + s), st(8 + s)
                dve.tensor_reduce(mx[:, 0:1], biased[:, s, 0:128], AX, ALU.max).then_inc(row_max, 1)
                dve.tensor_reduce(mx[:, 1:2], biased[:, s, 128:384], AX, ALU.max).then_inc(row_max, 1)
                dve.wait_ge(row_max, 2 * (i + 1))
                if i < NH:
                    dve.tensor_scalar(nm, mx, sink8[:, h:h + 1], -HD ** -0.5, ALU.max, ALU.mult).then_inc(neg_max, 1)
                else:
                    dve.tensor_scalar(nm, mx, -HD ** -0.5, None, ALU.mult).then_inc(neg_max, 1)

            def recip(i):
                s = i % 2
                den, es, rd = st(10 + s), st(12 + s), st(30 + s)
                dve.wait_ge(exp_done, 3 * (i + 1))
                if i >= 2:
                    dve.wait_ge(out_done, i - 1)
                if i < NH:
                    dve.tensor_tensor(rd, den, es, ALU.add).then_inc(den_done, 1)
                    dve.wait_ge(den_done, i + 1)
                    dve.reciprocal(rd, rd).then_inc(recip_done, 1)
                else:
                    dve.reciprocal(rd, den).then_inc(recip_done, 1)

            def normalise(i):
                s = i % 2
                dve.wait_ge(pv_done, i + 1)
                dve.wait_ge(recip_done, i + 1)
                dve.tensor_tensor(work[:, :, i * HD:(i + 1) * HD], bank[7][:, 0:P].rearrange("p (b n) -> p b n", b=NB),
                                  broadcast(st(30 + s), [P, NB, HD]), ALU.mult).then_inc(out_done, 1)

            def head(i):
                if i < 2 * NH:
                    bias(i)
                if 1 <= i <= 2 * NH:
                    recip(i - 1)
                if 2 <= i < 2 * NH + 2:
                    normalise(i - 2)

            dve.wait_ge(pool_ready, 12)
            dve.wait_ge(consts_loaded, 32)
            dve.tensor_scalar(sink8[:, :], sink[:, :], HD ** 0.5, None, ALU.mult).then_inc(dve_ready, 1)
            group(0)
            dve.tensor_copy(va[:, :, :].rearrange("p a b -> p (a b)"), bank[1][:, 0:S]).then_inc(banks_free, 1)
            dve.wait_ge(fr_done, 1)
            dve.tensor_tensor(fz[:, :, :], bank[7][:, 0:32].rearrange("p (b n) -> p b n", b=NB),
                              bf[:, :].unsqueeze(1).broadcast_to([P, NB, 16]), ALU.add).then_inc(f_z, 1)
            dve.wait_ge(f_z, 1)
            dve.tensor_scalar(fm[:, :, :], fz[:, :, :], 0.0, None, ALU.min).then_inc(f_min, 1)
            dve.wait_ge(f_min, 1)
            dve.wait_ge(f_ln, 1)
            dve.tensor_tensor(lf[:, :, :], fm[:, :, :], fa[:, :, :], ALU.subtract).then_inc(f_log, 1)
            for g in (1, 2):
                group(g)
                copy_out(qaT[:, 4 * (g - 1) + 2:4 * g, :].rearrange("p a b -> p (a b)"), g)
                if g == 1:
                    dve.wait_ge(f_cum, 1)
                    dve.tensor_scalar(c8[:, :, :].rearrange("p a b -> p (a b)"), bank[6][:, 0:32], HD ** 0.5, None, ALU.mult).then_inc(f_c, 1)
                    dve.tensor_scalar(cT8[:, :], bank[7][0:16, 0:S], -HD ** 0.5, None, ALU.mult).then_inc(f_c, 1)
            dve.wait_ge(conv_T, 1)
            dve.tensor_copy(conv[:, :, :].rearrange("p a b -> p (a b)"), bank[7][:, 0:4 * 2 * FFT]).then_inc(conv_ready, 1)
            for g in (3, 4):
                group(g, side=lambda j, g=g: head(4 * (g - 3) + j // 2) if j % 2 else None)
                copy_out(vb[:, 1, W * (g - 3):W * (g - 2)], g)
            for n, g in enumerate((5, 6, 7, 8)):
                group(g, side=lambda j, n=n: head(8 + 4 * n + j // 2) if j % 2 else None)
                dst = (qbT, kbT)[n % 2]
                copy_out(dst[:, 4 * (n // 2) + 2:4 * (n // 2) + 4, :].rearrange("p a b -> p (a b)"), g)
            for i in range(24, 2 * NH + 2):
                head(i)
            dve.wait_ge(out_done, 2 * NH)
            rstd(2, 1, 5, D_SWA, 4)
            for k in range(2):
                for b in range(NB):
                    dve.tensor_scalar(work[:, b, 1024 * k:1024 * (k + 1)], work[:, b, 1024 * k:1024 * (k + 1)],
                                      stat[:, 4 + 2 * b + k:5 + 2 * b + k], None, ALU.mult).then_inc(scaled, 1)
            phase(1)
            def take(dst, gain, g, i, n, step_n):
                for b in (1, 0):
                    if b == 0:
                        dve.wait_ge(sq_first, n + 1 + i * 2)
                    c = bass.ds(i * (2 * W) + step_n * W, W)
                    dve.tensor_tensor(dst[:, b, c], out_of(g, b), gain[:, c], ALU.mult).then_inc(mul_first if b else banks_free, 1)

            dve.wait_ge(gain_loaded, 16)
            with dve.Fori(0, 2) as i:
                for e in range(2):
                    g = GROUP["w_out"][e]
                    group(g, i, 16)
                    take(work, mix_gain, g, i, e, e)

            def residual(n, k, src, m, done):
                dve.wait_ge(banks_free, m)
                total_squares(k)
                rstd(n, k, 0, D)
                for b in range(NB):
                    dve.scalar_tensor_tensor(out=x_tok[:, b, :], in0=src[:, b, :], scalar=st(k)[:, b:b + 1], in1=x_tok[:, b, :],
                                             op0=ALU.mult, op1=ALU.add).then_inc(x_added, 1)

            residual(3, 2, work, evacuated(GROUP["w_out"][3]), 0)
            rstd(4, 3, 7, D)
            scale_rows(work, x_tok, 3)
            phase(2)
            def taps(e, i):
                g = GROUP["w_up"][e]
                cv = (cv_gate, cv_val)[e]
                dve.wait_ge(conv_tap2, 2 * i + e + 1)
                for tap in (1, 0):
                    back = 2 - tap
                    for ft in range(4):
                        ps = bank[2 * (g % 2) + ft // 2][:, ft % 2 * S:(ft % 2 + 1) * S]
                        ins = dve.scalar_tensor_tensor(out=cv[:, ft, back:S], in0=ps[:, 0:S - back], scalar=coef[:, e, tap, ft:ft + 1],
                                                       in1=cv[:, ft, back:S], op0=ALU.mult, op1=ALU.add)
                        if tap == 0 and ft % 2:
                            ins.then_inc(banks_free, 1)
                    if tap:
                        ins.then_inc(conv_tap1, 1)
                        dve.wait_ge(conv_tap1, 2 * i + e + 1)

            def glu(i):
                dve.wait_ge(gelu_done, i + 1)
                dve.wait_ge(banks_free, evacuated(GROUP["w_up"][1]) + i * 4)
                dve.tensor_tensor(cv_val[:, :, :], cv_gate[:, :, :], cv_val[:, :, :], ALU.mult).then_inc(glu_done, 1)

            def glu_lo(i):
                dve.wait_ge(g_hi_done, i + 1)
                dve.tensor_tensor(g_lo[:, bass.ds(i * 4, 4), :], cv_val[:, :, :], g_hi[:, bass.ds(i * 4, 4), :].bitcast(F32),
                                  ALU.subtract).then_inc(g_lo_done, 1)

            def up(i, last=None):
                if last is not None:
                    dve.wait_ge(banks_free, evacuated(GROUP["w_up"][1]) + last * 4)
                for e in range(2):
                    ins = dve.tensor_copy(coef[:, e, :, :], conv[:, :, bass.ds(i * 4 + e * FFT, 4)])
                ins.then_inc(coef_ready, 1)

                def finish(j):
                    if last is not None and j == 1:
                        glu(last)
                    if last is not None and j == 3:
                        glu_lo(last)
                group(GROUP["w_up"][0], i, 16, side=finish)
                dve.wait_ge(coef_ready, i + 1)
                taps(0, i)
                group(GROUP["w_up"][1], i, 16)
                taps(1, i)

            dve.wait_ge(conv_ready, 1)
            up(0)
            with dve.Fori(1, 11) as i:
                up(i, i - 1)
            glu(10)
            glu_lo(10)
            dve.wait_ge(gain_loaded, 32)
            with dve.Fori(0, 2) as i:
                for e in range(2):
                    g = GROUP["w_down"][e]
                    group(g, i, 48)
                    take(y_tok, ffn_gain, g, i, 4 + e, e)
            residual(5, 4, y_tok, evacuated(GROUP["w_down"][3]), 2)
            rstd(6, 5, 9, D)
            scale_rows(mix2, x_tok, 5)
            dve.wait_ge(fr_split_hi, 2)
            dve.tensor_tensor(fr_lo[:, :, :], fr_raw[:, :, :], fr_hi[:, :, :].bitcast(F32), ALU.subtract).then_inc(fr_split_lo, 1)
            phase(3)

            dve.wait_ge(second_pool, 9)
            dve.tensor_tensor(xor_s[:, :], xor_s[:, :], xor_t[:, :], ALU.bitwise_xor).then_inc(second_dve, 1)
            dve.wait_ge(second_dve, 1)
            dve.tensor_copy(lev[:, :], xor_s[:, :]).then_inc(second_dve, 1)
            dve.tensor_scalar(prod[:, 0:P], tri[:, :], -1024.0, 1024.0, ALU.mult, ALU.add).then_inc(second_dve, 1)
            dve.wait_ge(second_dve, 3)
            dve.tensor_tensor(lev[:, :], lev[:, :], prod[:, 0:P], ALU.add).then_inc(second_dve, 1)
            dve.wait_ge(second_dve, 4)
            for n in range(1, 8):
                dve.tensor_scalar(levels[:, n - 1, :], lev[:, :], float(P >> n), None, ALU.is_ge).then_inc(second_dve, 1)
            dve.wait_ge(second_dve, 11)
            for n in range(1, 8):
                dve.scalar_tensor_tensor(out=levels[:, n - 1, :], in0=lev[:, :], scalar=float(2 * (P >> n)), in1=levels[:, n - 1, :],
                                         op0=ALU.is_lt, op1=ALU.mult).then_inc(second_dve, 1)
            dve.tensor_scalar(levels[:, 7, :], lev[:, :], 1.0, None, ALU.is_lt).then_inc(second_dve, 1)
            dve.wait_ge(second_dve, 19)

            g = GROUP["gla_qk"][0]
            group(g)
            copy_out(gqk[:, 1, :, :].rearrange("p a b -> p (a b)"), g)
            g = GROUP["gla_v"][0]
            group(g)
            copy_out(gvv[:, 1, :], g)

            def gate_logs():
                dve.wait_ge(ga_ln, 1)
                dve.scalar_tensor_tensor(out=la[:, :, :].rearrange("p a b -> p (a b)"), in0=bank[5][:, :], scalar=0.0,
                                         in1=la[:, :, :].rearrange("p a b -> p (a b)"), op0=ALU.min, op1=ALU.subtract).then_inc(ga_log, 1)
                dve.memset(acc[:, :, :], 0.0).then_inc(cleared, 1)
                dve.memset(decay[:, :, :], 0.0).then_inc(cleared, 1)
                dve.memset(qkd[:, :, :, :], 0.0).then_inc(cleared, 1)

            def level(n):
                half = P >> n
                k = 2 * S // (2 * half)
                bv = bT[:, :, :].rearrange("p a (m c) -> p (a m) c", c=2 * half)
                ref = bv[:, :, half - 1:half].broadcast_to([P, k, half])
                if n == 0:
                    dve.wait_ge(b_ready, 1)
                    dve.wait_ge(cleared, 3)
                def halves(ap, a):
                    return ap.rearrange("p (m c) -> p m c", c=2 * half)[:, :, a:a + half]
                if n >= 1:
                    dve.wait_ge(qk_decayed, n)
                dve.tensor_tensor(halves(decay[:, 0, :], half), bv[:, :, half:2 * half], ref, ALU.subtract)
                dve.tensor_tensor(halves(decay[:, 1, :], 0), ref, bv[:, :, 0:half], ALU.subtract).then_inc(rel_ready, 1)
                dve.wait_ge(decayed, n + 1)
                if n == 0:
                    dve.wait_ge(banks_free, evacuated(GROUP["gla_qk"][0]))
                for c, a in ((0, half), (1, 0)):
                    ins = dve.tensor_tensor(halves(qkd[:, c, :, :].rearrange("p a b -> p (a b)"), a),
                                            halves(gqk[:, c, :, :].rearrange("p a b -> p (a b)"), a),
                                            halves(decay[:, c, :], a), ALU.mult)
                ins.then_inc(qk_decayed, 1)

            def collect(n):
                dve.wait_ge(level_scores, n + 1)

                def heads(ap):
                    return ap.rearrange("p (c m t) -> p c m t", c=2, m=2)

                def pairs(b):
                    return upper[:, 2 * b:2 * b + 2, 0:2 * P].rearrange("p c (m t) -> p c m t", m=2)
                if n == 0:
                    dve.tensor_copy(heads(inter[:, :]), pairs(0)).then_inc(level_added, 2)
                    return
                if n >= 2:
                    dve.wait_ge(level_added, 2 * n)
                for b in range(NB):
                    mask = levels[:, n - 1, :].bitcast(I32).unsqueeze(1).unsqueeze(1).broadcast_to([P, 2, 2, P])
                    dve.copy_predicated(heads(acc[:, b, :]), mask, pairs(b)).then_inc(level_added, 1)

            def gla_side(n):
                if n == 0:
                    gate_logs()
                if n % 2 == 0 and 4 <= n <= 20:
                    collect(n // 2 - 2)
                if n % 2 == 0 and 2 <= n < 18:
                    level(n // 2 - 1)
                if n == 22:
                    dve.wait_ge(gla_out, 2)
                    dve.tensor_copy(mix2[:, 1, 1024:1536], bank[7][:, :]).then_inc(gla_copied, 1)

            dsts = [(sbq, 0), (sbq, 4), (sbk, 0), (sbk, 4)]
            for n in range(6):
                g = GROUP["sb_q"][0] + n
                group(g, side=lambda j, n=n: gla_side(4 * n + j // 2) if j % 2 else None)
                if n < 4:
                    copy_out(dsts[n][0][:, dsts[n][1] + 2:dsts[n][1] + 4, :].rearrange("p a b -> p (a b)"), g)
                else:
                    copy_out(sbv[:, 1, W * (n - 4):W * (n - 3)], g)

            def stick(i):
                if 1 <= i <= SB_HEADS:
                    k = i - 1
                    s = k % 2
                    dve.wait_ge(zln_done, k + 1)
                    if k >= 2:
                        dve.wait_ge(inc_done, k - 1)
                    dve.scalar_tensor_tensor(out=z_p[:, s, :], in0=z_s[:, s, :], scalar=0.0, in1=z_e[:, s, :],
                                             op0=ALU.max, op1=ALU.add).then_inc(sp_done, 1)
                    dve.wait_ge(sp_done, k + 1)
                    for c in (0, 256):
                        ins = dve.tensor_tensor(z_p[:, s, c:c + P], z_p[:, s, c:c + P], sb_one[:, :], ALU.mult)
                    ins.then_inc(spm_done, 1)
                    if k >= 2:
                        dve.wait_ge(a_done, k - 1)
                    for c in (0, 256):
                        ins = dve.tensor_tensor(z_m[:, s, c:c + P], z_s[:, s, c:c + P], sb_neg[:, :], ALU.add)
                    dve.tensor_copy(z_m[:, s, P:256], z_s[:, s, P:256]).then_inc(zmask_done, 1)
                if 2 <= i < SB_HEADS + 2:
                    k = i - 2
                    dve.wait_ge(inc_done, k + 1)
                    dve.wait_ge(zmask_done, k + 1)
                    dve.tensor_tensor(z_m[:, k % 2, :], z_m[:, k % 2, :], bank[5 + k % 2][:, 0:384], ALU.add).then_inc(t_done, 1)
                if 4 <= i < SB_HEADS + 4:
                    k = i - 4
                    dve.wait_ge(so_done, k + 1)
                    dve.tensor_copy(mix2[:, :, k * P:(k + 1) * P], bank[7][:, 0:256].rearrange("p (b n) -> p b n", b=NB)).then_inc(so_copied, 1)

            for n, name in enumerate(("gla_g", "sgu_u", "sgu_v", "sgu_g")):
                group(GROUP[name][0], side=lambda j, n=n: stick(3 * n + j // 2) if j in (1, 3, 5) else None)

            def sgu_norm():
                a = st(14)
                dve.wait_ge(sgu_sq, 2)
                dve.tensor_scalar(a, a, 1.0 / 512, EPS, ALU.mult, ALU.add).then_inc(sgu_mean, 1)
                dve.wait_ge(sgu_root, 1)
                dve.reciprocal(a, a).then_inc(sgu_rstd, 1)
                dve.wait_ge(sgu_rstd, 1)
                dve.wait_ge(second_loaded, 64)
                for b in range(NB):
                    dve.scalar_tensor_tensor(out=sgu_v[:, b, :], in0=sgu_v[:, b, :], scalar=a[:, b:b + 1], in1=sgu_gain[:, :],
                                             op0=ALU.mult, op1=ALU.mult).then_inc(sgu_vn, 1)

            def sgu_weights():
                dve.wait_ge(sguT_done, 1)
                dve.tensor_tensor(w_sguT[:, :, :], bank[6][:, :].rearrange("p (g t) -> p g t", t=P),
                                  tri[:, :].unsqueeze(1).broadcast_to([P, SGU_GROUPS, P]), ALU.mult).then_inc(sguT_ready, 1)

            def sgu_result():
                dve.wait_ge(sgu_mixed, 2)
                for b in range(NB):
                    for k in range(SGU_GROUPS):
                        dve.scalar_tensor_tensor(out=mix2[:, b, 1536 + k * P:1536 + (k + 1) * P], in0=bank[4 + b][:, k * P:(k + 1) * P],
                                                 scalar=gains[:, BSGU_AT + k:BSGU_AT + k + 1], in1=sgu_u[:, b, k * P:(k + 1) * P],
                                                 op0=ALU.add, op1=ALU.mult).then_inc(sgu_done, 1)

            def tail(j, n):
                if n == 0 and j == 1:
                    sgu_weights()
                    sgu_norm()
                if n == 0 and j == 5:
                    sgu_result()
                if n == 0 and j == 7:
                    head_squares(0)
                if n == 1 and j == 1:
                    mem_mean()
                    head_squares(1)
                if n == 1 and j == 3:
                    mem_rows()

            def mem_mean():
                a = st(6)
                dve.wait_ge(squares, 11)
                dve.tensor_scalar(a, a, 1.0 / D, EPS, ALU.mult, ALU.add).then_inc(mean_ready, 1)

            def mem_rows():
                a = st(6)
                dve.wait_ge(root_ready, 7)
                dve.reciprocal(a, a).then_inc(rstd_ready, 1)
                dve.wait_ge(rstd_ready, 7)
                scale_rows(mem_tok, mem_tok, 6)

            def head_squares(b):
                dve.wait_ge(so_copied, SB_HEADS)
                dve.wait_ge(gla_copied, 2)
                dve.wait_ge(sgu_done, 8)
                if b:
                    dve.wait_ge(hsum_done, 1)
                sq = sbv[:, :, :].rearrange("p a b -> p (a b)")
                dve.tensor_tensor(sq, mix2[:, b, :], mix2[:, b, :], ALU.mult).then_inc(hsq_done, 1)
                dve.wait_ge(hsq_done, b + 1)
                dve.tensor_reduce(stat[:, 128 + 16 * b:144 + 16 * b], sq.rearrange("p (h n) -> p h n", n=P), AX, ALU.add).then_inc(hsum_done, 1)

            for n in range(2):
                group(GROUP["sb_g"][n], side=lambda j, n=n: tail(j, n))
            phase(4)
            hs = stat[:, 128:160]
            dve.wait_ge(hsum_done, 2)
            dve.tensor_scalar(hs, hs, 1.0 / P, EPS, ALU.mult, ALU.add).then_inc(hmean, 1)

            def gated(j):
                if j == 1:
                    dve.wait_ge(hroot, 1)
                    dve.reciprocal(hs, hs).then_inc(hrstd, 1)
                    dve.wait_ge(hrstd, 1)
                if j in (2, 4):
                    b = j // 2 - 1
                    m = mix2[:, b, :].rearrange("p (h n) -> p h n", n=P)
                    dve.tensor_tensor(m, m, stat[:, 128 + 16 * b:144 + 16 * b].unsqueeze(2).broadcast_to([P, 16, P]), ALU.mult).then_inc(hscaled, 1)
                if j in (3, 5):
                    b = j // 2 - 1
                    dve.wait_ge(hscaled, b + 1)
                    dve.wait_ge(banks_free, evacuated(GROUP["sb_g"][1]))
                    dve.tensor_tensor(mix2[:, b, :], mix2[:, b, :], gate[:, b, :], ALU.mult).then_inc(scaled, 1)

            g = GROUP["xk"][0]
            group(g, side=gated)
            copy_out(xkT[:, 2:4, :].rearrange("p a b -> p (a b)"), g)
            g = GROUP["xv"][0]
            group(g)
            copy_out(xv[:, 1, :], g)
            phase(5)

            def onto_x(g, i, step, col):
                for b in range(NB):
                    dst = x_tok[:, b, bass.ds(col, W)] if i is not None else x_tok[:, b, col:col + W]
                    dve.tensor_tensor(dst, out_of(g, b), dst, ALU.add).then_inc(banks_free, 1)

            with dve.Fori(0, 2) as i:
                for e in range(2):
                    g = GROUP["w_out2"][e]
                    group(g, i, 16)
                    onto_x(g, i, 16, i * (2 * W) + e * W)
            dve.wait_ge(sq_first, 16)
            total_squares(7)
            rstd(8, 7, 0, D)
            scale_rows(mem_tok, x_tok, 7)
            phase(6)
            g = GROUP["xq"][0]
            group(g)
            copy_out(mix2[:, 1, 0:W], g)
            for h in range(XA_HEADS):
                dve.wait_ge(xs_done, h + 1)
                dve.tensor_reduce(st(20 + h), bank[4 + h][:, :].rearrange("p (b k) -> p b k", b=NB), AX, ALU.max).then_inc(xmax_done, 1)
                dve.wait_ge(xmax_done, h + 1)
                dve.tensor_scalar(st(20 + h), st(20 + h), -WIDE_SCALE, None, ALU.mult).then_inc(xneg_done, 1)
            for h in range(XA_HEADS):
                dve.wait_ge(xexp_done, 2 * (h + 1))
                dve.reciprocal(st(24 + h), st(24 + h)).then_inc(xrecip_done, 1)
                dve.wait_ge(xrecip_done, h + 1)
                pv = x_p[:, h, :].rearrange("p (b k) -> p b k", b=NB)
                dve.tensor_tensor(pv, pv, broadcast(st(24 + h), [P, NB, S]), ALU.mult).then_inc(xnorm_done, 1)
            for h in range(XA_HEADS):
                dve.wait_ge(xo_hi, h + 1)
                dve.tensor_tensor(hT_lo[:, h, :], bank[4 + h][:, 0:S], hT_hi[:, h, :].bitcast(F32), ALU.subtract).then_inc(xo_lo, 1)
            for e in range(4):
                g = GROUP["xo"][e]
                group(g)
                onto_x(g, None, 0, e * W)
                dve.wait_ge(gain_loaded, 48)
                for b in range(NB):
                    dve.wait_ge(sq_first, 16 + 2 * e + b + 1)
                    dve.tensor_tensor(x_tok[:, b, e * W:(e + 1) * W], x_tok[:, b, e * W:(e + 1) * W], out_gain[:, e * W:(e + 1) * W],
                                      ALU.mult).then_inc(x_gained, 1)
            total_squares(16)
            dve.wait_ge(x_gained, 8)
            rstd(9, 16, 0, D)
            dve.tensor_scalar(mem_tok[:, 1, :], x_tok[:, 1, :], st(16)[:, 1:2], None, ALU.mult).then_inc(out_scaled, 1)

        @block.tensor
        def _(pe):
            def three(o, l_hi, l_lo, r_hi, r_lo, start, stop):
                pe.matmul(o, l_hi, r_hi, start=start, stop=False, skip_group_check=True)
                pe.matmul(o, l_hi, r_lo, start=False, stop=False, skip_group_check=True)
                return pe.matmul(o, l_lo, r_hi, start=False, stop=stop, skip_group_check=True)

            def group(g, mode, i=None, step=0, kcs=(2,) * 8, a_hi=hT_hi, a_lo=hT_lo, first=None, chunks=False, side=None):
                u = FIRST_PIECE[g]
                pair = 2 * (g % 2)
                if g >= 2:
                    pe.wait_ge(banks_free, 2 * (g - 1) + (0 if i is None else i * (4 if step else 0)))
                k = 0
                total = sum(kcs)
                for j, n in enumerate(kcs):
                    s = (u + j) % SLOTS
                    pe.wait_ge(lo_ready, u + j + 1 + (0 if i is None else i * step))
                    hi, lo = wide(w_hi, s, n, W), wide(w_lo, s, n, W)
                    for c in range(n):
                        if first is not None:
                            pe.wait_ge(loT_done, first * KC + max(k + 1, 4))
                        if chunks:
                            pe.wait_ge(g_lo_done, 10 + (k >= 40))
                        if mode == "tok":
                            for b in range(NB):
                                ins = three(bank[pair + b][:, :], a_hi[:, k, b * P:(b + 1) * P], a_lo[:, k, b * P:(b + 1) * P],
                                            hi[:, c, :], lo[:, c, :], k == 0, k == total - 1)
                        else:
                            for ft in range(4):
                                o = bank[pair + ft // 2][:, ft % 2 * S:(ft % 2 + 1) * S]
                                ins = three(o, hi[:, c, ft * P:(ft + 1) * P], lo[:, c, ft * P:(ft + 1) * P],
                                            a_hi[:, k, :], a_lo[:, k, :], k == 0 and ft % 2 == 0, k == total - 1)
                        k += 1
                    ins.then_inc(mm_done, 1)
                    if side:
                        side(j)

            def phase(n, src, ready, more=2):
                g = READER[n]
                for q in range(KC // 2):
                    if q % 4 == 0:
                        pe.wait_ge(scaled, ready + more * (q // 4))
                    if q == 0 and n > 0:
                        pe.wait_ge(banks_free, evacuated(g - 2))
                    if q == 6 and n > 0:
                        pe.wait_ge(banks_free, evacuated(g - 1))
                    for c in (2 * q, 2 * q + 1):
                        for b in range(NB):
                            ins = pe.transpose(bank[pair_bank(n, q)][:, c % 2 * S + b * P:c % 2 * S + (b + 1) * P],
                                               src[:, b, c * P:(c + 1) * P], ident[:, :])
                    ins.then_inc(tr_done, 1)

            pe.wait_ge(ident_ready, 2)
            pe.wait_ge(rows_loaded, 16 * 9)
            pe.transpose(bank[6][:, 0:GAIN_ROWS], gain_rows[:, :], ident[0:GAIN_ROWS, 0:GAIN_ROWS]).then_inc(rows_T, 1)
            pe.wait_ge(tables_ready, 1)
            phase(0, work, 2)

            for j in range(4):
                pe.wait_ge(lo_ready, j + 1)
                hi, lo = wide(w_hi, j, 4, 256), wide(w_lo, j, 4, 256)
                for c in range(4):
                    k = 4 * j + c
                    pe.wait_ge(loT_done, max(k + 1, 4))
                    three(bank[0][:, 0:S], hi[:, c, 0:P], lo[:, c, 0:P], hT_hi[:, k, :], hT_lo[:, k, :], k == 0, k == KC - 1)
                    for b in range(NB):
                        ins = three(bank[1][:, b * P:(b + 1) * P], hT_hi[:, k, b * P:(b + 1) * P], hT_lo[:, k, b * P:(b + 1) * P],
                                    hi[:, c, P:256], lo[:, c, P:256], k == 0 and b == 0, k == KC - 1)
                ins.then_inc(mm_done, 1)
            pe.wait_ge(fr_split_lo, 1)
            for k in range(KC):
                for b in range(NB):
                    ins = three(bank[7][:, b * 16:(b + 1) * 16], hT_hi[:, k, b * P:(b + 1) * P], hT_lo[:, k, b * P:(b + 1) * P],
                                fr_hi[:, k, :], fr_lo[:, k, :], k == 0 and b == 0, k == KC - 1)
            ins.then_inc(fr_done, 1)
            pe.wait_ge(dve_ready, 1)
            pe.wait_ge(pool_ready, 12)

            def forget_sums():
                pe.wait_ge(f_log, 1)
                pe.matmul(bank[6][:, 0:16], tri[:, :], lf[:, 0, :], start=True, stop=True)
                pe.matmul(bank[6][:, 16:32], ones[:, :], lf[:, 0, :], start=True, stop=False)
                pe.matmul(bank[6][:, 16:32], tri[:, :], lf[:, 1, :], start=False, stop=True)
                pe.matmul(bank[7][0:16, 0:128], lf[:, 0, :], tri[:, :], start=True, stop=True)
                pe.matmul(bank[7][0:16, 128:256], lf[:, 0, :], ones[:, :], start=True, stop=False)
                pe.matmul(bank[7][0:16, 128:256], lf[:, 1, :], tri[:, :], start=False, stop=True).then_inc(f_cum, 1)

            def scores(i):
                s, h = i % 2, i % NH
                po = h % 2 * HD
                if i >= 2:
                    pe.wait_ge(biased_done, 2 * (i - 1))
                if i == 0:
                    pe.wait_ge(k_copied, 64)
                    pe.wait_ge(banks_free, evacuated(2))
                if i == NH:
                    pe.wait_ge(f_c, 2)
                    pe.wait_ge(banks_free, evacuated(6))
                if i == NH + 8:
                    pe.wait_ge(banks_free, evacuated(8))
                o = bank[4 + s]
                for b, (lo, hi) in enumerate(((0, 128), (128, 384))):
                    n = hi - lo
                    if i < NH:
                        ins = pe.matmul(o[:, lo:hi], qaT[po:po + HD, h // 2, b * P:(b + 1) * P], ka2[po:po + HD, h // 8, 0:n],
                                        start=True, stop=True)
                    else:
                        pe.matmul(o[:, lo:hi], qbT[po:po + HD, h // 2, b * P:(b + 1) * P], kbT[po:po + HD, h // 2, 0:n],
                                  start=True, stop=False)
                        ins = pe.matmul(o[:, lo:hi], sel[:, h, :], cT8[:, 0:n], start=False, stop=True)
                ins.then_inc(scores_done, 1)

            def turn(i):
                s = i % 2
                pe.wait_ge(exp_done, 3 * (i + 1))
                if i >= 1:
                    pe.wait_ge(probsT_copied, i)
                if i == 0:
                    pe.wait_ge(f_c, 2)
                for c in range(3):
                    ins = pe.transpose(bank[6][:, c * P:(c + 1) * P], probs[:, s, c * P:(c + 1) * P], ident[:, :])
                ins.then_inc(probs_T, 1)

            def values(i):
                s, h = i % 2, i % NH
                pe.wait_ge(probsT_copied, i + 1)
                if i >= 1:
                    pe.wait_ge(out_done, i)

                def v(b):
                    return va[:, b, h // 8 * HD:(h // 8 + 1) * HD] if i < NH else vb[:, b, h * HD:(h + 1) * HD]
                o = bank[7]
                pe.matmul(o[:, 0:HD], probsT[:, s, 0:128], v(0), start=True, stop=True)
                pe.matmul(o[:, HD:P], probsT[:, s, 128:256], v(0), start=True, stop=False)
                pe.matmul(o[:, HD:P], probsT[:, s, 256:384], v(1), start=False, stop=True).then_inc(pv_done, 1)

            def head(i):
                if i < 2 * NH:
                    scores(i)
                if 1 <= i <= 2 * NH:
                    turn(i - 1)
                if 2 <= i < 2 * NH + 2:
                    values(i - 2)

            group(1, "T")
            forget_sums()
            group(2, "T")
            pe.wait_ge(f_c, 2)
            pe.wait_ge(conv_loaded, 32)
            for c in range(4):
                ins = pe.transpose(bank[7][:, c * 2 * FFT:(c + 1) * 2 * FFT], conv_rows[:, c, :], ident[0:2 * FFT, 0:2 * FFT])
            ins.then_inc(conv_T, 1)
            pe.wait_ge(conv_ready, 1)
            for g in (3, 4):
                group(g, "tok", side=lambda j, g=g: head(4 * (g - 3) + j // 2) if j % 2 else None)
            for n, g in enumerate((5, 6, 7, 8)):
                group(g, "T", side=lambda j, n=n: head(8 + 4 * n + j // 2) if j % 2 else None)
            for i in range(24, 2 * NH + 2):
                head(i)
            phase(1, work, 6)
            with pe.Fori(0, 2) as i:
                for e in range(2):
                    group(GROUP["w_out"][e], "tok", i, 16, first=1 if e == 0 else None)
            phase(2, work, 10)
            with pe.Fori(0, 11) as i:
                for e in range(2):
                    group(GROUP["w_up"][e], "T", i, 16, first=2 if e == 0 else None)
            with pe.Fori(0, 2) as i:
                for e in range(2):
                    group(GROUP["w_down"][e], "tok", i, 48, kcs=DOWN, a_hi=g_hi, a_lo=g_lo, chunks=True)
            phase(3, mix2, 14)

            pe.wait_ge(fr_split_lo, 2)
            group(GROUP["gla_qk"][0], "T", first=3)
            for k in range(KC):
                ins = three(bank[4][0:16, 0:S], fr_hi[:, k, :], fr_lo[:, k, :], hT_hi[:, k, :], hT_lo[:, k, :], k == 0, k == KC - 1)
            ins.then_inc(fr_done, 1)

            def gate_mm(j):
                if j == 3:
                    pe.wait_ge(r_copied, 1)
                    pe.wait_ge(second_loaded, 64)
                    for b in range(NB):
                        pe.matmul(bank[5][:, b * S:(b + 1) * S], rT[:, b * P:(b + 1) * P], wgu[:, :], start=True, stop=False)
                        ins = pe.matmul(bank[5][:, b * S:(b + 1) * S], ones[0:1, :], bgg[:, :], start=False, stop=True)
                    ins.then_inc(gate_logits, 1)

            group(GROUP["gla_v"][0], "tok", side=gate_mm)

            def gate_sums():
                pe.wait_ge(ga_log, 1)
                for t in range(2):
                    o = bank[6][:, t * S:(t + 1) * S]
                    pe.matmul(o[:, 0:P], la[:, 0, t * P:(t + 1) * P], tri[:, :], start=True, stop=True)
                    pe.matmul(o[:, P:S], la[:, 0, t * P:(t + 1) * P], ones[:, :], start=True, stop=False)
                    ins = pe.matmul(o[:, P:S], la[:, 1, t * P:(t + 1) * P], tri[:, :], start=False, stop=True)
                ins.then_inc(cum_done, 1)

            def level(n):
                if n < 8:
                    pe.wait_ge(qk_decayed, n + 1)
                    src = qkd
                else:
                    src = gqk
                if n >= 1:
                    pe.wait_ge(level_added, 2 * n)
                for b in range(NB if n else 1):
                    for h in range(GLA_HEADS):
                        po, t = h % 2 * HD, h // 2
                        qb = b if n else 1
                        ins = pe.matmul(bank[4 + 2 * b + h % 2][:, t * P:(t + 1) * P], src[po:po + HD, 1, t, b * P:(b + 1) * P],
                                        src[po:po + HD, 0, t, qb * P:(qb + 1) * P], start=True, stop=True)
                ins.then_inc(level_scores, 1)

            def gla_values():
                pe.wait_ge(level_added, 18)
                pe.wait_ge(b_ready, 1)
                for h in range(GLA_HEADS):
                    c = slice(h * P, (h + 1) * P)
                    a = slice((h % 2 * 2 + h // 2) * P, (h % 2 * 2 + h // 2 + 1) * P)
                    pe.matmul(bank[6][:, c], acc[:, 0, a], gvv[:, 0, c], start=True, stop=True)
                    pe.matmul(bank[7][:, c], inter[:, a], gvv[:, 0, c], start=True, stop=False)
                    ins = pe.matmul(bank[7][:, c], acc[:, 1, a], gvv[:, 1, c], start=False, stop=True)
                ins.then_inc(gla_out, 2)

            def gla_side(n):
                if n == 1:
                    gate_sums()
                if n % 2 and 3 <= n <= 19:
                    level(n // 2 - 1)
                if n == 21:
                    gla_values()

            for n in range(6):
                group(GROUP["sb_q"][0] + n, "T" if n < 4 else "tok",
                      side=lambda j, n=n: gla_side(4 * n + j // 2) if j % 2 else None)

            def stick(i):
                if i < SB_HEADS:
                    if i == 0:
                        pe.wait_ge(gla_copied, 2)
                        pe.wait_ge(banks_free, evacuated(GROUP["sb_k"][1]))
                    if i >= 1:
                        pe.wait_ge(zs_done, i)
                    pe.matmul(bank[4][:, 0:256], sbk[:, i, 0:P], sbq[:, i, :], start=True, stop=True)
                    pe.matmul(bank[4][:, 256:384], sbk[:, i, P:S], sbq[:, i, P:S], start=True, stop=True).then_inc(z_done, 1)
                if 2 <= i < SB_HEADS + 2:
                    k = i - 2
                    r = k % 2
                    pe.wait_ge(spm_done, k + 1)
                    if k >= 2:
                        pe.wait_ge(t_done, k - 1)
                    pe.matmul(bank[5 + r][:, 0:384], tri_neg[:, :], z_p[:, r, :], start=True, stop=False, skip_group_check=True)
                    pe.matmul(bank[5 + r][:, P:256], ones_neg[:, :], z_p[:, r, 256:384], start=False, stop=True,
                              skip_group_check=True).then_inc(inc_done, 1)
                if 4 <= i < SB_HEADS + 4:
                    k = i - 4
                    r = k % 2
                    pe.wait_ge(a_done, k + 1)
                    if k >= 1:
                        pe.wait_ge(so_copied, k)
                    if k == 0:
                        pe.wait_ge(banks_free, evacuated(GROUP["sb_v"][1]))
                    c = slice(k * P, (k + 1) * P)
                    pe.matmul(bank[7][:, 0:P], z_a[:, r, 0:P], sbv[:, 0, c], start=True, stop=True)
                    pe.matmul(bank[7][:, P:256], z_a[:, r, P:256], sbv[:, 0, c], start=True, stop=False)
                    pe.matmul(bank[7][:, P:256], z_a[:, r, 256:384], sbv[:, 1, c], start=False, stop=True).then_inc(so_done, 1)

            for n, name in enumerate(("gla_g", "sgu_u", "sgu_v", "sgu_g")):
                group(GROUP[name][0], "tok", side=lambda j, n=n: stick(3 * n + j // 2) if j in (1, 3, 5) else None)

            def tail(j, n):
                if n == 0 and j == 0:
                    pe.wait_ge(t_done, SB_HEADS)
                    for k in range(SGU_GROUPS):
                        ins = pe.transpose(bank[6][:, k * P:(k + 1) * P], w_sgu[:, k, :], ident[:, :])
                    ins.then_inc(sguT_done, 1)
                if n == 0 and j == 4:
                    pe.wait_ge(sguT_ready, 1)
                    pe.wait_ge(sgu_vn, 2)
                    for b in range(NB):
                        for k in range(SGU_GROUPS):
                            ins = pe.matmul(bank[4 + b][:, k * P:(k + 1) * P], w_sguT[:, k, :], sgu_v[:, b, k * P:(k + 1) * P],
                                            start=True, stop=True)
                    ins.then_inc(sgu_mixed, 2)

            for n in range(2):
                group(GROUP["sb_g"][n], "tok", side=lambda j, n=n: tail(j, n))
            pe.wait_ge(sgu_done, 8)
            phase(4, mem_tok, 18)
            group(GROUP["xk"][0], "T", first=4)
            group(GROUP["xv"][0], "tok")
            phase(5, mix2, 22, 0)
            with pe.Fori(0, 2) as i:
                for e in range(2):
                    group(GROUP["w_out2"][e], "tok", i, 16, first=5 if e == 0 else None)
            phase(6, mem_tok, 24)
            group(GROUP["xq"][0], "T", first=6)
            pe.wait_ge(banks_free, evacuated(GROUP["xq"][0]))
            for h in range(XA_HEADS):
                for b in range(NB):
                    ins = pe.matmul(bank[4 + h][:, b * S:(b + 1) * S], mix2[:, h // 2, h % 2 * S + b * P:h % 2 * S + (b + 1) * P],
                                    xkT[:, h, :], start=True, stop=True)
                ins.then_inc(xs_done, 1)
            for h in range(XA_HEADS):
                pe.wait_ge(xnorm_done, h + 1)
                for k in range(2):
                    for b in range(NB):
                        ins = pe.transpose(bank[4 + h][:, k * S + b * P:k * S + (b + 1) * P], x_p[:, h, b * S + k * P:b * S + (k + 1) * P], ident[:, :])
                ins.then_inc(xpT_done, 1)
            for h in range(XA_HEADS):
                pe.wait_ge(xpT_copied, h + 1)
                for k in range(2):
                    ins = pe.matmul(bank[4 + h][:, 0:S], xv[:, k, h * P:(h + 1) * P], x_pT[:, h % 2, k * S:(k + 1) * S],
                                    start=(k == 0), stop=(k == 1))
                ins.then_inc(xo_done, 1)
            pe.wait_ge(xo_lo, XA_HEADS)
            for e in range(4):
                group(GROUP["xo"][e], "tok", kcs=(2, 2))


_INS = ['x', 'pre_mix_g', 'w_in', 'b_forget', 'sinks', 'grp_swa_g', 'grp_fox_g', 'w_out', 'post_mix_g', 'pre_ffn_g',
        'w_up', 'conv_w', 'conv_b', 'w_down', 'post_ffn_g', 'mem_2', 'norm_mix_2', 'w_in_2', 'w_gla_gate_up_2',
        'b_gla_gate_2', 'sgu_norm_2', 'w_sgu_2', 'b_sgu_2', 'out_norm_2', 'w_out_2', 'norm_xattn_2', 'norm_mem_2',
        'w_xq_2', 'w_xkv_2', 'w_xo_2', 'final_norm_2']


def kernel(**inputs):
    import numpy as np
    import concourse.bacc as bacc
    from concourse.bass_utils import run_bass_kernel_spmd

    nc = bacc.Bacc("TRN2", target_bir_lowering=False, num_devices=1)
    arrays, aps = {}, {}
    for name in _INS:
        a = np.ascontiguousarray(inputs[name])
        arrays[f"in_{name}"] = a
        aps[name] = nc.dram_tensor(f"in_{name}", a.shape, mybir.dt.from_np(a.dtype), kind="ExternalInput").ap()
    out = nc.dram_tensor("out_0", (1, S, D), F32, kind="ExternalOutput").ap()
    build(nc, aps, out)
    r = run_bass_kernel_spmd(nc, [arrays], core_ids=[0])
    return r.results[0]["out_0"]
```

```python
from contextlib import ExitStack

import concourse.bass as bass
from concourse import mybir

F32 = mybir.dt.float32
F32R = mybir.dt.float32r
BF16 = mybir.dt.bfloat16
I32 = mybir.dt.int32
ALU = mybir.AluOpType
ACT = mybir.ActivationFunctionType
AX = mybir.AxisListType.X

P = 128
S = 256
NB = S // P
D = 2048
KC = D // P
EPS = 1e-6
BIG = 1e30

HD = 64
NH = 16
D_SWA = NH * HD
WINDOW = 128
D_FF = 5632
FFT = D_FF // P
QA, KA, VA, QB, KB, VB, FB = 0, 1024, 1152, 1280, 2304, 3328, 4352
SBQ, SBK, SBV, SBG = 0, 1024, 2048, 3072
GLQ, GLV, GLR, GLG = 4096, 4608, 5120, 5136
SGUU, SGUV, SGUG = 5648, 6160, 6672
SB_HEADS = 8
GLA_HEADS = 4
GATE_RANK = 16
GATE_TAU = 16.0
SGU_GROUPS = 4
XA_HEADS = 4
WIDE_SCALE = 128 ** -0.5

W = 512
PIECE = 1024
SLOTS = 4

PLAN = (
    [("kv_a", 4), ("q_a", 8), ("q_a", 8), ("v_b", 8), ("v_b", 8), ("q_b", 8), ("k_b", 8), ("q_b", 8), ("k_b", 8)]
    + [("w_out", 8)] * 4 + [("w_up", 8)] * 22 + [("w_down", 24)] * 4
    + [("gla_qk", 8), ("gla_v", 8)] + [("sb_q", 8)] * 2 + [("sb_k", 8)] * 2 + [("sb_v", 8)] * 2
    + [("gla_g", 8), ("sgu_u", 8), ("sgu_v", 8), ("sgu_g", 8)] + [("sb_g", 8)] * 2
    + [("xk", 8), ("xv", 8)] + [("w_out2", 8)] * 4 + [("xq", 8)] + [("xo", 2)] * 4
)
FIRST_PIECE = [sum(n for _, n in PLAN[:g]) for g in range(len(PLAN) + 1)]
GROUP = {}
for _g, (_name, _n) in enumerate(PLAN):
    GROUP.setdefault(_name, []).append(_g)
TOTAL = FIRST_PIECE[-1]
DOWN = [2] * 20 + [1] * 4

GAINS = ["pre_mix", "grp", "pre_ffn", "norm_mix_2", "out_norm_2", "norm_mem_2", "norm_xattn_2"]
GAIN_AT = {n: i * KC for i, n in enumerate(GAINS)}
BSGU_AT = KC * len(GAINS)
GAIN_ROWS = BSGU_AT + SGU_GROUPS
PHASES = ["pre_mix", "grp", "pre_ffn", "norm_mix_2", "norm_mem_2", "out_norm_2", "norm_xattn_2"]
READER = [GROUP[n][0] for n in ("kv_a", "w_out", "w_up", "gla_qk", "xk", "w_out2", "xq")]


def pair_bank(n, q):
    p = 2 * (READER[n] % 2)
    return [p, p + 1, 4, 5, 6, 7, 2 - p, 3 - p][q]


def build(nc, A, out):
    with ExitStack() as ctx:
        def sem(name):
            return ctx.enter_context(nc.semaphore(name))

        def region(specs):
            with ExitStack() as scope:
                return [scope.enter_context(nc.sbuf_tensor(n, shape, dt)) for n, shape, dt in specs]

        def keep(name, shape, dt=F32):
            return ctx.enter_context(nc.sbuf_tensor(name, shape, dt))

        x_tok = keep("x_tok", [P, NB, D])
        raw = keep("raw", [P, SLOTS, PIECE])
        w_hi = keep("w_hi", [P, SLOTS, PIECE], F32R)
        w_lo = keep("w_lo", [P, SLOTS, PIECE], F32R)
        ident = keep("ident", [P, P])
        tri = keep("tri", [P, P])
        ones = keep("ones", [P, P])
        gains = keep("gains", [P, GAIN_ROWS])
        conv = keep("conv", [P, 4, 2 * FFT])
        fr_raw = keep("fr_raw", [P, KC, 16])
        fr_hi = keep("fr_hi", [P, KC, 16], F32R)
        fr_lo = keep("fr_lo", [P, KC, 16], F32R)
        stat = keep("stat", [P, 4 * 64])

        idle = keep("idle", [P, S], BF16)
        part_sq = keep("part_sq", [P, NB, 8])

        hT_hi, hT_lo = region([("hT_hi", [P, KC, S], F32R), ("hT_lo", [P, KC, S], F32R)])
        y_tok, ffn_gain = region([("y_tok", [P, NB, D], F32), ("ffn_gain", [P, D], F32)])
        hold = ctx.enter_context(nc.sbuf_tensor("h_place", [P, 2 * KC * S], F32))

        (work, mix_gain, qaT, kaT, ka2, va, qbT, kbT, vb, eye2, eye_f, distm, foxm, probs, probsT, biased, sink, sink8,
         bf, fz, fm, fa, lf2, c8, cT2, gain_rows, conv_rows, junk, junk_d) = region([
             ("work", [P, NB, D], F32), ("mix_gain", [P, D], F32), ("qaT", [P, 8, S], F32), ("kaT", [P, S], F32),
             ("ka2", [P, 2, S], F32), ("va", [P, NB, P], F32), ("qbT", [P, 8, S], F32), ("kbT", [P, 8, S], F32),
             ("vb", [P, NB, 1024], F32), ("eye2", [P, NH], F32R), ("eye_f", [P, NH], F32), ("distm", [P, 384], F32), ("foxm", [P, 384], F32),
             ("probs", [P, 3, 384], F32), ("probsT", [P, 2, 384], F32), ("biased", [P, 2, 384], F32),
             ("sink", [P, NH], F32), ("sink8", [P, NH], F32), ("bf", [16, 1], F32), ("fz", [16, S], F32),
             ("fm", [16, S], F32), ("fa", [16, S], F32), ("lf2", [P, NB, P], F32), ("c8", [P, NB, 16], F32),
             ("cT2", [P, S], F32R), ("gain_rows", [GAIN_ROWS, P], F32), ("conv_rows", [2 * FFT, 4, P], F32),
             ("junk", [P, 2048], BF16), ("junk_d", [P, 2048], BF16)])
        g_hi, g_lo, cv_gate, cv_val, coef = region([
            ("g_hi", [P, FFT, S], F32R), ("g_lo", [P, FFT, S], F32R), ("cv_gate", [P, 4, S], F32),
            ("cv_val", [P, 4, S], F32), ("coef", [P, 2, 4, 4], F32)])
        with ExitStack() as scope:
            def loc(name, shape, dt=F32):
                return scope.enter_context(nc.sbuf_tensor(name, shape, dt))
            mix2 = loc("mix2", [P, NB, D])
            with ExitStack() as inner:
                def part(name, shape, dt=F32):
                    return inner.enter_context(nc.sbuf_tensor(name, shape, dt))
                gqk = part("gqk", [P, 2, 2, S])
                gvv = part("gvv", [P, NB, 512])
                la = part("la", [P, NB, S])
                bT = part("bT", [P, 2, S])
            with ExitStack() as inner:
                x_p = inner.enter_context(nc.sbuf_tensor("x_p", [P, XA_HEADS, 512], F32))
                x_pT = inner.enter_context(nc.sbuf_tensor("x_pT", [P, 2, 512], F32))
            gate = loc("gate", [P, NB, D])
            with ExitStack() as inner:
                sbq = inner.enter_context(nc.sbuf_tensor("sbq", [P, 8, S], F32))
                sbk = inner.enter_context(nc.sbuf_tensor("sbk", [P, 8, S], F32))
            mem_tok = loc("mem_tok", [P, NB, D])
            sbv = loc("sbv", [P, NB, 1024])
            xkT = loc("xkT", [P, XA_HEADS, S])
            xv = loc("xv", [P, NB, 512])
            with ExitStack() as inner:
                xor_s = inner.enter_context(nc.sbuf_tensor("xor_s", [P, P], I32))
                xor_t = inner.enter_context(nc.sbuf_tensor("xor_t", [P, P], I32))
                lev = inner.enter_context(nc.sbuf_tensor("lev", [P, P], F32))
            sgu_u = loc("sgu_u", [P, NB, 512])
            sgu_v = loc("sgu_v", [P, NB, 512])
            sgu_gain = loc("sgu_gain", [P, 512])
            w_sgu = loc("w_sgu", [P, SGU_GROUPS, P])
            w_sguT = loc("w_sguT", [P, SGU_GROUPS, P])
            sb_neg = loc("sb_neg", [P, P])
            sb_one = loc("sb_one", [P, P])
            tri_neg = loc("tri_neg", [P, P])
            ones_neg = loc("ones_neg", [P, P])
            with ExitStack() as inner:
                def part(name, shape, dt=F32):
                    return inner.enter_context(nc.sbuf_tensor(name, shape, dt))
                rT = part("rT", [16, S])
                wgu = part("wgu", [16, S])
                bgg = part("bgg", [1, S])
                decay = part("decay", [P, 2, 2 * S])
                qkd = part("qkd", [P, 2, 2, S])
                acc = part("acc", [P, NB, 512])
                inter = part("inter", [P, 512])
                prod = part("prod", [P, 512])
                levels = part("levels", [P, 8, P])
            with ExitStack() as inner:
                def part(name, shape, dt=F32):
                    return inner.enter_context(nc.sbuf_tensor(name, shape, dt))
                z_s = part("z_s", [P, 2, 384])
                z_m = part("z_m", [P, 2, 384])
                z_e = part("z_e", [P, 2, 384])
                z_p = part("z_p", [P, 2, 384])
                z_a = part("z_a", [P, 2, 384])
            with ExitStack() as inner:
                def part(name, shape, dt=F32):
                    return inner.enter_context(nc.sbuf_tensor(name, shape, dt))
                out_gain = part("out_gain", [P, D])
                junk2 = part("junk2", [P, 2048], BF16)
                junk2_d = part("junk2_d", [P, 2048], BF16)

        bank = [ctx.enter_context(nc.psum_tensor(f"bank{i}", [P, 512], F32)) for i in range(4)]
        upper = ctx.enter_context(nc.psum_tensor("upper", [P, 4, 512], F32))
        bank += [upper[:, i, :] for i in range(4)]

        raw_loaded = [sem(f"raw_loaded{i}") for i in range(SLOTS)]
        hi_ready, lo_ready, mm_done = sem("hi_ready"), sem("lo_ready"), sem("mm_done")
        banks_free = sem("banks_free")
        x_loaded = [sem("x_loaded0"), sem("x_loaded1")]
        rows_loaded, consts_loaded = sem("rows_loaded"), sem("consts_loaded")
        conv_loaded, conv_T, conv_ready = sem("conv_loaded"), sem("conv_T"), sem("conv_ready")
        fr_loaded, fr_split_hi, fr_split_lo, fr_done = sem("fr_loaded"), sem("fr_split_hi"), sem("fr_split_lo"), sem("fr_done")
        ident_ready, pool_ready, dve_ready = sem("ident_ready"), sem("pool_ready"), sem("dve_ready")
        rows_T, tables_ready, first_row = sem("rows_T"), sem("tables_ready"), sem("first_row")
        va_T, va_ready, lf_T, lf_ready, lf_cleared = [sem(n) for n in ("va_T", "va_ready", "lf_T", "lf_ready", "lf_cleared")]
        squares, mean_ready, root_ready, rstd_ready, scaled = (
            sem("squares"), sem("mean_ready"), sem("root_ready"), sem("rstd_ready"), sem("scaled"))
        squares_d, scaled_act, idle_ready = sem("squares_d"), sem("scaled_act"), sem("idle_ready")
        tr_done, hiT_done, loT_done = sem("tr_done"), sem("hiT_done"), sem("loT_done")
        k_copied = sem("k_copied")
        f_z, f_abs, f_exp, f_ln, f_min, f_log, f_cum, f_c = [sem("f_" + n) for n in ("z", "abs", "exp", "ln", "min", "log", "cum", "c")]
        scores_done, biased_done, row_max, neg_max, exp_done, den_done, recip_done, probs_T, probsT_copied, pv_done, out_done = [
            sem(n) for n in ("scores_done", "biased_done", "row_max", "neg_max", "exp_done", "den_done", "recip_done",
                             "probs_T", "probsT_copied", "pv_done", "out_done")]
        gain_loaded, y_scaled, x_added = sem("gain_loaded"), sem("y_scaled"), sem("x_added")
        sq_first, mul_first, sums_ready = sem("sq_first"), sem("mul_first"), sem("sums_ready")
        coef_ready, conv_tap2, conv_tap1, gelu_done, glu_done, g_hi_done, g_lo_done = [
            sem(n) for n in ("coef_ready", "conv_tap2", "conv_tap1", "gelu_done", "glu_done", "g_hi_done", "g_lo_done")]
        second_loaded, second_pool, second_dve = sem("second_loaded"), sem("second_pool"), sem("second_dve")
        r_copied, gate_logits, ga_abs, ga_exp, ga_ln, ga_log, cum_done, b_ready = [
            sem(n) for n in ("r_copied", "gate_logits", "ga_abs", "ga_exp", "ga_ln", "ga_log", "cum_done", "b_ready")]
        cleared, rel_ready, decayed, qk_decayed, level_scores, level_added, gla_out, gla_copied = [
            sem(n) for n in ("cleared", "rel_ready", "decayed", "qk_decayed", "level_scores", "level_added", "gla_out", "gla_copied")]
        z_done, zs_done, zabs_done, zexp_done, zln_done, zmask_done, zmax_done, sp_done, spm_done, inc_done, t_done, a_done, so_done, so_copied = [
            sem(n) for n in ("z_done", "zs_done", "zabs_done", "zexp_done", "zln_done", "zmask_done", "zmax_done", "sp_done",
                             "spm_done", "inc_done", "t_done", "a_done", "so_done", "so_copied")]
        sgu_sq, sgu_mean, sgu_root, sgu_rstd, sgu_vn, sguT_done, sguT_ready, sgu_mixed, sgu_done = [
            sem(n) for n in ("sgu_sq", "sgu_mean", "sgu_root", "sgu_rstd", "sgu_vn", "sguT_done", "sguT_ready", "sgu_mixed", "sgu_done")]
        mem_loaded, hsq_done, hsum_done, hmean, hroot, hrstd, hscaled, hgated = [
            sem(n) for n in ("mem_loaded", "hsq_done", "hsum_done", "hmean", "hroot", "hrstd", "hscaled", "hgated")]
        xs_done, xmax_done, xneg_done, xexp_done, xrecip_done, xnorm_done, xpT_done, xpT_copied, xo_done, xo_hi, xo_lo = [
            sem(n) for n in ("xs_done", "xmax_done", "xneg_done", "xexp_done", "xrecip_done", "xnorm_done", "xpT_done",
                             "xpT_copied", "xo_done", "xo_hi", "xo_lo")]
        out_scaled0, out_scaled, stored, x_gained = sem("out_scaled0"), sem("out_scaled"), sem("stored"), sem("x_gained")

        def st(k, n=2):
            return stat[:, 4 * k:4 * k + n]

        def head_factor(b, c):
            return stat[:, 4 + 2 * b + c // 2:5 + 2 * b + c // 2]

        def wide(t, s, kcs, w):
            return t[:, s, 0:kcs * w].rearrange("p (k n) -> p k n", k=kcs)

        def broadcast(ap, shape):
            return ap.unsqueeze(2).broadcast_to(shape)

        def evacuated(g, off=0):
            return 2 * (g + 1) + off

        def piece_size(u):
            g = max(i for i in range(len(PLAN)) if FIRST_PIECE[i] <= u)
            return P * 4 if PLAN[g][0] == "w_down" and u - FIRST_PIECE[g] >= 20 else PIECE

        block = ctx.enter_context(nc.Block())

        @block.sync
        def _(sp):
            def load(src, row, kcs, col, w, u, i=None, step=0):
                s = u % SLOTS
                if u >= SLOTS:
                    sp.wait_ge(lo_ready, u - SLOTS + 1 + (0 if i is None else i * step))
                rows = src[row:row + kcs * P]
                cols = rows[:, col:col + w] if i is None or isinstance(col, int) else rows[:, bass.ds(col, w)]
                sp.dma_start(wide(raw, s, kcs, w), cols.rearrange("(k p) n -> p k n", p=P)).then_inc(raw_loaded[s], 16)

            def group(src, col, g, i=None, step=0, pieces=(2,) * 8, w=W):
                row = 0
                for j, kcs in enumerate(pieces):
                    load(src, row, kcs, col, w, FIRST_PIECE[g] + j, i, step)
                    row += kcs * P

            w_in = A["w_in"][0]
            xr = A["x"][0].rearrange("(b p) d -> b p d", p=P)
            for b in range(NB):
                sp.dma_start(x_tok[:, b, :], xr[b]).then_inc(x_loaded[b], 16)
            group(w_in, KA, 0, pieces=(4,) * 4, w=256)
            sp.dma_start(fr_raw[:, :, :], w_in[:, FB:FB + 16].rearrange("(k p) n -> p k n", p=P)).then_inc(fr_loaded, 16)
            def gain(name, lo, n, src):
                r = GAIN_AT[name] + lo
                sp.dma_start(gain_rows[r:r + n, :], src[0].rearrange("(k p) -> k p", p=P)).then_inc(rows_loaded, 16)
            gain("grp", 0, 8, A["grp_swa_g"])
            gain("grp", 8, 8, A["grp_fox_g"])
            gain("pre_ffn", 0, 16, A["pre_ffn_g"])
            gain("norm_mix_2", 0, 16, A["norm_mix_2"])
            gain("out_norm_2", 0, 16, A["out_norm_2"])
            gain("norm_mem_2", 0, 16, A["norm_mem_2"])
            gain("norm_xattn_2", 0, 16, A["norm_xattn_2"])
            sp.dma_start(gain_rows[BSGU_AT:BSGU_AT + SGU_GROUPS, :], A["b_sgu_2"][0]).then_inc(rows_loaded, 16)
            for g, col in enumerate([QA, QA + W, VB, VB + W, QB, KB, QB + W, KB + W], 1):
                group(w_in, col, g)
            with sp.Fori(0, 2) as i:
                for e in range(2):
                    group(A["w_out"][0], i * (2 * W) + e * W, GROUP["w_out"][e], i, 16)
            with sp.Fori(0, 11) as i:
                for e in range(2):
                    group(A["w_up"][0], i * W + e * D_FF, GROUP["w_up"][e], i, 16)
            with sp.Fori(0, 2) as i:
                for e in range(2):
                    group(A["w_down"][0], i * (2 * W) + e * W, GROUP["w_down"][e], i, 48, pieces=DOWN)
            w_in2 = A["w_in_2"][0]
            sp.wait_ge(fr_split_lo, 1)
            sp.dma_start(fr_raw[:, :, :], w_in2[:, GLR:GLR + 16].rearrange("(k p) n -> p k n", p=P)).then_inc(fr_loaded, 16)
            group(w_in2, GLQ, GROUP["gla_qk"][0])
            group(w_in2, GLV, GROUP["gla_v"][0])
            with sp.Fori(0, 3) as i:
                for e in range(2):
                    group(w_in2, i * (2 * W) + e * W, GROUP["sb_q"][e], i, 16)
            for n, col in (("gla_g", GLG), ("sgu_u", SGUU), ("sgu_v", SGUV), ("sgu_g", SGUG)):
                group(w_in2, col, GROUP[n][0])
            sp.wait_ge(z_done, SB_HEADS)
            mr = A["mem_2"][0].rearrange("(b p) d -> b p d", p=P)
            for b in range(NB):
                sp.dma_start(mem_tok[:, b, :], mr[b]).then_inc(mem_loaded, 16)
            for e in range(2):
                group(w_in2, SBG + e * W, GROUP["sb_g"][e])
            group(A["w_xkv_2"][0], 0, GROUP["xk"][0])
            group(A["w_xkv_2"][0], W, GROUP["xv"][0])
            with sp.Fori(0, 2) as i:
                for e in range(2):
                    group(A["w_out_2"][0], i * (2 * W) + e * W, GROUP["w_out2"][e], i, 16)
            group(A["w_xq_2"][0], 0, GROUP["xq"][0])
            for e in range(4):
                group(A["w_xo_2"][0], e * W, GROUP["xo"][e], pieces=(2, 2))
            orr = out[0].rearrange("(b p) d -> b p d", p=P)
            for c in range(2):
                for b in (1, 0):
                    sp.wait_ge(out_scaled if b else out_scaled0, c + 1)
                    cols = slice(c * D // 2, (c + 1) * D // 2)
                    sp.dma_start(orr[b][:, cols], mem_tok[:, b, cols]).then_inc(stored, 16)
            sp.wait_ge(stored, 16 * 2 * NB)

        @block.gpsimd
        def _(pool):
            pool.memset(ident[:, :], 0.0).then_inc(ident_ready, 1)
            pool.wait_ge(ident_ready, 1)
            pool.affine_select(out=ident[:, :], in_=ident[:, :], compare_op=ALU.not_equal, fill=1.0, base=0,
                               pattern=[[-1, P]], channel_multiplier=1).then_inc(ident_ready, 1)
            pool.memset(tri[:, :], 1.0).then_inc(pool_ready, 1)
            pool.memset(foxm[:, :], 0.0).then_inc(pool_ready, 1)
            pool.memset(eye_f[:, :], 0.0).then_inc(pool_ready, 1)
            pool.iota(distm[:, 0:128], [[-1, 128]], base=0, channel_multiplier=1, allow_small_or_imprecise_dtypes=True).then_inc(pool_ready, 1)
            pool.iota(distm[:, 128:384], [[-1, 256]], base=128, channel_multiplier=1, allow_small_or_imprecise_dtypes=True).then_inc(pool_ready, 1)
            pool.wait_ge(x_loaded[0], 16)
            pool.wait_ge(x_loaded[1], 16)
            pool.dma_start(conv_rows[:, 0:3, :], A["conv_w"][0].rearrange("c (t p) -> t c p", p=P)).then_inc(conv_loaded, 16)
            pool.dma_start(conv_rows[:, 3, :], A["conv_b"][0].rearrange("(t p) -> t p", p=P)).then_inc(conv_loaded, 16)
            pool.dma_start(sink[:, :], A["sinks"][0].partition_broadcast(P)).then_inc(consts_loaded, 16)
            pool.dma_start(bf[:, :], A["b_forget"][0].rearrange("(h a) -> h a", a=1)).then_inc(consts_loaded, 16)
            pool.wait_ge(pool_ready, 5)
            pool.affine_select(out=tri[:, :], in_=tri[:, :], compare_op=ALU.is_ge, fill=0.0, base=0,
                               pattern=[[1, P]], channel_multiplier=-1).then_inc(pool_ready, 1)
            pool.affine_select(out=eye_f[:, :], in_=eye_f[:, :], compare_op=ALU.not_equal, fill=1.0, base=0,
                               pattern=[[-1, NH]], channel_multiplier=1).then_inc(pool_ready, 1)
            for t, fill in ((distm, BIG), (foxm, -BIG)):
                pool.affine_select(out=t[:, 0:128], in_=t[:, 0:128], compare_op=ALU.is_ge, fill=fill, base=0,
                                   pattern=[[-1, 128]], channel_multiplier=1).then_inc(pool_ready, 1)
                pool.affine_select(out=t[:, 128:384], in_=t[:, 128:384], compare_op=ALU.is_ge, fill=fill, base=128,
                                   pattern=[[-1, 256]], channel_multiplier=1).then_inc(pool_ready, 1)
            pool.wait_ge(pool_ready, 11)
            pool.affine_select(out=eye_f[:, :], in_=eye_f[:, :], compare_op=ALU.not_equal, fill=1.0, base=-32,
                               pattern=[[-1, NH]], channel_multiplier=1).then_inc(pool_ready, 1)
            pool.affine_select(out=distm[:, 128:384], in_=distm[:, 128:384], compare_op=ALU.is_ge, fill=BIG,
                               base=WINDOW - 1 - 128, pattern=[[1, 256]], channel_multiplier=-1).then_inc(pool_ready, 1)
            pool.wait_ge(banks_free, evacuated(0))
            for kv in range(2):
                for half in range(2):
                    pool.dma_start(ka2[half * HD:(half + 1) * HD, kv, :], kaT[kv * HD:(kv + 1) * HD, :]).then_inc(k_copied, 16)
            pool.dma_start(mix_gain[:, :], A["post_mix_g"][0].partition_broadcast(P)).then_inc(gain_loaded, 16)
            pool.wait_ge(mm_done, FIRST_PIECE[GROUP["w_down"][0]])
            pool.dma_start(ffn_gain[:, :], A["post_ffn_g"][0].partition_broadcast(P)).then_inc(gain_loaded, 16)
            pool.wait_ge(mm_done, FIRST_PIECE[GROUP["gla_qk"][0]])
            pool.dma_start(wgu[:, :], A["w_gla_gate_up_2"][0]).then_inc(second_loaded, 16)
            pool.dma_start(bgg[:, :], A["b_gla_gate_2"][0].rearrange("(a n) -> a n", a=1)).then_inc(second_loaded, 16)
            pool.dma_start(sgu_gain[:, :], A["sgu_norm_2"][0].partition_broadcast(P)).then_inc(second_loaded, 16)
            pool.dma_start(w_sgu[:, :, :], A["w_sgu_2"][0].rearrange("g t s -> t g s")).then_inc(second_loaded, 16)
            pool.iota(xor_s[:, :], [[0, P]], base=0, channel_multiplier=1).then_inc(second_pool, 1)
            pool.iota(xor_t[:, :], [[1, P]], base=0, channel_multiplier=0).then_inc(second_pool, 1)
            pool.memset(sb_neg[:, :], 0.0).then_inc(second_pool, 1)
            pool.memset(sb_one[:, :], 1.0).then_inc(second_pool, 1)
            pool.memset(tri_neg[:, :], -1.0).then_inc(second_pool, 1)
            pool.memset(ones_neg[:, :], -1.0).then_inc(second_pool, 1)
            pool.wait_ge(second_pool, 6)
            pool.affine_select(out=sb_neg[:, :], in_=sb_neg[:, :], compare_op=ALU.is_gt, fill=-BIG, base=0,
                               pattern=[[1, P]], channel_multiplier=-1).then_inc(second_pool, 1)
            pool.affine_select(out=sb_one[:, :], in_=sb_one[:, :], compare_op=ALU.is_gt, fill=0.0, base=0,
                               pattern=[[1, P]], channel_multiplier=-1).then_inc(second_pool, 1)
            pool.affine_select(out=tri_neg[:, :], in_=tri_neg[:, :], compare_op=ALU.is_ge, fill=0.0, base=0,
                               pattern=[[-1, P]], channel_multiplier=1).then_inc(second_pool, 1)
            pool.wait_ge(so_copied, SB_HEADS)
            pool.dma_start(out_gain[:, :], A["final_norm_2"].partition_broadcast(P)).then_inc(gain_loaded, 16)

        @block.scalar
        def _(act):
            def split(u, i=None, step=0, n=None):
                if u >= TOTAL:
                    return
                s = u % SLOTS
                n = n or piece_size(u)
                act.wait_ge(raw_loaded[s], 16 * (u // SLOTS + 1) + (0 if i is None else i * (16 * step // SLOTS)))
                if u >= SLOTS:
                    act.wait_ge(mm_done, u - SLOTS + 1 + (0 if i is None else i * step))
                act.activation(w_hi[:, s, 0:n], raw[:, s, 0:n], ACT.Copy).then_inc(hi_ready, 1)

            def group(g, i=None, step=0, side=None, take=None):
                u, n = FIRST_PIECE[g], PLAN[g][1]
                for j in range(n):
                    split(u + j + SLOTS - 1, i, step)
                    if side and j:
                        side(j - 1)
                if side and not take:
                    side(n - 1)
                act.wait_ge(mm_done, FIRST_PIECE[g + 1] + (0 if i is None else i * step))
                if take:
                    take()
                if side and take:
                    side(n - 1)

            def out_of(g, b):
                return bank[2 * (g % 2) + b][:, :]

            def copy_out(dst, g, b=0, func=ACT.Copy):
                act.activation(dst, out_of(g, b), func).then_inc(banks_free, 1)

            def warm(k, func):
                act.wait_ge(dve_ready, 1)
                act.activation(stat[:, 240 + k:241 + k], ones[:, 0:1], func)

            def phase(n, side=None):
                at = GAIN_AT[PHASES[n]]
                if n == 0:
                    act.wait_ge(tables_ready, 1)
                for c in range(KC):
                    if side and c % 4 == 0 and c // 4 < SLOTS - 1:
                        side(c // 4)
                    if c % 2 == 0:
                        act.wait_ge(tr_done, (KC * n + c) // 2 + 1)
                    ins = act.activation(hT_hi[:, c, :], bank[pair_bank(n, c // 2)][:, c % 2 * S:(c % 2 + 1) * S], ACT.Copy,
                                         scale=gains[:, at + c:at + c + 1])
                    if c % 2:
                        ins.then_inc(hiT_done, 1)

            def scale_part(dst, src, n, factor):
                act.wait_ge(rstd_ready, n)
                for b in range(NB):
                    act.activation(dst[:, b, 3 * W:D], src[:, b, 3 * W:D], ACT.Copy, scale=factor(b, 3)).then_inc(scaled_act, 1)

            n_squares = [0]

            def square(src, col, done, jk):
                if done is squares:
                    if n_squares[0]:
                        act.wait_ge(squares, n_squares[0])
                    n_squares[0] += 1
                act.activation(jk, src, ACT.Square, accum_out=col).then_inc(done, 1)

            def root(n, k, wait, done, width=2):
                act.wait_ge(wait, n)
                act.activation(stat[:, 4 * k:4 * k + width], stat[:, 4 * k:4 * k + width], ACT.Sqrt).then_inc(done, 1)

            act.dma_start(gain_rows[0:KC, :], A["pre_mix_g"][0].rearrange("(k p) -> k p", p=P)).then_inc(first_row, 16)
            warm(0, ACT.Sqrt)
            act.wait_ge(x_loaded[0], 16)
            square(x_tok[:, 0, :], st(0)[:, 0:1], squares, junk[:, :])
            act.wait_ge(x_loaded[1], 16)
            square(x_tok[:, 1, D // 2:D], part_sq[:, 1, 1:2], squares, junk[:, 0:D // 2])
            root(1, 0, mean_ready, root_ready)
            scale_part(work, x_tok, 1, lambda b, c: st(0)[:, b:b + 1])
            phase(0, side=split)
            act.wait_ge(fr_loaded, 16)
            act.activation(fr_hi[:, :, :], fr_raw[:, :, :], ACT.Copy).then_inc(fr_split_hi, 1)

            def probs_copy(i):
                act.wait_ge(probs_T, i + 1)
                if i >= 2:
                    act.wait_ge(pv_done, i - 1)
                act.activation(probsT[:, i % 2, :], bank[6][:, 0:384], ACT.Copy).then_inc(probsT_copied, 1)

            def exps(i):
                act.wait_ge(neg_max, i + 1)
                if i >= 3:
                    act.wait_ge(probs_T, i - 2)
                    act.wait_ge(recip_done, i - 2)
                s, r = i % 2, i % 3
                nm, den, es = st(40 + r), st(43 + r), st(46 + r)
                if i < NH:
                    act.activation(es, nm, ACT.Exp, bias=sink[:, i:i + 1]).then_inc(exp_done, 1)
                else:
                    act.activation(es, nm, ACT.Exp).then_inc(exp_done, 1)
                act.activation(probs[:, r, 0:128], biased[:, s, 0:128], ACT.Exp, bias=nm[:, 0:1], scale=HD ** -0.5,
                               accum_out=den[:, 0:1]).then_inc(exp_done, 1)
                act.activation(probs[:, r, 128:384], biased[:, s, 128:384], ACT.Exp, bias=nm[:, 1:2], scale=HD ** -0.5,
                               accum_out=den[:, 1:2]).then_inc(exp_done, 1)

            def out_squares(heads, b, col):
                act.wait_ge(out_done, heads.stop)
                square(work[:, b, HD * heads.start:HD * heads.stop], col, squares, junk[:, 0:HD * len(heads)])

            def head(i):
                if 2 <= i < 2 * NH + 2:
                    probs_copy(i - 2)
                if i < 2 * NH:
                    exps(i)
                if i in (19, 21):
                    b = (i - 19) // 2
                    out_squares(range(0, NH), b, stat[:, 4 + 2 * b:5 + 2 * b])
                if i in (27, 28):
                    out_squares(range(NH, 24), i - 27, part_sq[:, i - 27, 0:1])
                if i == 2 * NH + 1:
                    for b in range(NB):
                        out_squares(range(24, 28), b, part_sq[:, b, 1:2])
                    warm(2, ACT.Sqrt)
                if i == 2 * NH + 2:
                    for b in range(NB):
                        out_squares(range(28, 2 * NH), b, part_sq[:, b, 2:3])

            group(0)
            act.activation(kaT[:, :], bank[0][:, 0:S], ACT.Copy).then_inc(banks_free, 1)
            act.wait_ge(f_z, 1)
            act.activation(fa[:, :], fz[:, :], ACT.Abs).then_inc(f_abs, 1)
            act.wait_ge(f_abs, 1)
            act.activation(fa[:, :], fa[:, :], ACT.Exp, scale=-1.0).then_inc(f_exp, 1)
            act.wait_ge(f_exp, 1)
            act.activation(fa[:, :], fa[:, :], ACT.Ln, bias=1.0).then_inc(f_ln, 1)
            for g in (1, 2):
                group(g)
                copy_out(qaT[:, 4 * (g - 1):4 * (g - 1) + 2, :].rearrange("p a b -> p (a b)"), g)
            for g in (3, 4):
                group(g, side=lambda j, g=g: head(4 * (g - 3) + j // 2) if j % 2 else None,
                      take=lambda g=g: copy_out(vb[:, 0, W * (g - 3):W * (g - 2)], g))
            for n, g in enumerate((5, 6, 7, 8)):
                dst = (qbT, kbT)[n % 2][:, 4 * (n // 2):4 * (n // 2) + 2, :].rearrange("p a b -> p (a b)")
                group(g, side=lambda j, n=n: head(8 + 4 * n + j // 2) if j % 2 else None,
                      take=lambda g=g, dst=dst: copy_out(dst, g))
            for i in range(24, 2 * NH + 3):
                head(i)
            root(2, 1, mean_ready, root_ready, 4)
            scale_part(work, work, 2, head_factor)
            phase(1)
            def squares_out(g, i, jk, n):
                m = i * 2 + n % 4
                act.activation(jk[:, 0:W], out_of(g, 0), ACT.Square, accum_out=part_sq[:, 0, bass.ds(m, 1)]).then_inc(sq_first, 1)
                act.wait_ge(mul_first, n + 1 + i * 2)
                act.activation(jk[:, W:2 * W], out_of(g, 1), ACT.Square, accum_out=part_sq[:, 1, bass.ds(m, 1)]).then_inc(banks_free, 1)

            def x_squares(k, n):
                for b in range(NB):
                    for c in range(2):
                        act.wait_ge(x_added, n + 2 * b + c)
                        square(x_tok[:, b, c * D // 2:(c + 1) * D // 2], part_sq[:, b, c:c + 1], squares,
                               (junk if k == 3 else junk2)[:, 0:D // 2])

            with act.Fori(0, 2) as i:
                for e in range(2):
                    g = GROUP["w_out"][e]
                    if e == 0:
                        act.wait_ge(squares, 10)
                    group(g, i, 16, take=lambda g=g, e=e: squares_out(g, i, junk, e))
                    act.wait_ge(banks_free, evacuated(g) + i * 4)
            root(3, 2, mean_ready, root_ready)
            x_squares(3, 1)
            root(4, 3, mean_ready, root_ready)
            scale_part(work, x_tok, 4, lambda b, c: st(3)[:, b:b + 1])
            phase(2)
            def taps(e, i):
                g = GROUP["w_up"][e]
                cv = (cv_gate, cv_val)[e]
                act.wait_ge(coef_ready, i + 1)
                for ft in range(4):
                    ins = act.activation(cv[:, ft, :], bank[2 * (g % 2) + ft // 2][:, ft % 2 * S:(ft % 2 + 1) * S], ACT.Identity,
                                         bias=coef[:, e, 3, ft:ft + 1], scale=coef[:, e, 2, ft:ft + 1])
                ins.then_inc(conv_tap2, 1)

            def glu_hi(i):
                act.wait_ge(glu_done, i + 1)
                act.activation(g_hi[:, bass.ds(i * 4, 4), :], cv_val[:, :, :], ACT.Copy).then_inc(g_hi_done, 1)

            def up(i, last=None):
                group(GROUP["w_up"][0], i, 16, side=lambda j: glu_hi(last) if j == 2 and last is not None else None)
                taps(0, i)

                def gelu(j):
                    if j == 1:
                        act.wait_ge(banks_free, evacuated(GROUP["w_up"][0]) + i * 4)
                        act.activation(cv_gate[:, :, :], cv_gate[:, :, :], ACT.Gelu_apprx_tanh).then_inc(gelu_done, 1)
                group(GROUP["w_up"][1], i, 16, side=gelu)
                act.wait_ge(g_lo_done, i) if last is not None else None
                taps(1, i)

            up(0)
            with act.Fori(1, 11) as i:
                up(i, i - 1)
            warm(1, ACT.Sqrt)
            act.wait_ge(squares, 14)
            for i in range(2):
                for e in range(2):
                    g = GROUP["w_down"][e]
                    group(g, i, 48, side=(lambda j: glu_hi(10) if j == 1 else None) if i + e == 0 else None,
                          take=lambda g=g, e=e, i=i: squares_out(g, i, junk2, 4 + e))
                    act.wait_ge(banks_free, evacuated(g) + i * 4)
            root(5, 4, mean_ready, root_ready)
            x_squares(5, 5)
            root(6, 5, mean_ready, root_ready)
            scale_part(mix2, x_tok, 6, lambda b, c: st(5)[:, b:b + 1])
            act.wait_ge(fr_loaded, 32)
            act.wait_ge(fr_done, 1)
            act.activation(fr_hi[:, :, :], fr_raw[:, :, :], ACT.Copy).then_inc(fr_split_hi, 1)
            phase(3)

            g = GROUP["gla_qk"][0]
            group(g)
            act.activation(gqk[:, 0, :, :].rearrange("p a b -> p (a b)"), out_of(g, 0), ACT.Copy, scale=HD ** -0.5).then_inc(banks_free, 1)
            g = GROUP["gla_v"][0]
            act.wait_ge(fr_done, 2)
            act.activation(rT[:, :], bank[4][0:16, 0:S], ACT.Copy).then_inc(r_copied, 1)
            group(g)
            copy_out(gvv[:, 0, :], g)

            def gate_logs():
                act.wait_ge(gate_logits, 1)
                act.activation(la[:, :, :].rearrange("p a b -> p (a b)"), bank[5][:, :], ACT.Abs).then_inc(ga_abs, 1)
                act.wait_ge(ga_abs, 1)
                act.activation(la[:, :, :], la[:, :, :], ACT.Exp, scale=-1.0).then_inc(ga_exp, 1)
                act.wait_ge(ga_exp, 1)
                act.activation(la[:, :, :], la[:, :, :], ACT.Ln, bias=1.0).then_inc(ga_ln, 1)

            def decay_sums():
                act.wait_ge(cum_done, 1)
                act.activation(bT[:, :, :].rearrange("p a b -> p (a b)"), bank[6][:, :], ACT.Copy, scale=1.0 / GATE_TAU).then_inc(b_ready, 1)

            def level(n):
                if n == 0:
                    act.wait_ge(rel_ready, 1)
                half = P >> n
                for c, a in ((0, half), (1, 0)):
                    v = decay[:, c, :].rearrange("p (m c) -> p m c", c=2 * half)[:, :, a:a + half]
                    act.wait_ge(rel_ready, n + 1)
                    ins = act.activation(v, v, ACT.Exp)
                ins.then_inc(decayed, 1)

            def gla_side(n):
                if n == 0:
                    gate_logs()
                elif n == 2:
                    decay_sums()
                if n % 2 == 0 and 2 <= n < 18:
                    level(n // 2 - 1)
                if n == 22:
                    act.wait_ge(gla_out, 2)
                    act.activation(mix2[:, 0, 1024:1536], bank[6][:, :], ACT.Copy).then_inc(gla_copied, 1)

            dsts = [(sbq, 0), (sbq, 4), (sbk, 0), (sbk, 4)]
            for n in range(6):
                g = GROUP["sb_q"][0] + n
                group(g, side=lambda j, n=n: gla_side(4 * n + j // 2) if j % 4 == 0 else None)
                if n < 4:
                    copy_out(dsts[n][0][:, dsts[n][1]:dsts[n][1] + 2, :].rearrange("p a b -> p (a b)"), g)
                else:
                    copy_out(sbv[:, 0, W * (n - 4):W * (n - 3)], g)

            def stick(i):
                if i < SB_HEADS:
                    s = i % 2
                    act.wait_ge(z_done, i + 1)
                    if i >= 2:
                        act.wait_ge(zmask_done, i - 1)
                        act.wait_ge(sp_done, i - 1)
                    act.activation(z_s[:, s, :], bank[4][:, 0:384], ACT.Copy, scale=WIDE_SCALE).then_inc(zs_done, 1)
                    act.wait_ge(zs_done, i + 1)
                    act.activation(z_e[:, s, :], z_s[:, s, :], ACT.Abs).then_inc(zabs_done, 1)
                    act.wait_ge(zabs_done, i + 1)
                    act.activation(z_e[:, s, :], z_e[:, s, :], ACT.Exp, scale=-1.0).then_inc(zexp_done, 1)
                    act.wait_ge(zexp_done, i + 1)
                    act.activation(z_e[:, s, :], z_e[:, s, :], ACT.Ln, bias=1.0).then_inc(zln_done, 1)
                if 3 <= i < SB_HEADS + 3:
                    k = i - 3
                    act.wait_ge(t_done, k + 1)
                    if k >= 2:
                        act.wait_ge(so_done, k - 1)
                    act.activation(z_a[:, k % 2, :], z_m[:, k % 2, :], ACT.Exp).then_inc(a_done, 1)

            def both(dst, g, func):
                for b in range(NB):
                    copy_out(dst[b], g, b, func)

            gates = {"gla_g": 1024, "sgu_g": 1536}
            for n, name in enumerate(("gla_g", "sgu_u", "sgu_v", "sgu_g")):
                g = GROUP[name][0]
                group(g, side=lambda j, n=n: stick(3 * n + j // 2) if j in (1, 3, 5) else None)
                if name in gates:
                    both([gate[:, b, gates[name]:gates[name] + W] for b in range(NB)], g, ACT.Silu)
                else:
                    t = sgu_u if name == "sgu_u" else sgu_v
                    both([t[:, b, :] for b in range(NB)], g, ACT.Gelu_apprx_tanh)
            for n in range(2):
                g = GROUP["sb_g"][n]

                def side(j, n=n):
                    if n == 0 and j == 1:
                        for b in range(NB):
                            act.wait_ge(banks_free, evacuated(GROUP["sgu_v"][0]))
                            square(sgu_v[:, b, :], st(14)[:, b:b + 1], sgu_sq, junk2[:, b * W:(b + 1) * W])
                        root(1, 14, sgu_mean, sgu_root)
                    if n == 0 and j in (3, 5):
                        b = j // 2 - 1
                        act.wait_ge(mem_loaded, 32)
                        square(mem_tok[:, b, :], st(6)[:, b:b + 1], squares, junk2[:, :])
                    if n == 1 and j == 1:
                        root(7, 6, mean_ready, root_ready)
                    if n == 1 and j == 5:
                        scale_part(mem_tok, mem_tok, 7, lambda b, c: st(6)[:, b:b + 1])
                group(g, side=side, take=lambda g=g, n=n: both([gate[:, b, W * n:W * (n + 1)] for b in range(NB)], g, ACT.Silu))
            phase(4)
            act.wait_ge(hmean, 1)
            act.activation(stat[:, 128:160], stat[:, 128:160], ACT.Sqrt).then_inc(hroot, 1)
            g = GROUP["xk"][0]
            group(g)
            copy_out(xkT[:, 0:2, :].rearrange("p a b -> p (a b)"), g)
            g = GROUP["xv"][0]
            group(g, take=lambda: copy_out(xv[:, 0, :], g))
            phase(5)
            with act.Fori(0, 2) as i:
                for e in range(2):
                    g = GROUP["w_out2"][e]

                    def x_columns(g=g, e=e):
                        for b in range(NB):
                            act.wait_ge(banks_free, evacuated(g) - 1 + b + i * 4)
                            act.activation(junk2[:, b * W:(b + 1) * W], x_tok[:, b, bass.ds(i * (2 * W) + e * W, W)], ACT.Square,
                                           accum_out=part_sq[:, b, bass.ds(i * 2 + e, 1)]).then_inc(sq_first, 1)
                    group(g, i, 16, take=x_columns)
                    act.wait_ge(sq_first, 8 + 2 * (e + 1) + i * 4)
            root(8, 7, mean_ready, root_ready)
            scale_part(mem_tok, x_tok, 8, lambda b, c: st(7)[:, b:b + 1])
            phase(6)
            warm(3, ACT.Exp)
            g = GROUP["xq"][0]
            group(g, take=lambda: copy_out(mix2[:, 0, 0:W], g))
            def x_exps(h):
                act.wait_ge(xneg_done, h + 1)
                for b in range(NB):
                    ins = act.activation(x_p[:, h, b * S:(b + 1) * S], bank[4 + h][:, b * S:(b + 1) * S], ACT.Exp,
                                         bias=st(20 + h)[:, b:b + 1], scale=WIDE_SCALE, accum_out=st(24 + h)[:, b:b + 1])
                    ins.then_inc(xexp_done, 1)

            def x_probs(h):
                act.wait_ge(xpT_done, h + 1)
                if h >= 2:
                    act.wait_ge(xo_done, h - 1)
                act.activation(x_pT[:, h % 2, :], bank[4 + h][:, :], ACT.Copy).then_inc(xpT_copied, 1)

            def x_out_hi(h):
                act.wait_ge(xo_done, h + 1)
                act.activation(hT_hi[:, h, :], bank[4 + h][:, 0:S], ACT.Copy).then_inc(xo_hi, 1)

            x_exps(0)
            x_exps(1)
            x_exps(2)
            x_probs(0)
            x_exps(3)
            x_probs(1)
            x_out_hi(0)
            x_probs(2)
            x_out_hi(1)
            x_probs(3)
            x_out_hi(2)
            x_out_hi(3)
            warm(4, ACT.Sqrt)
            for e in range(4):
                g = GROUP["xo"][e]
                group(g)
                for b in range(NB):
                    act.wait_ge(banks_free, evacuated(g) - 1 + b)
                    act.activation(junk2[:, b * W:(b + 1) * W], x_tok[:, b, e * W:(e + 1) * W], ACT.Square,
                                   accum_out=part_sq[:, b, e:e + 1]).then_inc(sq_first, 1)
                act.wait_ge(sq_first, 16 + 2 * (e + 1))
            root(9, 16, mean_ready, root_ready)
            act.wait_ge(rstd_ready, 9)
            act.wait_ge(x_gained, 8)
            for c in range(2):
                act.activation(mem_tok[:, 0, c * D // 2:(c + 1) * D // 2], x_tok[:, 0, c * D // 2:(c + 1) * D // 2], ACT.Copy,
                               scale=st(16)[:, 0:1]).then_inc(out_scaled0, 1)

        @block.vector
        def _(dve):
            def split(u, i=None, step=0, n=None):
                if u >= TOTAL:
                    return
                s = u % SLOTS
                n = n or piece_size(u)
                dve.wait_ge(hi_ready, u + 1 + (0 if i is None else i * step))
                dve.tensor_tensor(w_lo[:, s, 0:n], raw[:, s, 0:n], w_hi[:, s, 0:n].bitcast(F32), ALU.subtract).then_inc(lo_ready, 1)

            def group(g, i=None, step=0, side=None, take=None):
                u, n = FIRST_PIECE[g], PLAN[g][1]
                for j in range(n):
                    split(u + j + SLOTS - 1, i, step)
                    if side and j:
                        side(j - 1)
                if side and not take:
                    side(n - 1)
                dve.wait_ge(mm_done, FIRST_PIECE[g + 1] + (0 if i is None else i * step))
                if take:
                    take()
                if side and take:
                    side(n - 1)

            def out_of(g, b):
                return bank[2 * (g % 2) + b][:, :]

            def copy_out(dst, g, b=1):
                dve.tensor_copy(dst, out_of(g, b)).then_inc(banks_free, 1)

            def phase(n, side=None):
                at = GAIN_AT[PHASES[n]]
                for c in range(KC):
                    if side and c % 4 == 0 and c // 4 < SLOTS - 1:
                        side(c // 4)
                    if c % 2 == 0:
                        dve.wait_ge(hiT_done, (KC * n + c) // 2 + 1)
                    dve.scalar_tensor_tensor(out=hT_lo[:, c, :], in0=bank[pair_bank(n, c // 2)][:, c % 2 * S:(c % 2 + 1) * S],
                                             scalar=gains[:, at + c:at + c + 1], in1=hT_hi[:, c, :].bitcast(F32),
                                             op0=ALU.mult, op1=ALU.subtract).then_inc(loT_done, 1)

            def rstd(n, k, n_sq, size, width=2):
                a = stat[:, 4 * k:4 * k + width]
                if n_sq:
                    dve.wait_ge(squares, n_sq)
                dve.tensor_scalar(a, a, 1.0 / size, EPS, ALU.mult, ALU.add).then_inc(mean_ready, 1)
                dve.wait_ge(root_ready, n)
                dve.reciprocal(a, a).then_inc(rstd_ready, 1)
                dve.wait_ge(rstd_ready, n)

            def square1(src, col, n, jk):
                dve.tensor_tensor_reduce(jk, src, src, 1.0, 0.0, ALU.mult, ALU.add, col).then_inc(squares_d, 1)
                dve.wait_ge(squares_d, n)

            def scale_rows(dst, src, factor):
                for c in range(3):
                    for b in range(NB):
                        dve.tensor_scalar(dst[:, b, c * W:(c + 1) * W], src[:, b, c * W:(c + 1) * W], factor(b, c), None,
                                          ALU.mult).then_inc(scaled, 1)

            n_sums = [0]

            def total_squares(k, n=4):
                dve.tensor_reduce(st(k), part_sq[:, :, 0:n], AX, ALU.add).then_inc(sums_ready, 1)
                n_sums[0] += 1
                dve.wait_ge(sums_ready, n_sums[0])

            dve.memset(ones[:, :], 1.0).then_inc(dve_ready, 1)
            dve.memset(idle[:, :], 0.0).then_inc(idle_ready, 1)
            dve.memset(lf2[:, :, :], 0.0).then_inc(lf_cleared, 1)
            dve.wait_ge(rows_T, 1)
            dve.tensor_copy(gains[:, 0:KC], bank[6][:, 0:KC]).then_inc(tables_ready, 1)
            dve.wait_ge(x_loaded[1], 16)
            square1(x_tok[:, 1, 0:D // 2], part_sq[:, 1, 0:1], 1, junk_d[:, 0:D // 2])
            dve.wait_ge(squares, 2)
            dve.tensor_tensor(st(0)[:, 1:2], part_sq[:, 1, 0:1], part_sq[:, 1, 1:2], ALU.add).then_inc(sums_ready, 1)
            n_sums[0] += 1
            dve.wait_ge(sums_ready, n_sums[0])
            rstd(1, 0, 2, D)
            dve.wait_ge(x_loaded[0], 16)
            scale_rows(work, x_tok, lambda b, c: st(0)[:, b:b + 1])
            dve.wait_ge(tables_ready, 1)
            phase(0, side=split)
            dve.wait_ge(fr_split_hi, 1)
            dve.tensor_tensor(fr_lo[:, :, :], fr_raw[:, :, :], fr_hi[:, :, :].bitcast(F32), ALU.subtract).then_inc(fr_split_lo, 1)

            def bias(i):
                s = i % 2
                dve.wait_ge(scores_done, i + 1)
                if i >= 2:
                    dve.wait_ge(exp_done, 3 * (i - 1))
                h = i % NH
                if i < NH:
                    slope = 2.0 ** (-8.0 * (h + 1) / NH)
                    dve.scalar_tensor_tensor(out=biased[:, s, :], in0=distm[:, :], scalar=-slope * HD ** 0.5,
                                             in1=bank[4 + s][:, 0:384], op0=ALU.mult, op1=ALU.add).then_inc(biased_done, 2)
                else:
                    for b, (lo, hi) in enumerate(((0, 128), (128, 384))):
                        dve.scalar_tensor_tensor(out=biased[:, s, lo:hi], in0=bank[4 + s][:, lo:hi], scalar=c8[:, b, h:h + 1],
                                                 in1=foxm[:, lo:hi], op0=ALU.add, op1=ALU.add).then_inc(biased_done, 1)
                dve.wait_ge(biased_done, 2 * (i + 1))
                mx, nm = st(52 + i % 3), st(40 + i % 3)
                dve.tensor_reduce(mx[:, 0:1], biased[:, s, 0:128], AX, ALU.max).then_inc(row_max, 1)
                dve.tensor_reduce(mx[:, 1:2], biased[:, s, 128:384], AX, ALU.max).then_inc(row_max, 1)
                dve.wait_ge(row_max, 2 * (i + 1))
                if i < NH:
                    dve.tensor_scalar(nm, mx, sink8[:, h:h + 1], -HD ** -0.5, ALU.max, ALU.mult).then_inc(neg_max, 1)
                else:
                    dve.tensor_scalar(nm, mx, -HD ** -0.5, None, ALU.mult).then_inc(neg_max, 1)

            def recip(i):
                r = i % 3
                den, es, rd = st(43 + r), st(46 + r), st(49 + r)
                dve.wait_ge(exp_done, 3 * (i + 1))
                if i >= 3:
                    dve.wait_ge(out_done, i - 2)
                if i < NH:
                    dve.tensor_tensor(rd, den, es, ALU.add).then_inc(den_done, 1)
                    dve.wait_ge(den_done, i + 1)
                    dve.reciprocal(rd, rd).then_inc(recip_done, 1)
                else:
                    dve.reciprocal(rd, den).then_inc(recip_done, 1)

            def normalise(i):
                dve.wait_ge(pv_done, i + 1)
                dve.wait_ge(recip_done, i + 1)
                dve.tensor_tensor(work[:, :, i * HD:(i + 1) * HD], bank[7][:, 0:P].rearrange("p (b n) -> p b n", b=NB),
                                  broadcast(st(49 + i % 3), [P, NB, HD]), ALU.mult).then_inc(out_done, 1)

            def head(i):
                if i < 2 * NH:
                    bias(i)
                if 1 <= i <= 2 * NH:
                    recip(i - 1)
                if 3 <= i < 2 * NH + 3:
                    normalise(i - 3)

            dve.wait_ge(pool_ready, 13)
            dve.wait_ge(consts_loaded, 32)
            dve.tensor_scalar(sink8[:, :], sink[:, :], HD ** 0.5, None, ALU.mult).then_inc(dve_ready, 1)
            dve.tensor_copy(eye2[:, :], eye_f[:, :]).then_inc(dve_ready, 1)
            group(0)
            dve.tensor_copy(va[:, :, :].rearrange("p a b -> p (a b)"), bank[1][:, 0:S]).then_inc(banks_free, 1)
            dve.wait_ge(fr_done, 1)
            dve.tensor_scalar(fz[:, :], bank[7][0:16, 0:S], bf[:, :], None, ALU.add).then_inc(f_z, 1)
            dve.wait_ge(f_z, 1)
            dve.tensor_scalar(fm[:, :], fz[:, :], 0.0, None, ALU.min).then_inc(f_min, 1)
            dve.wait_ge(f_min, 1)
            dve.wait_ge(f_ln, 1)
            dve.tensor_tensor(fa[:, :], fm[:, :], fa[:, :], ALU.subtract).then_inc(f_log, 1)
            for g in (1, 2):
                group(g)
                copy_out(qaT[:, 4 * (g - 1) + 2:4 * g, :].rearrange("p a b -> p (a b)"), g)
                if g == 1:
                    dve.wait_ge(lf_T, 1)
                    dve.wait_ge(lf_cleared, 1)
                    dve.tensor_copy(lf2[:, :, 0:64].rearrange("p b (c n) -> p b c n", c=2)[:, :, :, 0:16],
                                    bank[6][:, 0:32].rearrange("p (b n) -> p b n", b=NB).unsqueeze(2).broadcast_to([P, NB, 2, 16])
                                    ).then_inc(lf_ready, 1)
                    dve.wait_ge(va_T, 1)
                    dve.tensor_copy(va[:, :, :].rearrange("p a b -> p (a b)"), bank[5][:, 0:S]).then_inc(va_ready, 1)
                    dve.wait_ge(conv_T, 1)
                    dve.tensor_copy(conv[:, :, :].rearrange("p a b -> p (a b)"), bank[4][:, 0:4 * 2 * FFT]).then_inc(conv_ready, 1)
                    dve.tensor_copy(gains[:, KC:GAIN_ROWS], bank[4][:, 4 * 2 * FFT + KC:4 * 2 * FFT + GAIN_ROWS]).then_inc(tables_ready, 1)
                else:
                    dve.wait_ge(f_cum, 1)
                    dve.tensor_scalar(c8[:, :, :].rearrange("p a b -> p (a b)"), bank[6][:, 0:32], HD ** 0.5, None, ALU.mult).then_inc(f_c, 1)
                    dve.tensor_scalar(cT2[:, :], bank[7][:, 0:S], -HD ** 0.5, None, ALU.mult).then_inc(f_c, 1)
                    dve.wait_ge(f_c, 2)
                    dve.scalar_tensor_tensor(out=cT2[32:48, :], in0=bank[7][32:48, 0:S], scalar=-HD ** 0.5,
                                             in1=cT2[32:48, :].bitcast(F32), op0=ALU.mult, op1=ALU.subtract).then_inc(f_c, 1)
            for g in (3, 4):
                group(g, side=lambda j, g=g: head(4 * (g - 3) + j // 2) if j % 2 else None,
                      take=lambda g=g: copy_out(vb[:, 1, W * (g - 3):W * (g - 2)], g))
            for n, g in enumerate((5, 6, 7, 8)):
                dst = (qbT, kbT)[n % 2][:, 4 * (n // 2) + 2:4 * (n // 2) + 4, :].rearrange("p a b -> p (a b)")
                group(g, side=lambda j, n=n: head(8 + 4 * n + j // 2) if j % 2 else None,
                      take=lambda g=g, dst=dst: copy_out(dst, g))
            for i in range(24, 2 * NH + 3):
                head(i)
            dve.wait_ge(out_done, 2 * NH)
            dve.wait_ge(squares, 10)
            dve.tensor_reduce(stat[:, 4:8].rearrange("p (b k) -> p b k", k=2)[:, :, 1], part_sq[:, :, 0:3], AX, ALU.add).then_inc(sums_ready, 1)
            n_sums[0] += 1
            dve.wait_ge(sums_ready, n_sums[0])
            rstd(2, 1, 10, D_SWA, 4)
            scale_rows(work, work, head_factor)
            phase(1)
            def gained_out(dst, gain, g, i, n, step_n):
                for b in (1, 0):
                    if b == 0:
                        dve.wait_ge(sq_first, n + 1 + i * 2)
                    c = bass.ds(i * (2 * W) + step_n * W, W)
                    dve.tensor_tensor(dst[:, b, c], out_of(g, b), gain[:, c], ALU.mult).then_inc(mul_first if b else banks_free, 1)

            dve.wait_ge(gain_loaded, 16)
            with dve.Fori(0, 2) as i:
                for e in range(2):
                    g = GROUP["w_out"][e]
                    group(g, i, 16, take=lambda g=g, e=e: gained_out(work, mix_gain, g, i, e, e))

            def residual(n, k, src, m, done):
                dve.wait_ge(banks_free, m)
                total_squares(k)
                rstd(n, k, 0, D)
                for b in range(NB):
                    for c in range(2):
                        cols = slice(c * D // 2, (c + 1) * D // 2)
                        dve.scalar_tensor_tensor(out=x_tok[:, b, cols], in0=src[:, b, cols], scalar=st(k)[:, b:b + 1],
                                                 in1=x_tok[:, b, cols], op0=ALU.mult, op1=ALU.add).then_inc(x_added, 1)
                dve.wait_ge(squares, done)
                total_squares(k + 1, 2)

            residual(3, 2, work, evacuated(GROUP["w_out"][3]), 14)
            rstd(4, 3, 14, D)
            scale_rows(work, x_tok, lambda b, c: st(3)[:, b:b + 1])
            phase(2)
            def taps(e, i):
                g = GROUP["w_up"][e]
                cv = (cv_gate, cv_val)[e]
                dve.wait_ge(conv_tap2, 2 * i + e + 1)
                for tap in (1, 0):
                    back = 2 - tap
                    for ft in range(4):
                        ps = bank[2 * (g % 2) + ft // 2][:, ft % 2 * S:(ft % 2 + 1) * S]
                        ins = dve.scalar_tensor_tensor(out=cv[:, ft, back:S], in0=ps[:, 0:S - back], scalar=coef[:, e, tap, ft:ft + 1],
                                                       in1=cv[:, ft, back:S], op0=ALU.mult, op1=ALU.add)
                        if tap == 0 and ft % 2:
                            ins.then_inc(banks_free, 1)
                    if tap:
                        ins.then_inc(conv_tap1, 1)
                        dve.wait_ge(conv_tap1, 2 * i + e + 1)

            def glu(i):
                dve.wait_ge(gelu_done, i + 1)
                dve.wait_ge(banks_free, evacuated(GROUP["w_up"][1]) + i * 4)
                dve.tensor_tensor(cv_val[:, :, :], cv_gate[:, :, :], cv_val[:, :, :], ALU.mult).then_inc(glu_done, 1)

            def glu_lo(i):
                dve.wait_ge(g_hi_done, i + 1)
                dve.tensor_tensor(g_lo[:, bass.ds(i * 4, 4), :], cv_val[:, :, :], g_hi[:, bass.ds(i * 4, 4), :].bitcast(F32),
                                  ALU.subtract).then_inc(g_lo_done, 1)

            def up(i, last=None):
                if last is not None:
                    dve.wait_ge(banks_free, evacuated(GROUP["w_up"][1]) + last * 4)
                for e in range(2):
                    ins = dve.tensor_copy(coef[:, e, :, :], conv[:, :, bass.ds(i * 4 + e * FFT, 4)])
                ins.then_inc(coef_ready, 1)

                def finish(j):
                    if last is not None and j == 1:
                        glu(last)
                    if last is not None and j == 3:
                        glu_lo(last)
                group(GROUP["w_up"][0], i, 16, side=finish)
                dve.wait_ge(coef_ready, i + 1)
                taps(0, i)
                group(GROUP["w_up"][1], i, 16)
                taps(1, i)

            up(0)
            with dve.Fori(1, 11) as i:
                up(i, i - 1)
            def last_glu(j):
                if j == 0:
                    glu(10)
                if j == 1:
                    glu_lo(10)
                if j == 4:
                    dve.wait_ge(gain_loaded, 32)

            for i in range(2):
                for e in range(2):
                    g = GROUP["w_down"][e]
                    group(g, i, 48, side=last_glu if i + e == 0 else None,
                          take=lambda g=g, e=e, i=i: gained_out(y_tok, ffn_gain, g, i, 4 + e, e))
            residual(5, 4, y_tok, evacuated(GROUP["w_down"][3]), 18)
            rstd(6, 5, 18, D)
            scale_rows(mix2, x_tok, lambda b, c: st(5)[:, b:b + 1])
            dve.wait_ge(fr_split_hi, 2)
            dve.tensor_tensor(fr_lo[:, :, :], fr_raw[:, :, :], fr_hi[:, :, :].bitcast(F32), ALU.subtract).then_inc(fr_split_lo, 1)
            phase(3)

            def level_masks():
                dve.wait_ge(second_pool, 9)
                dve.tensor_tensor(xor_s[:, :], xor_s[:, :], xor_t[:, :], ALU.bitwise_xor).then_inc(second_dve, 1)
                dve.wait_ge(second_dve, 1)
                dve.tensor_copy(lev[:, :], xor_s[:, :]).then_inc(second_dve, 1)
                dve.tensor_scalar(prod[:, 0:P], tri[:, :], -1024.0, 1024.0, ALU.mult, ALU.add).then_inc(second_dve, 1)
                dve.wait_ge(second_dve, 3)
                dve.tensor_tensor(lev[:, :], lev[:, :], prod[:, 0:P], ALU.add).then_inc(second_dve, 1)
                dve.wait_ge(second_dve, 4)
                for n in range(1, 8):
                    dve.tensor_scalar(levels[:, n - 1, :], lev[:, :], float(P >> n), None, ALU.is_ge).then_inc(second_dve, 1)
                dve.wait_ge(second_dve, 11)
                for n in range(1, 8):
                    dve.scalar_tensor_tensor(out=levels[:, n - 1, :], in0=lev[:, :], scalar=float(2 * (P >> n)), in1=levels[:, n - 1, :],
                                             op0=ALU.is_lt, op1=ALU.mult).then_inc(second_dve, 1)
                dve.tensor_scalar(levels[:, 7, :], lev[:, :], 1.0, None, ALU.is_lt).then_inc(second_dve, 1)
                dve.wait_ge(second_dve, 19)

            g = GROUP["gla_qk"][0]
            group(g, side=lambda j: level_masks() if j == 2 else None)
            copy_out(gqk[:, 1, :, :].rearrange("p a b -> p (a b)"), g)
            g = GROUP["gla_v"][0]
            group(g)
            copy_out(gvv[:, 1, :], g)

            def gate_logs():
                dve.wait_ge(ga_ln, 1)
                dve.scalar_tensor_tensor(out=la[:, :, :].rearrange("p a b -> p (a b)"), in0=bank[5][:, :], scalar=0.0,
                                         in1=la[:, :, :].rearrange("p a b -> p (a b)"), op0=ALU.min, op1=ALU.subtract).then_inc(ga_log, 1)
                dve.memset(acc[:, :, :], 0.0).then_inc(cleared, 1)
                dve.memset(decay[:, :, :], 0.0).then_inc(cleared, 1)
                dve.memset(qkd[:, :, :, :], 0.0).then_inc(cleared, 1)

            def level(n):
                half = P >> n
                k = 2 * S // (2 * half)
                bv = bT[:, :, :].rearrange("p a (m c) -> p (a m) c", c=2 * half)
                ref = bv[:, :, half - 1:half].broadcast_to([P, k, half])
                if n == 0:
                    dve.wait_ge(b_ready, 1)
                    dve.wait_ge(cleared, 3)
                def halves(ap, a):
                    return ap.rearrange("p (m c) -> p m c", c=2 * half)[:, :, a:a + half]
                if n >= 1:
                    dve.wait_ge(qk_decayed, n)
                dve.tensor_tensor(halves(decay[:, 0, :], half), bv[:, :, half:2 * half], ref, ALU.subtract)
                dve.tensor_tensor(halves(decay[:, 1, :], 0), ref, bv[:, :, 0:half], ALU.subtract).then_inc(rel_ready, 1)
                dve.wait_ge(decayed, n + 1)
                if n == 0:
                    dve.wait_ge(banks_free, evacuated(GROUP["gla_qk"][0]))
                for c, a in ((0, half), (1, 0)):
                    ins = dve.tensor_tensor(halves(qkd[:, c, :, :].rearrange("p a b -> p (a b)"), a),
                                            halves(gqk[:, c, :, :].rearrange("p a b -> p (a b)"), a),
                                            halves(decay[:, c, :], a), ALU.mult)
                ins.then_inc(qk_decayed, 1)

            def collect(n):
                dve.wait_ge(level_scores, n + 1)

                def heads(ap):
                    return ap.rearrange("p (c m t) -> p c m t", c=2, m=2)

                def pairs(b):
                    return upper[:, 2 * b:2 * b + 2, 0:2 * P].rearrange("p c (m t) -> p c m t", m=2)
                if n == 0:
                    dve.tensor_copy(heads(inter[:, :]), pairs(0)).then_inc(level_added, 2)
                    return
                if n >= 2:
                    dve.wait_ge(level_added, 2 * n)
                for b in range(NB):
                    mask = levels[:, n - 1, :].bitcast(I32).unsqueeze(1).unsqueeze(1).broadcast_to([P, 2, 2, P])
                    dve.copy_predicated(heads(acc[:, b, :]), mask, pairs(b)).then_inc(level_added, 1)

            def gla_side(n):
                if n == 0:
                    gate_logs()
                if n % 2 == 0 and 4 <= n <= 20:
                    collect(n // 2 - 2)
                if n % 2 == 0 and 2 <= n < 18:
                    level(n // 2 - 1)
                if n == 22:
                    dve.wait_ge(gla_out, 2)
                    dve.tensor_copy(mix2[:, 1, 1024:1536], bank[7][:, :]).then_inc(gla_copied, 1)

            dsts = [(sbq, 0), (sbq, 4), (sbk, 0), (sbk, 4)]
            for n in range(6):
                g = GROUP["sb_q"][0] + n
                group(g, side=lambda j, n=n: gla_side(4 * n + j // 2) if j % 4 == 0 else None)
                if n < 4:
                    copy_out(dsts[n][0][:, dsts[n][1] + 2:dsts[n][1] + 4, :].rearrange("p a b -> p (a b)"), g)
                else:
                    copy_out(sbv[:, 1, W * (n - 4):W * (n - 3)], g)

            def stick(i):
                if 1 <= i <= SB_HEADS:
                    k = i - 1
                    s = k % 2
                    dve.wait_ge(zln_done, k + 1)
                    if k >= 2:
                        dve.wait_ge(inc_done, k - 1)
                    dve.scalar_tensor_tensor(out=z_p[:, s, :], in0=z_s[:, s, :], scalar=0.0, in1=z_e[:, s, :],
                                             op0=ALU.max, op1=ALU.add).then_inc(sp_done, 1)
                    dve.wait_ge(sp_done, k + 1)
                    for c in (0, 256):
                        ins = dve.tensor_tensor(z_p[:, s, c:c + P], z_p[:, s, c:c + P], sb_one[:, :], ALU.mult)
                    ins.then_inc(spm_done, 1)
                    if k >= 2:
                        dve.wait_ge(a_done, k - 1)
                    for c in (0, 256):
                        ins = dve.tensor_tensor(z_m[:, s, c:c + P], z_s[:, s, c:c + P], sb_neg[:, :], ALU.add)
                    dve.tensor_copy(z_m[:, s, P:256], z_s[:, s, P:256]).then_inc(zmask_done, 1)
                if 2 <= i < SB_HEADS + 2:
                    k = i - 2
                    dve.wait_ge(inc_done, k + 1)
                    dve.wait_ge(zmask_done, k + 1)
                    dve.tensor_tensor(z_m[:, k % 2, :], z_m[:, k % 2, :], bank[5 + k % 2][:, 0:384], ALU.add).then_inc(t_done, 1)
                if 4 <= i < SB_HEADS + 4:
                    k = i - 4
                    dve.wait_ge(so_done, k + 1)
                    dve.tensor_copy(mix2[:, :, k * P:(k + 1) * P], bank[7][:, 0:256].rearrange("p (b n) -> p b n", b=NB)).then_inc(so_copied, 1)

            for n, name in enumerate(("gla_g", "sgu_u", "sgu_v", "sgu_g")):
                group(GROUP[name][0], side=lambda j, n=n: stick(3 * n + j // 2) if j in (1, 3, 5) else None)

            def sgu_norm():
                a = st(14)
                dve.wait_ge(sgu_sq, 2)
                dve.tensor_scalar(a, a, 1.0 / 512, EPS, ALU.mult, ALU.add).then_inc(sgu_mean, 1)
                dve.wait_ge(sgu_root, 1)
                dve.reciprocal(a, a).then_inc(sgu_rstd, 1)
                dve.wait_ge(sgu_rstd, 1)
                dve.wait_ge(second_loaded, 64)
                for b in range(NB):
                    dve.scalar_tensor_tensor(out=sgu_v[:, b, :], in0=sgu_v[:, b, :], scalar=a[:, b:b + 1], in1=sgu_gain[:, :],
                                             op0=ALU.mult, op1=ALU.mult).then_inc(sgu_vn, 1)

            def sgu_weights():
                dve.wait_ge(sguT_done, 1)
                dve.tensor_tensor(w_sguT[:, :, :], bank[6][:, :].rearrange("p (g t) -> p g t", t=P),
                                  tri[:, :].unsqueeze(1).broadcast_to([P, SGU_GROUPS, P]), ALU.mult).then_inc(sguT_ready, 1)

            def sgu_result():
                dve.wait_ge(sgu_mixed, 2)
                for b in range(NB):
                    for k in range(SGU_GROUPS):
                        dve.scalar_tensor_tensor(out=mix2[:, b, 1536 + k * P:1536 + (k + 1) * P], in0=bank[4 + b][:, k * P:(k + 1) * P],
                                                 scalar=gains[:, BSGU_AT + k:BSGU_AT + k + 1], in1=sgu_u[:, b, k * P:(k + 1) * P],
                                                 op0=ALU.add, op1=ALU.mult).then_inc(sgu_done, 1)

            def tail(j, n):
                if n == 0 and j == 1:
                    sgu_weights()
                    sgu_norm()
                if n == 0 and j == 5:
                    sgu_result()
                if n == 0 and j == 7:
                    head_squares(0)
                if n == 1 and j == 1:
                    mem_mean()
                    head_squares(1)
                if n == 1 and j == 3:
                    mem_rows()

            def mem_mean():
                a = st(6)
                dve.wait_ge(squares, 20)
                dve.tensor_scalar(a, a, 1.0 / D, EPS, ALU.mult, ALU.add).then_inc(mean_ready, 1)

            def mem_rows():
                a = st(6)
                dve.wait_ge(root_ready, 7)
                dve.reciprocal(a, a).then_inc(rstd_ready, 1)
                dve.wait_ge(rstd_ready, 7)
                scale_rows(mem_tok, mem_tok, lambda b, c: st(6)[:, b:b + 1])

            def head_squares(b):
                dve.wait_ge(so_copied, SB_HEADS)
                dve.wait_ge(gla_copied, 2)
                dve.wait_ge(sgu_done, 8)
                if b:
                    dve.wait_ge(hsum_done, 1)
                sq = sbv[:, :, :].rearrange("p a b -> p (a b)")
                dve.tensor_tensor(sq, mix2[:, b, :], mix2[:, b, :], ALU.mult).then_inc(hsq_done, 1)
                dve.wait_ge(hsq_done, b + 1)
                dve.tensor_reduce(stat[:, 128 + 16 * b:144 + 16 * b], sq.rearrange("p (h n) -> p h n", n=P), AX, ALU.add).then_inc(hsum_done, 1)

            for n in range(2):
                group(GROUP["sb_g"][n], side=lambda j, n=n: tail(j, n))
            phase(4)
            hs = stat[:, 128:160]
            dve.wait_ge(hsum_done, 2)
            dve.tensor_scalar(hs, hs, 1.0 / P, EPS, ALU.mult, ALU.add).then_inc(hmean, 1)

            def gated(j):
                if j == 1:
                    dve.wait_ge(hroot, 1)
                    dve.reciprocal(hs, hs).then_inc(hrstd, 1)
                    dve.wait_ge(hrstd, 1)
                if j in (2, 4):
                    b = j // 2 - 1
                    m = mix2[:, b, :].rearrange("p (h n) -> p h n", n=P)
                    dve.tensor_tensor(m, m, stat[:, 128 + 16 * b:144 + 16 * b].unsqueeze(2).broadcast_to([P, 16, P]), ALU.mult).then_inc(hscaled, 1)
                if j in (3, 5):
                    b = j // 2 - 1
                    dve.wait_ge(hscaled, b + 1)
                    dve.wait_ge(banks_free, evacuated(GROUP["sb_g"][1]))
                    dve.tensor_tensor(mix2[:, b, :], mix2[:, b, :], gate[:, b, :], ALU.mult).then_inc(scaled, 1)

            g = GROUP["xk"][0]
            group(g, side=gated)
            copy_out(xkT[:, 2:4, :].rearrange("p a b -> p (a b)"), g)
            g = GROUP["xv"][0]
            group(g, take=lambda: copy_out(xv[:, 1, :], g))
            phase(5)

            def onto_x(g, i, step, col):
                for b in range(NB):
                    dst = x_tok[:, b, bass.ds(col, W)] if i is not None else x_tok[:, b, col:col + W]
                    dve.tensor_tensor(dst, out_of(g, b), dst, ALU.add).then_inc(banks_free, 1)

            with dve.Fori(0, 2) as i:
                for e in range(2):
                    g = GROUP["w_out2"][e]
                    group(g, i, 16, take=lambda g=g, e=e: onto_x(g, i, 16, i * (2 * W) + e * W))
            dve.wait_ge(sq_first, 16)
            total_squares(7)
            rstd(8, 7, 0, D)
            scale_rows(mem_tok, x_tok, lambda b, c: st(7)[:, b:b + 1])
            phase(6)
            g = GROUP["xq"][0]
            group(g, take=lambda: copy_out(mix2[:, 1, 0:W], g))
            def x_max(h):
                dve.wait_ge(xs_done, h + 1)
                dve.tensor_reduce(st(20 + h), bank[4 + h][:, :].rearrange("p (b k) -> p b k", b=NB), AX, ALU.max).then_inc(xmax_done, 1)
                dve.wait_ge(xmax_done, h + 1)
                dve.tensor_scalar(st(20 + h), st(20 + h), -WIDE_SCALE, None, ALU.mult).then_inc(xneg_done, 1)

            def x_norm(h):
                dve.wait_ge(xexp_done, 2 * (h + 1))
                dve.reciprocal(st(24 + h), st(24 + h)).then_inc(xrecip_done, 1)
                dve.wait_ge(xrecip_done, h + 1)
                pv = x_p[:, h, :].rearrange("p (b k) -> p b k", b=NB)
                dve.tensor_tensor(pv, pv, broadcast(st(24 + h), [P, NB, S]), ALU.mult).then_inc(xnorm_done, 1)

            def x_out_lo(h):
                dve.wait_ge(xo_hi, h + 1)
                dve.tensor_tensor(hT_lo[:, h, :], bank[4 + h][:, 0:S], hT_hi[:, h, :].bitcast(F32), ALU.subtract).then_inc(xo_lo, 1)

            x_max(0)
            x_max(1)
            x_norm(0)
            x_max(2)
            x_norm(1)
            x_max(3)
            x_norm(2)
            x_norm(3)
            x_out_lo(0)
            x_out_lo(1)
            x_out_lo(2)
            x_out_lo(3)
            for e in range(4):
                g = GROUP["xo"][e]
                group(g)
                onto_x(g, None, 0, e * W)
                dve.wait_ge(gain_loaded, 48)
                for b in range(NB):
                    dve.wait_ge(sq_first, 16 + 2 * e + b + 1)
                    if e == 3 and b:
                        total_squares(16)
                        dve.tensor_scalar(st(16), st(16), 1.0 / D, EPS, ALU.mult, ALU.add).then_inc(mean_ready, 1)
                    dve.tensor_tensor(x_tok[:, b, e * W:(e + 1) * W], x_tok[:, b, e * W:(e + 1) * W], out_gain[:, e * W:(e + 1) * W],
                                      ALU.mult).then_inc(x_gained, 1)
            dve.wait_ge(x_gained, 8)
            dve.wait_ge(root_ready, 9)
            dve.reciprocal(st(16), st(16)).then_inc(rstd_ready, 1)
            dve.wait_ge(rstd_ready, 9)
            for c in range(2):
                dve.tensor_scalar(mem_tok[:, 1, c * D // 2:(c + 1) * D // 2], x_tok[:, 1, c * D // 2:(c + 1) * D // 2], st(16)[:, 1:2],
                                  None, ALU.mult).then_inc(out_scaled, 1)

        @block.tensor
        def _(pe):
            def three(o, l_hi, l_lo, r_hi, r_lo, start, stop):
                pe.matmul(o, l_hi, r_hi, start=start, stop=False, skip_group_check=True)
                pe.matmul(o, l_hi, r_lo, start=False, stop=False, skip_group_check=True)
                return pe.matmul(o, l_lo, r_hi, start=False, stop=stop, skip_group_check=True)

            def group(g, mode, i=None, step=0, kcs=(2,) * 8, a_hi=hT_hi, a_lo=hT_lo, first=None, chunks=False, heads=False, side=None):
                u = FIRST_PIECE[g]
                pair = 2 * (g % 2)
                if g >= 2:
                    pe.wait_ge(banks_free, 2 * (g - 1) + (0 if i is None else i * (4 if step else 0)))
                k = 0
                total = sum(kcs)
                for j, n in enumerate(kcs):
                    s = (u + j) % SLOTS
                    pe.wait_ge(lo_ready, u + j + 1 + (0 if i is None else i * step))
                    hi, lo = wide(w_hi, s, n, W), wide(w_lo, s, n, W)
                    for c in range(n):
                        if first is not None:
                            pe.wait_ge(loT_done, first * KC + max(k + 1, 4))
                        if heads:
                            pe.wait_ge(xo_lo, k + 1)
                        if chunks:
                            pe.wait_ge(g_lo_done, 10 + (k >= 40))
                        if mode == "tok":
                            for b in range(NB):
                                ins = three(bank[pair + b][:, :], a_hi[:, k, b * P:(b + 1) * P], a_lo[:, k, b * P:(b + 1) * P],
                                            hi[:, c, :], lo[:, c, :], k == 0, k == total - 1)
                        else:
                            for ft in range(4):
                                o = bank[pair + ft // 2][:, ft % 2 * S:(ft % 2 + 1) * S]
                                ins = three(o, hi[:, c, ft * P:(ft + 1) * P], lo[:, c, ft * P:(ft + 1) * P],
                                            a_hi[:, k, :], a_lo[:, k, :], k == 0 and ft % 2 == 0, k == total - 1)
                        k += 1
                    ins.then_inc(mm_done, 1)
                    if side:
                        side(j)

            def phase(n, src, done, done_act=None):
                g = READER[n]
                for q in range(KC // 2):
                    if q == 0 or done_act and q in (2, 4):
                        pe.wait_ge(scaled, done + 2 * (q // 2) + 2)
                    if done_act and q == 6:
                        pe.wait_ge(scaled_act, done_act)
                    if q == 0 and n > 0:
                        pe.wait_ge(banks_free, evacuated(g - 2))
                    if q == 6 and n > 0:
                        pe.wait_ge(banks_free, evacuated(g - 1))
                    for c in (2 * q, 2 * q + 1):
                        for b in range(NB):
                            ins = pe.transpose(bank[pair_bank(n, q)][:, c % 2 * S + b * P:c % 2 * S + (b + 1) * P],
                                               src[:, b, c * P:(c + 1) * P], ident[:, :])
                    ins.then_inc(tr_done, 1)

            def stay_warm(o, n):
                for _ in range(n):
                    pe.matmul(bank[o][:, 0:S], idle[:, 0:P], idle[:, :], start=True, stop=True)

            pe.wait_ge(idle_ready, 1)
            pe.wait_ge(ident_ready, 2)
            pe.wait_ge(first_row, 16)
            pe.transpose(bank[6][:, 0:KC], gain_rows[0:KC, :], ident[0:KC, 0:KC]).then_inc(rows_T, 1)
            pe.wait_ge(tables_ready, 1)
            stay_warm(7, 48)
            phase(0, work, 0, 2)

            for j in range(4):
                pe.wait_ge(lo_ready, j + 1)
                hi, lo = wide(w_hi, j, 4, 256), wide(w_lo, j, 4, 256)
                for c in range(4):
                    k = 4 * j + c
                    pe.wait_ge(loT_done, max(k + 1, 4))
                    for m in range(2):
                        ins = three(bank[m][:, 0:S], hi[:, c, m * P:(m + 1) * P], lo[:, c, m * P:(m + 1) * P],
                                    hT_hi[:, k, :], hT_lo[:, k, :], k == 0, k == KC - 1)
                ins.then_inc(mm_done, 1)
            pe.wait_ge(fr_split_lo, 1)
            for k in range(KC):
                ins = three(bank[7][0:16, 0:S], fr_hi[:, k, :], fr_lo[:, k, :], hT_hi[:, k, :], hT_lo[:, k, :], k == 0, k == KC - 1)
            ins.then_inc(fr_done, 1)
            pe.wait_ge(dve_ready, 3)
            pe.wait_ge(pool_ready, 13)

            def to_tokens():
                pe.wait_ge(f_log, 1)
                for b in range(NB):
                    ins = pe.transpose(bank[6][:, b * 16:(b + 1) * 16], fa[:, b * P:(b + 1) * P], ident[0:16, 0:16])
                ins.then_inc(lf_T, 1)
                pe.wait_ge(banks_free, evacuated(0))
                for b in range(NB):
                    ins = pe.transpose(bank[5][:, b * P:(b + 1) * P], va[:, b, :], ident[:, :])
                ins.then_inc(va_T, 1)
                pe.wait_ge(conv_loaded, 32)
                pe.wait_ge(rows_loaded, 16 * 8)
                pe.wait_ge(first_row, 16)
                for c in range(4):
                    pe.transpose(bank[4][:, c * 2 * FFT:(c + 1) * 2 * FFT], conv_rows[:, c, :], ident[0:2 * FFT, 0:2 * FFT])
                pe.transpose(bank[4][:, 4 * 2 * FFT:4 * 2 * FFT + GAIN_ROWS], gain_rows[:, :], ident[0:GAIN_ROWS, 0:GAIN_ROWS]
                             ).then_inc(conv_T, 1)

            def forget_sums():
                pe.wait_ge(lf_ready, 1)
                pe.matmul(bank[6][:, 0:16], tri[:, :], lf2[:, 0, 0:16], start=True, stop=True)
                pe.matmul(bank[6][:, 16:32], ones[:, :], lf2[:, 0, 0:16], start=True, stop=False)
                pe.matmul(bank[6][:, 16:32], tri[:, :], lf2[:, 1, 0:16], start=False, stop=True)
                pe.matmul(bank[7][:, 0:128], lf2[:, 0, :], tri[:, :], start=True, stop=True)
                pe.matmul(bank[7][:, 128:256], lf2[:, 0, :], ones[:, :], start=True, stop=False)
                pe.matmul(bank[7][:, 128:256], lf2[:, 1, :], tri[:, :], start=False, stop=True).then_inc(f_cum, 1)

            def scores(i):
                s, h = i % 2, i % NH
                po = h % 2 * HD
                if i >= 2:
                    pe.wait_ge(biased_done, 2 * (i - 1))
                if i == 0:
                    pe.wait_ge(k_copied, 64)
                    pe.wait_ge(banks_free, evacuated(2))
                    pe.wait_ge(conv_ready, 1)
                    pe.wait_ge(tables_ready, 2)
                if i == 1:
                    pe.wait_ge(va_ready, 1)
                if i == NH:
                    pe.wait_ge(f_c, 3)
                    pe.wait_ge(banks_free, evacuated(6))
                if i == NH + 8:
                    pe.wait_ge(banks_free, evacuated(8))
                o = bank[4 + s]
                for b, (lo, hi) in enumerate(((0, 128), (128, 384))):
                    n = hi - lo
                    if i < NH:
                        ins = pe.matmul(o[:, lo:hi], qaT[po:po + HD, h // 2, b * P:(b + 1) * P], ka2[po:po + HD, h // 8, 0:n],
                                        start=True, stop=True)
                    else:
                        pe.matmul(o[:, lo:hi], qbT[po:po + HD, h // 2, b * P:(b + 1) * P], kbT[po:po + HD, h // 2, 0:n],
                                  start=True, stop=False)
                        ins = pe.matmul(o[:, lo:hi], eye2[:, h:h + 1].broadcast_to([P, P]), cT2[:, 0:n], start=False, stop=True)
                ins.then_inc(scores_done, 1)

            def turn(i):
                s = i % 3
                pe.wait_ge(exp_done, 3 * (i + 1))
                if i >= 1:
                    pe.wait_ge(probsT_copied, i)
                if i == 0:
                    pe.wait_ge(f_c, 3)
                for c in range(3):
                    ins = pe.transpose(bank[6][:, c * P:(c + 1) * P], probs[:, s, c * P:(c + 1) * P], ident[:, :])
                ins.then_inc(probs_T, 1)

            def values(i):
                s, h = i % 2, i % NH
                pe.wait_ge(probsT_copied, i + 1)
                if i >= 1:
                    pe.wait_ge(out_done, i)

                def v(b):
                    return va[:, b, h // 8 * HD:(h // 8 + 1) * HD] if i < NH else vb[:, b, h * HD:(h + 1) * HD]
                o = bank[7]
                pe.matmul(o[:, 0:HD], probsT[:, s, 0:128], v(0), start=True, stop=True)
                pe.matmul(o[:, HD:P], probsT[:, s, 128:256], v(0), start=True, stop=False)
                pe.matmul(o[:, HD:P], probsT[:, s, 256:384], v(1), start=False, stop=True).then_inc(pv_done, 1)

            def head(i):
                if i < 2 * NH:
                    scores(i)
                if 2 <= i < 2 * NH + 2:
                    turn(i - 2)
                if 3 <= i < 2 * NH + 3:
                    values(i - 3)

            group(1, "T")
            to_tokens()
            group(2, "T")
            forget_sums()
            for g in (3, 4):
                group(g, "tok", side=lambda j, g=g: head(4 * (g - 3) + j // 2) if j % 2 else None)
            for n, g in enumerate((5, 6, 7, 8)):
                group(g, "T", side=lambda j, n=n: head(8 + 4 * n + j // 2) if j % 2 else None)
            for i in range(24, 2 * NH + 3):
                head(i)
            stay_warm(4, 16)
            phase(1, work, 6, 4)
            with pe.Fori(0, 2) as i:
                for e in range(2):
                    group(GROUP["w_out"][e], "tok", i, 16, first=1 if e == 0 else None)
            for n in (1, 2, 3, 4):
                stay_warm(7, 8)
                pe.wait_ge(x_added, n)
            stay_warm(7, 8)
            phase(2, work, 12, 6)
            with pe.Fori(0, 11) as i:
                for e in range(2):
                    group(GROUP["w_up"][e], "T", i, 16, first=2 if e == 0 else None)
            with pe.Fori(0, 2) as i:
                for e in range(2):
                    group(GROUP["w_down"][e], "tok", i, 48, kcs=DOWN, a_hi=g_hi, a_lo=g_lo, chunks=True)
            for n in (5, 6, 7, 8):
                stay_warm(7, 8)
                pe.wait_ge(x_added, n)
            stay_warm(7, 8)
            phase(3, mix2, 18, 8)

            pe.wait_ge(fr_split_lo, 2)
            group(GROUP["gla_qk"][0], "T", first=3)
            for k in range(KC):
                ins = three(bank[4][0:16, 0:S], fr_hi[:, k, :], fr_lo[:, k, :], hT_hi[:, k, :], hT_lo[:, k, :], k == 0, k == KC - 1)
            ins.then_inc(fr_done, 1)

            def gate_mm(j):
                if j == 3:
                    pe.wait_ge(r_copied, 1)
                    pe.wait_ge(second_loaded, 64)
                    for b in range(NB):
                        pe.matmul(bank[5][:, b * S:(b + 1) * S], rT[:, b * P:(b + 1) * P], wgu[:, :], start=True, stop=False)
                        ins = pe.matmul(bank[5][:, b * S:(b + 1) * S], ones[0:1, :], bgg[:, :], start=False, stop=True)
                    ins.then_inc(gate_logits, 1)

            group(GROUP["gla_v"][0], "tok", side=gate_mm)

            def gate_sums():
                pe.wait_ge(ga_log, 1)
                for t in range(2):
                    o = bank[6][:, t * S:(t + 1) * S]
                    pe.matmul(o[:, 0:P], la[:, 0, t * P:(t + 1) * P], tri[:, :], start=True, stop=True)
                    pe.matmul(o[:, P:S], la[:, 0, t * P:(t + 1) * P], ones[:, :], start=True, stop=False)
                    ins = pe.matmul(o[:, P:S], la[:, 1, t * P:(t + 1) * P], tri[:, :], start=False, stop=True)
                ins.then_inc(cum_done, 1)

            def level(n):
                if n < 8:
                    pe.wait_ge(qk_decayed, n + 1)
                    src = qkd
                else:
                    src = gqk
                if n >= 1:
                    pe.wait_ge(level_added, 2 * n)
                for b in range(NB if n else 1):
                    for h in range(GLA_HEADS):
                        po, t = h % 2 * HD, h // 2
                        qb = b if n else 1
                        ins = pe.matmul(bank[4 + 2 * b + h % 2][:, t * P:(t + 1) * P], src[po:po + HD, 1, t, b * P:(b + 1) * P],
                                        src[po:po + HD, 0, t, qb * P:(qb + 1) * P], start=True, stop=True)
                ins.then_inc(level_scores, 1)

            def gla_values():
                pe.wait_ge(level_added, 18)
                pe.wait_ge(b_ready, 1)
                for h in range(GLA_HEADS):
                    c = slice(h * P, (h + 1) * P)
                    a = slice((h % 2 * 2 + h // 2) * P, (h % 2 * 2 + h // 2 + 1) * P)
                    pe.matmul(bank[6][:, c], acc[:, 0, a], gvv[:, 0, c], start=True, stop=True)
                    pe.matmul(bank[7][:, c], inter[:, a], gvv[:, 0, c], start=True, stop=False)
                    ins = pe.matmul(bank[7][:, c], acc[:, 1, a], gvv[:, 1, c], start=False, stop=True)
                ins.then_inc(gla_out, 2)

            def gla_side(n):
                if n == 1:
                    gate_sums()
                if n % 2 and 3 <= n <= 19:
                    level(n // 2 - 1)
                if n == 21:
                    gla_values()

            for n in range(6):
                group(GROUP["sb_q"][0] + n, "T" if n < 4 else "tok",
                      side=lambda j, n=n: gla_side(4 * n + j // 2) if j % 2 else None)

            def stick(i):
                if i < SB_HEADS:
                    if i == 0:
                        pe.wait_ge(gla_copied, 2)
                        pe.wait_ge(banks_free, evacuated(GROUP["sb_k"][1]))
                    if i >= 1:
                        pe.wait_ge(zs_done, i)
                    pe.matmul(bank[4][:, 0:256], sbk[:, i, 0:P], sbq[:, i, :], start=True, stop=True)
                    pe.matmul(bank[4][:, 256:384], sbk[:, i, P:S], sbq[:, i, P:S], start=True, stop=True).then_inc(z_done, 1)
                if 2 <= i < SB_HEADS + 2:
                    k = i - 2
                    r = k % 2
                    pe.wait_ge(spm_done, k + 1)
                    if k >= 2:
                        pe.wait_ge(t_done, k - 1)
                    pe.matmul(bank[5 + r][:, 0:384], tri_neg[:, :], z_p[:, r, :], start=True, stop=False, skip_group_check=True)
                    pe.matmul(bank[5 + r][:, P:256], ones_neg[:, :], z_p[:, r, 256:384], start=False, stop=True,
                              skip_group_check=True).then_inc(inc_done, 1)
                if 4 <= i < SB_HEADS + 4:
                    k = i - 4
                    r = k % 2
                    pe.wait_ge(a_done, k + 1)
                    if k >= 1:
                        pe.wait_ge(so_copied, k)
                    if k == 0:
                        pe.wait_ge(banks_free, evacuated(GROUP["sb_v"][1]))
                    c = slice(k * P, (k + 1) * P)
                    pe.matmul(bank[7][:, 0:P], z_a[:, r, 0:P], sbv[:, 0, c], start=True, stop=True)
                    pe.matmul(bank[7][:, P:256], z_a[:, r, P:256], sbv[:, 0, c], start=True, stop=False)
                    pe.matmul(bank[7][:, P:256], z_a[:, r, 256:384], sbv[:, 1, c], start=False, stop=True).then_inc(so_done, 1)

            for n, name in enumerate(("gla_g", "sgu_u", "sgu_v", "sgu_g")):
                group(GROUP[name][0], "tok", side=lambda j, n=n: stick(3 * n + j // 2) if j in (1, 3, 5) else None)

            def tail(j, n):
                if n == 0 and j == 0:
                    pe.wait_ge(t_done, SB_HEADS)
                    for k in range(SGU_GROUPS):
                        ins = pe.transpose(bank[6][:, k * P:(k + 1) * P], w_sgu[:, k, :], ident[:, :])
                    ins.then_inc(sguT_done, 1)
                if n == 0 and j == 4:
                    pe.wait_ge(sguT_ready, 1)
                    pe.wait_ge(sgu_vn, 2)
                    for b in range(NB):
                        for k in range(SGU_GROUPS):
                            ins = pe.matmul(bank[4 + b][:, k * P:(k + 1) * P], w_sguT[:, k, :], sgu_v[:, b, k * P:(k + 1) * P],
                                            start=True, stop=True)
                    ins.then_inc(sgu_mixed, 2)

            for n in range(2):
                group(GROUP["sb_g"][n], "tok", side=lambda j, n=n: tail(j, n))
            pe.wait_ge(sgu_done, 8)
            phase(4, mem_tok, 24, 10)
            group(GROUP["xk"][0], "T", first=4)
            group(GROUP["xv"][0], "tok")
            phase(5, mix2, 30)
            with pe.Fori(0, 2) as i:
                for e in range(2):
                    group(GROUP["w_out2"][e], "tok", i, 16, first=5 if e == 0 else None)
            stay_warm(7, 16)
            phase(6, mem_tok, 32, 12)
            group(GROUP["xq"][0], "T", first=6)
            pe.wait_ge(banks_free, evacuated(GROUP["xq"][0]))
            for h in range(XA_HEADS):
                for b in range(NB):
                    ins = pe.matmul(bank[4 + h][:, b * S:(b + 1) * S], mix2[:, h // 2, h % 2 * S + b * P:h % 2 * S + (b + 1) * P],
                                    xkT[:, h, :], start=True, stop=True)
                ins.then_inc(xs_done, 1)
            def x_turn(h):
                pe.wait_ge(xnorm_done, h + 1)
                for k in range(2):
                    for b in range(NB):
                        ins = pe.transpose(bank[4 + h][:, k * S + b * P:k * S + (b + 1) * P], x_p[:, h, b * S + k * P:b * S + (k + 1) * P], ident[:, :])
                ins.then_inc(xpT_done, 1)

            def x_values(h):
                pe.wait_ge(xpT_copied, h + 1)
                for k in range(2):
                    ins = pe.matmul(bank[4 + h][:, 0:S], xv[:, k, h * P:(h + 1) * P], x_pT[:, h % 2, k * S:(k + 1) * S],
                                    start=(k == 0), stop=(k == 1))
                ins.then_inc(xo_done, 1)

            x_turn(0)
            x_turn(1)
            x_values(0)
            x_turn(2)
            x_values(1)
            x_turn(3)
            x_values(2)
            x_values(3)
            for e in range(4):
                group(GROUP["xo"][e], "tok", kcs=(2, 2), heads=e == 0)


_INS = ['x', 'pre_mix_g', 'w_in', 'b_forget', 'sinks', 'grp_swa_g', 'grp_fox_g', 'w_out', 'post_mix_g', 'pre_ffn_g',
        'w_up', 'conv_w', 'conv_b', 'w_down', 'post_ffn_g', 'mem_2', 'norm_mix_2', 'w_in_2', 'w_gla_gate_up_2',
        'b_gla_gate_2', 'sgu_norm_2', 'w_sgu_2', 'b_sgu_2', 'out_norm_2', 'w_out_2', 'norm_xattn_2', 'norm_mem_2',
        'w_xq_2', 'w_xkv_2', 'w_xo_2', 'final_norm_2']


def kernel(**inputs):
    import numpy as np
    import concourse.bacc as bacc
    from concourse.bass_utils import run_bass_kernel_spmd

    nc = bacc.Bacc("TRN2", target_bir_lowering=False, num_devices=1)
    arrays, aps = {}, {}
    for name in _INS:
        a = np.ascontiguousarray(inputs[name])
        arrays[f"in_{name}"] = a
        aps[name] = nc.dram_tensor(f"in_{name}", a.shape, mybir.dt.from_np(a.dtype), kind="ExternalInput").ap()
    out = nc.dram_tensor("out_0", (1, S, D), F32, kind="ExternalOutput").ap()
    build(nc, aps, out)
    r = run_bass_kernel_spmd(nc, [arrays], core_ids=[0])
    return r.results[0]["out_0"]
```
